# Optimizing a Trainium2 kernel written in Bass

```python
import math
import jax, jax.numpy as jnp
from jax import lax
import numpy as np

D_MODEL = 1024
BATCH = 1
SEQ = 256
DEPTH = 2

PLE_DIM = 256
ROPE_THETA = 500000.0
NORM_EPS = 1e-6
Q_BLOCK = 128

DA_HEADS = 4
DA_DQK = 64
DA_DV = 2 * DA_DQK
DA_ROT = DA_DQK // 4

SSD_HEADS = 8
SSD_HEADDIM = 64
SSD_DINNER = SSD_HEADS * SSD_HEADDIM
SSD_GROUPS = 2
SSD_DSTATE = 128
SSD_CONV = 4
SSD_CHUNK = 128
SSD_CONV_DIM = SSD_DINNER + 2 * SSD_GROUPS * SSD_DSTATE

GLA_HEADS = 4
GLA_DK = 64
GLA_DV = 128
GLA_GATE_RANK = 16
GLA_GATE_NORMALIZER = 16.0
GLA_CHUNK = 64

DA_WIDTH = DA_HEADS * DA_DV
GLA_WIDTH = GLA_HEADS * GLA_DV
MIX_WIDTH = DA_WIDTH + SSD_DINNER + GLA_WIDTH
D_FF = -(-8 * D_MODEL // (3 * 256)) * 256

IN_SIZES = (
    DA_HEADS * 2 * DA_DQK,
    DA_HEADS * 2 * DA_DQK,
    DA_WIDTH,
    SSD_DINNER,
    SSD_CONV_DIM,
    SSD_HEADS,
    GLA_HEADS * GLA_DK,
    GLA_HEADS * GLA_DK,
    GLA_WIDTH,
    GLA_WIDTH,
    GLA_GATE_RANK,
)
IN_COLS = sum(IN_SIZES)
IN_SPLITS = tuple(int(v) for v in np.cumsum(IN_SIZES)[:-1])


def rms_norm(x, gain):
    xf = x.astype(jnp.float32)
    y = xf * lax.rsqrt(jnp.mean(xf * xf, axis=-1, keepdims=True) + NORM_EPS)
    return (y * gain.astype(jnp.float32)).astype(x.dtype)

def rope_tables(positions):
    inv_freq = ROPE_THETA ** (-jnp.arange(0, DA_ROT, 2, dtype=jnp.float32) / DA_ROT)
    ang = positions.astype(jnp.float32)[..., None] * inv_freq
    return jnp.cos(ang), jnp.sin(ang)

def partial_rope(x, cos, sin):
    half = DA_ROT // 2
    x1 = x[..., :half].astype(jnp.float32)
    x2 = x[..., half:DA_ROT].astype(jnp.float32)
    c = cos[:, :, None, :]
    s = sin[:, :, None, :]
    r1 = (x1 * c - x2 * s).astype(x.dtype)
    r2 = (x2 * c + x1 * s).astype(x.dtype)
    return jnp.concatenate([r1, r2, x[..., DA_ROT:]], axis=-1)

def diff_attention(q, k, v, positions, g_q, g_k, lq1, lk1, lq2, lk2, g_sub, lambda_init):
    B, S = q.shape[:2]
    q = rms_norm(q.reshape(B, S, DA_HEADS * 2, DA_DQK), g_q)
    k = rms_norm(k.reshape(B, S, DA_HEADS * 2, DA_DQK), g_k)
    v = v.reshape(B, S, DA_HEADS, DA_DV)
    cos, sin = rope_tables(positions)
    q = partial_rope(q, cos, sin).reshape(B, S, DA_HEADS, 2, DA_DQK)
    k = partial_rope(k, cos, sin).reshape(B, S, DA_HEADS, 2, DA_DQK)
    lam = (jnp.exp(jnp.sum(lq1.astype(jnp.float32) * lk1.astype(jnp.float32)))
           - jnp.exp(jnp.sum(lq2.astype(jnp.float32) * lk2.astype(jnp.float32)))
           + lambda_init)
    scale = DA_DQK ** -0.5
    n_blk = S // Q_BLOCK
    qb = q.reshape(B, n_blk, Q_BLOCK, DA_HEADS, 2, DA_DQK).transpose(1, 0, 2, 3, 4, 5)
    key_idx = jnp.arange(S)

    def one_block(args):
        qi, bi = args
        s = jnp.einsum('bqhcd,bkhcd->bhcqk', qi, k,
                       preferred_element_type=jnp.float32) * scale
        q_idx = bi * Q_BLOCK + jnp.arange(Q_BLOCK)
        causal = key_idx[None, :] <= q_idx[:, None]
        s = jnp.where(causal, s, -jnp.inf)
        pr = jax.nn.softmax(s, axis=-1)
        attn = pr[:, :, 0] - lam * pr[:, :, 1]
        return jnp.einsum('bhqk,bkhd->bqhd', attn.astype(v.dtype), v)

    out = lax.map(one_block, (qb, jnp.arange(n_blk)))
    out = out.transpose(1, 0, 2, 3, 4).reshape(B, S, DA_HEADS, DA_DV)
    out = rms_norm(out, g_sub) * (1.0 - lambda_init)
    return out.reshape(B, S, DA_WIDTH)

def ssd_mixer(z, xbc, dt_raw, conv_w, conv_b, dt_bias, a_log, d_skip, g_norm):
    B, S = z.shape[:2]
    G, R, P, N, L = SSD_GROUPS, SSD_HEADS // SSD_GROUPS, SSD_HEADDIM, SSD_DSTATE, SSD_CHUNK
    nc = S // L
    xbc = lax.conv_general_dilated(
        xbc, conv_w[:, None, :], window_strides=(1,), padding=[(SSD_CONV - 1, 0)],
        dimension_numbers=('NWC', 'WIO', 'NWC'), feature_group_count=SSD_CONV_DIM) + conv_b
    xbc = jax.nn.silu(xbc)
    xs, bs, cs = jnp.split(xbc, [SSD_DINNER, SSD_DINNER + G * N], axis=-1)
    dt = jax.nn.softplus(dt_raw.astype(jnp.float32) + dt_bias.astype(jnp.float32))
    a = -jnp.exp(a_log.astype(jnp.float32))
    xh = xs.astype(jnp.float32).reshape(B, nc, L, G, R, P)
    xdt = xh * dt.reshape(B, nc, L, G, R)[..., None]
    bm = bs.astype(jnp.float32).reshape(B, nc, L, G, N)
    cm = cs.astype(jnp.float32).reshape(B, nc, L, G, N)
    cum = jnp.cumsum((dt * a).reshape(B, nc, L, G, R), axis=2)
    seg = cum[:, :, :, None] - cum[:, :, None, :]
    causal = jnp.tril(jnp.ones((L, L), dtype=bool))[:, :, None, None]
    decay = jnp.exp(jnp.where(causal, seg, -jnp.inf))
    cb = jnp.einsum('bclgn,bcsgn->bclsg', cm, bm)
    y_diag = jnp.einsum('bclsgr,bcsgrp->bclgrp', cb[..., None] * decay, xdt)
    decay_to_end = jnp.exp(cum[:, :, -1:] - cum)
    states = jnp.einsum('bclgn,bclgrp->bcgrpn', bm, xdt * decay_to_end[..., None])
    chunk_decay = jnp.exp(cum[:, :, -1])

    def step(h, inp):
        st, dec = inp
        return dec[..., None, None] * h + st, h

    h0 = jnp.zeros((B, G, R, P, N), jnp.float32)
    _, prev = lax.scan(step, h0, (states.transpose(1, 0, 2, 3, 4, 5),
                                  chunk_decay.transpose(1, 0, 2, 3)))
    prev = prev.transpose(1, 0, 2, 3, 4, 5)
    y_off = jnp.einsum('bclgn,bcgrpn->bclgrp', cm, prev) * jnp.exp(cum)[..., None]
    y = y_diag + y_off + d_skip.astype(jnp.float32).reshape(G, R)[:, :, None] * xh
    y = y.reshape(B, S, SSD_DINNER) * jax.nn.silu(z.astype(jnp.float32))
    y = rms_norm(y.reshape(B, S, G, SSD_DINNER // G), g_norm.reshape(G, SSD_DINNER // G))
    return y.reshape(B, S, SSD_DINNER).astype(z.dtype)

def gla_mixer(q, k, v, g_out, gate_lr, w_gate2, b_gate, g_norm):
    B, S = q.shape[:2]
    H, DK, DV, L = GLA_HEADS, GLA_DK, GLA_DV, GLA_CHUNK
    nc = S // L
    gk = jax.nn.log_sigmoid((gate_lr @ w_gate2 + b_gate).astype(jnp.float32)) / GLA_GATE_NORMALIZER
    qf = q.astype(jnp.float32).reshape(B, nc, L, H, DK) * (DK ** -0.5)
    kf = k.astype(jnp.float32).reshape(B, nc, L, H, DK)
    vf = v.astype(jnp.float32).reshape(B, nc, L, H, DV)
    bcum = jnp.cumsum(gk.reshape(B, nc, L, H, DK), axis=2)
    q_dec = qf * jnp.exp(bcum)
    k_inv = kf * jnp.exp(-bcum)
    att = jnp.einsum('bclhd,bcshd->bchls', q_dec, k_inv)
    att = jnp.where(jnp.tril(jnp.ones((L, L), dtype=bool)), att, 0.0)
    o_intra = jnp.einsum('bchls,bcshv->bclhv', att, vf)
    k_end = kf * jnp.exp(bcum[:, :, -1:] - bcum)
    states = jnp.einsum('bclhd,bclhv->bchdv', k_end, vf)
    chunk_decay = jnp.exp(bcum[:, :, -1])

    def step(st_prev, inp):
        st, dec = inp
        return dec[..., None] * st_prev + st, st_prev

    s0 = jnp.zeros((B, H, DK, DV), jnp.float32)
    _, prev = lax.scan(step, s0, (states.transpose(1, 0, 2, 3, 4),
                                  chunk_decay.transpose(1, 0, 2, 3)))
    prev = prev.transpose(1, 0, 2, 3, 4)
    o_inter = jnp.einsum('bclhd,bchdv->bclhv', q_dec, prev)
    o = (o_intra + o_inter).reshape(B, S, H, DV)
    o = rms_norm(o, g_norm) * jax.nn.silu(g_out.astype(jnp.float32).reshape(B, S, H, DV))
    return o.reshape(B, S, GLA_WIDTH).astype(q.dtype)

def first_inputs(seed: int = 0) -> dict:
    key = jax.random.key(seed)
    ks = iter(jax.random.split(key, 48))

    def nrm(shape, scale):
        return jax.random.normal(next(ks), shape, jnp.float32) * scale

    def gain(shape):
        return 1.0 + nrm(shape, 0.02)

    x = nrm((BATCH, SEQ, D_MODEL), 1.0)
    p = nrm((DEPTH, BATCH, SEQ, PLE_DIM), 1.0)
    positions = jnp.broadcast_to(jnp.arange(SEQ, dtype=jnp.int32)[None, :], (BATCH, SEQ))
    dt0 = jnp.exp(jax.random.uniform(next(ks), (DEPTH, SSD_HEADS), jnp.float32)
                  * (math.log(0.1) - math.log(0.001)) + math.log(0.001))
    ssd_dt_bias = dt0 + jnp.log(-jnp.expm1(-dt0))
    ssd_a_log = jnp.log(jax.random.uniform(next(ks), (DEPTH, SSD_HEADS), jnp.float32,
                                           minval=1.0, maxval=16.0))
    return {
        'x': x,
        'p': p,
        'positions': positions,
        'attn_norm': gain((DEPTH, D_MODEL)),
        'w_in': nrm((DEPTH, D_MODEL, IN_COLS), D_MODEL ** -0.5),
        'da_q_norm': gain((DEPTH, DA_DQK)),
        'da_k_norm': gain((DEPTH, DA_DQK)),
        'da_lambda_q1': nrm((DEPTH, DA_DQK), 0.1),
        'da_lambda_k1': nrm((DEPTH, DA_DQK), 0.1),
        'da_lambda_q2': nrm((DEPTH, DA_DQK), 0.1),
        'da_lambda_k2': nrm((DEPTH, DA_DQK), 0.1),
        'da_sub_norm': gain((DEPTH, DA_DV)),
        'ssd_conv_w': nrm((DEPTH, SSD_CONV, SSD_CONV_DIM), SSD_CONV ** -0.5),
        'ssd_conv_b': nrm((DEPTH, SSD_CONV_DIM), 0.02),
        'ssd_dt_bias': ssd_dt_bias,
        'ssd_a_log': ssd_a_log,
        'ssd_d': 1.0 + nrm((DEPTH, SSD_HEADS), 0.1),
        'ssd_norm': gain((DEPTH, SSD_DINNER)),
        'gla_w_gate2': nrm((DEPTH, GLA_GATE_RANK, GLA_HEADS * GLA_DK), GLA_GATE_RANK ** -0.5),
        'gla_b_gate': nrm((DEPTH, GLA_HEADS * GLA_DK), 0.02),
        'gla_norm': gain((DEPTH, GLA_DV)),
        'w_out': nrm((DEPTH, MIX_WIDTH, D_MODEL), MIX_WIDTH ** -0.5),
        'ffn_norm': gain((DEPTH, D_MODEL)),
        'w_ffn_gate': nrm((DEPTH, D_MODEL, D_FF), D_MODEL ** -0.5),
        'w_ffn_up': nrm((DEPTH, D_MODEL, D_FF), D_MODEL ** -0.5),
        'w_ffn_down': nrm((DEPTH, D_FF, D_MODEL), D_FF ** -0.5),
        'ple_w_proj': nrm((DEPTH, PLE_DIM, D_MODEL), PLE_DIM ** -0.5),
        'ple_w_gate': nrm((DEPTH, D_MODEL, D_MODEL), D_MODEL ** -0.5),
    }

def first_block(x, p, positions, attn_norm, w_in, da_q_norm, da_k_norm, da_lambda_q1,
              da_lambda_k1, da_lambda_q2, da_lambda_k2, da_sub_norm, ssd_conv_w, ssd_conv_b,
              ssd_dt_bias, ssd_a_log, ssd_d, ssd_norm, gla_w_gate2, gla_b_gate, gla_norm,
              w_out, ffn_norm, w_ffn_gate, w_ffn_up, w_ffn_down, ple_w_proj, ple_w_gate):
    h = x
    for i in range(DEPTH):
        lambda_init = 0.8 - 0.6 * math.exp(-0.3 * i)
        a = rms_norm(h, attn_norm[i])
        proj = a @ w_in[i]
        (da_q, da_k, da_v, ssd_z, ssd_xbc, ssd_dt,
         gla_q, gla_k, gla_v, gla_g, gla_lr) = jnp.split(proj, IN_SPLITS, axis=-1)
        y_da = diff_attention(da_q, da_k, da_v, positions, da_q_norm[i], da_k_norm[i],
                              da_lambda_q1[i], da_lambda_k1[i], da_lambda_q2[i],
                              da_lambda_k2[i], da_sub_norm[i], lambda_init)
        y_ssd = ssd_mixer(ssd_z, ssd_xbc, ssd_dt, ssd_conv_w[i], ssd_conv_b[i],
                          ssd_dt_bias[i], ssd_a_log[i], ssd_d[i], ssd_norm[i])
        y_gla = gla_mixer(gla_q, gla_k, gla_v, gla_g, gla_lr, gla_w_gate2[i],
                          gla_b_gate[i], gla_norm[i])
        mix = jnp.concatenate([y_da, y_ssd.astype(y_da.dtype), y_gla.astype(y_da.dtype)], axis=-1)
        h = h + mix @ w_out[i]
        f = rms_norm(h, ffn_norm[i])
        h = h + (jax.nn.silu(f @ w_ffn_gate[i]) * (f @ w_ffn_up[i])) @ w_ffn_down[i]
        h = h + jax.nn.sigmoid(h @ ple_w_gate[i]) * (p[i] @ ple_w_proj[i])
    return h


DEPTH_2 = 1

N_META = 16
HG_HEADS = 4
HG_HEAD_DIM = 128
D_HG = HG_HEADS * HG_HEAD_DIM
HG_CHUNK = 64
D_LRU = D_MODEL
LRU_BLOCKS = 8
LRU_BLOCK = D_LRU // LRU_BLOCKS
CONV_WIDTH = 4
LRU_C = 8.0
N_GROUPS = 4
EXPERTS_PER_GROUP = 8
N_EXPERTS = N_GROUPS * EXPERTS_PER_GROUP
TOP_K = 2
D_EXPERT = 512
MOE_BLOCK = 512
EPS = 1e-6
SPLIT_SIZES = (D_HG, D_HG, D_HG, D_HG, D_LRU, D_LRU, D_MODEL, D_MODEL)
D_IN = sum(SPLIT_SIZES)


def rmsnorm(x, g):
    xf = x.astype(jnp.float32)
    y = xf * lax.rsqrt(jnp.mean(xf * xf, axis=-1, keepdims=True) + EPS)
    return (y * g.astype(jnp.float32)).astype(x.dtype)

def hgrn2_chunked(q, k, v, log_f):
    B, T, H, DK = q.shape
    DV = v.shape[-1]
    C = HG_CHUNK
    NC = T // C

    def to_chunks(a):
        return a.reshape(B, NC, C, H, a.shape[-1]).transpose(1, 0, 3, 2, 4)

    qc, kc, vc, gc = to_chunks(q), to_chunks(k), to_chunks(v), to_chunks(log_f)
    causal = jnp.tril(jnp.ones((C, C), dtype=bool))[:, :, None]

    def step(S, inp):
        qb, kb, vb, gb = inp
        G = jnp.cumsum(gb, axis=2)
        diff = G[:, :, :, None, :] - G[:, :, None, :, :]
        decay = jnp.exp(jnp.where(causal, diff, -jnp.inf))
        scores = jnp.einsum('bhtd,bhsd,bhtsd->bhts', qb, kb, decay)
        o = (jnp.einsum('bhts,bhsv->bhtv', scores, vb)
             + jnp.einsum('bhtd,bhdv->bhtv', qb * jnp.exp(G), S))
        G_end = G[:, :, -1:, :]
        S_new = (jnp.exp(G_end[:, :, 0, :])[..., None] * S
                 + jnp.einsum('bhsd,bhsv->bhdv', kb * jnp.exp(G_end - G), vb))
        return S_new, o

    S0 = jnp.zeros((B, H, DK, DV), jnp.float32)
    _, o = lax.scan(step, S0, (qc, kc, vc, gc))
    return o.transpose(1, 0, 3, 2, 4).reshape(B, T, H, DV)

def hgrn2_branch(q_pre, f_pre, i_pre, og_pre, lb, norm_g):
    B, T, _ = q_pre.shape
    f32 = jnp.float32
    lb = lb.astype(f32)
    fp = f_pre.astype(f32)
    f = lb + (1.0 - lb) * jax.nn.sigmoid(fp)
    log_f = jnp.log(f)
    k = (1.0 - lb) * jax.nn.sigmoid(-fp)
    pad = (-N_META) % HG_CHUNK

    def prep(a):
        a = jnp.pad(a.astype(f32), ((0, 0), (pad, 0), (0, 0)))
        return a.reshape(B, T + pad, HG_HEADS, HG_HEAD_DIM)

    o = hgrn2_chunked(prep(q_pre), prep(k), prep(i_pre), prep(log_f))[:, pad:]
    o = o * lax.rsqrt(jnp.mean(o * o, axis=-1, keepdims=True) + EPS)
    o = o * norm_g.astype(f32).reshape(HG_HEADS, HG_HEAD_DIM)
    o = o.reshape(B, T, D_HG) * jax.nn.sigmoid(og_pre.astype(f32))
    return o.astype(q_pre.dtype)

def rglru_branch(xb, yb, conv_w, conv_b, w_r, b_r, w_i, b_i, lam):
    B, T, _ = xb.shape
    f32 = jnp.float32
    xc = lax.conv_general_dilated(
        xb, conv_w[:, None, :].astype(xb.dtype), window_strides=(1,),
        padding=[(CONV_WIDTH - 1, 0)], dimension_numbers=('NWC', 'WIO', 'NWC'),
        feature_group_count=D_LRU) + conv_b.astype(xb.dtype)
    xh = xc.reshape(B, T, LRU_BLOCKS, LRU_BLOCK)
    r = jax.nn.sigmoid(jnp.einsum('btni,nij->btnj', xh, w_r).reshape(B, T, D_LRU).astype(f32)
                       + b_r.astype(f32))
    i = jax.nn.sigmoid(jnp.einsum('btni,nij->btnj', xh, w_i).reshape(B, T, D_LRU).astype(f32)
                       + b_i.astype(f32))
    log_a = -LRU_C * r * jax.nn.softplus(-lam.astype(f32))
    a = jnp.exp(log_a)
    u = jnp.sqrt(-jnp.expm1(2.0 * log_a)) * (i * xc.astype(f32))

    def combine(left, right):
        a_l, b_l = left
        a_r, b_r2 = right
        return a_l * a_r, a_r * b_l + b_r2

    _, h = lax.associative_scan(combine, (a, u), axis=1)
    return (h * jax.nn.gelu(yb.astype(f32))).astype(xb.dtype)

def hier_moe(h, w_group, b_group, w_router, b_router, w_gate, w_up, w_down):
    B, T, D = h.shape
    N = B * T
    f32 = jnp.float32
    hf = h.reshape(N, D)
    group_logits = (hf @ w_group).astype(f32) + b_group.astype(f32)
    p_group = jax.nn.softmax(group_logits, axis=-1)
    g_sel = jnp.argmax(group_logits, axis=-1).astype(jnp.int32)
    p_sel = jnp.take_along_axis(p_group, g_sel[:, None], axis=-1)
    exp_logits = jnp.einsum('nd,gde->nge', hf, w_router).astype(f32) + b_router.astype(f32)
    sel_logits = jnp.take_along_axis(exp_logits, g_sel[:, None, None], axis=1)[:, 0]
    top_vals, top_idx = lax.top_k(sel_logits, TOP_K)
    weights = p_sel * jax.nn.softmax(top_vals, axis=-1)
    expert_ids = g_sel[:, None] * EXPERTS_PER_GROUP + top_idx.astype(jnp.int32)

    A = N * TOP_K
    e_flat = expert_ids.reshape(A)
    w_flat = weights.reshape(A)
    tok_flat = jnp.arange(A, dtype=jnp.int32) // TOP_K
    order = jnp.argsort(e_flat)
    e_sorted = e_flat[order]
    counts = jnp.zeros((N_EXPERTS,), jnp.int32).at[e_flat].add(1)
    starts = jnp.cumsum(counts) - counts
    pcounts = (counts + MOE_BLOCK - 1) // MOE_BLOCK * MOE_BLOCK
    pends = jnp.cumsum(pcounts)
    pstarts = pends - pcounts
    dest = pstarts[e_sorted] + (jnp.arange(A, dtype=jnp.int32) - starts[e_sorted])
    n_blocks = -(-A // MOE_BLOCK) + N_EXPERTS
    n_slots = n_blocks * MOE_BLOCK
    slot_tok = jnp.zeros((n_slots,), jnp.int32).at[dest].set(tok_flat[order])
    slot_w = jnp.zeros((n_slots,), f32).at[dest].set(w_flat[order])
    block_start = jnp.arange(n_blocks, dtype=jnp.int32) * MOE_BLOCK
    block_expert = jnp.minimum(jnp.searchsorted(pends, block_start, side='right'),
                               N_EXPERTS - 1).astype(jnp.int32)

    def run_block(args):
        toks, wts, e = args
        xb = hf[toks]
        y = (jax.nn.silu(xb @ w_gate[e]) * (xb @ w_up[e])) @ w_down[e]
        return y * wts[:, None].astype(y.dtype)

    ys = lax.map(run_block, (slot_tok.reshape(n_blocks, MOE_BLOCK),
                             slot_w.reshape(n_blocks, MOE_BLOCK), block_expert))
    out = jnp.zeros((N, D), h.dtype).at[slot_tok].add(ys.reshape(n_slots, D).astype(h.dtype))
    return out.reshape(B, T, D)

def mixer(hn, w_in, lb, hg_norm_g, conv_w, conv_b, w_r, b_r, w_i, b_i, lam, w_up_a, w_up_b, w_out):
    proj = hn @ w_in
    idx = [int(c) for c in np.cumsum(SPLIT_SIZES)[:-1]]
    q_pre, f_pre, i_pre, og_pre, lx, ly, ga, gb = jnp.split(proj, idx, axis=-1)
    o_a = hgrn2_branch(q_pre, f_pre, i_pre, og_pre, lb, hg_norm_g)
    o_b = rglru_branch(lx, ly, conv_w, conv_b, w_r, b_r, w_i, b_i, lam)
    merged = jax.nn.sigmoid(ga) * (o_a @ w_up_a) + jax.nn.sigmoid(gb) * (o_b @ w_up_b)
    return merged @ w_out

def second_inputs(seed: int = 0) -> dict:
    key = jax.random.key(seed)
    ks = jax.random.split(key, 26)
    f32 = jnp.float32
    nrm = lambda k, shape, scale: jax.random.normal(k, shape, f32) * scale
    u = jax.random.uniform(ks[13], (DEPTH_2, D_LRU), f32, minval=0.9, maxval=0.999)
    a0 = u ** (1.0 / LRU_C)
    return {
        "x": nrm(ks[0], (BATCH, SEQ, D_MODEL), 1.0),
        "meta_tokens": nrm(ks[1], (N_META, D_MODEL), 1.0),
        "norm1_g": 1.0 + nrm(ks[2], (DEPTH_2, D_MODEL), 0.02),
        "w_in": nrm(ks[3], (DEPTH_2, D_MODEL, D_IN), D_MODEL ** -0.5),
        "hg_lower_bounds": nrm(ks[4], (DEPTH_2 + 1, D_HG), 0.1),
        "hg_norm_g": 1.0 + nrm(ks[5], (DEPTH_2, D_HG), 0.02),
        "conv_w": nrm(ks[6], (DEPTH_2, CONV_WIDTH, D_LRU), CONV_WIDTH ** -0.5),
        "conv_b": nrm(ks[7], (DEPTH_2, D_LRU), 0.01),
        "lru_w_r": nrm(ks[8], (DEPTH_2, LRU_BLOCKS, LRU_BLOCK, LRU_BLOCK), LRU_BLOCK ** -0.5),
        "lru_b_r": nrm(ks[9], (DEPTH_2, D_LRU), 0.01),
        "lru_w_i": nrm(ks[10], (DEPTH_2, LRU_BLOCKS, LRU_BLOCK, LRU_BLOCK), LRU_BLOCK ** -0.5),
        "lru_b_i": nrm(ks[11], (DEPTH_2, D_LRU), 0.01),
        "lru_lambda": jnp.log(a0) - jnp.log1p(-a0),
        "w_up_a": nrm(ks[14], (DEPTH_2, D_HG, D_MODEL), D_HG ** -0.5),
        "w_up_b": nrm(ks[15], (DEPTH_2, D_LRU, D_MODEL), D_LRU ** -0.5),
        "w_out": nrm(ks[16], (DEPTH_2, D_MODEL, D_MODEL), D_MODEL ** -0.5),
        "norm2_g": 1.0 + nrm(ks[17], (DEPTH_2, D_MODEL), 0.02),
        "w_group": nrm(ks[18], (DEPTH_2, D_MODEL, N_GROUPS), D_MODEL ** -0.5),
        "b_group": nrm(ks[19], (DEPTH_2, N_GROUPS), 0.01),
        "w_router": nrm(ks[20], (DEPTH_2, N_GROUPS, D_MODEL, EXPERTS_PER_GROUP), D_MODEL ** -0.5),
        "b_router": nrm(ks[21], (DEPTH_2, N_GROUPS, EXPERTS_PER_GROUP), 0.01),
        "w_gate": nrm(ks[22], (DEPTH_2, N_EXPERTS, D_MODEL, D_EXPERT), D_MODEL ** -0.5),
        "w_up": nrm(ks[23], (DEPTH_2, N_EXPERTS, D_MODEL, D_EXPERT), D_MODEL ** -0.5),
        "w_down": nrm(ks[24], (DEPTH_2, N_EXPERTS, D_EXPERT, D_MODEL), D_EXPERT ** -0.5),
        "final_g": 1.0 + nrm(ks[25], (D_MODEL,), 0.02),
    }

def second_block(x, meta_tokens, norm1_g, w_in, hg_lower_bounds, hg_norm_g, conv_w, conv_b,
              lru_w_r, lru_b_r, lru_w_i, lru_b_i, lru_lambda, w_up_a, w_up_b, w_out,
              norm2_g, w_group, b_group, w_router, b_router, w_gate, w_up, w_down, final_g):
    B = x.shape[0]
    meta = jnp.broadcast_to(meta_tokens[None].astype(x.dtype), (B, N_META, D_MODEL))
    h = jnp.concatenate([meta, x], axis=1)
    lbs = jnp.cumsum(jax.nn.softmax(hg_lower_bounds.astype(jnp.float32), axis=0), axis=0)
    for l in range(DEPTH_2):
        mix = mixer(rmsnorm(h, norm1_g[l]), w_in[l], lbs[l], hg_norm_g[l], conv_w[l], conv_b[l],
                    lru_w_r[l], lru_b_r[l], lru_w_i[l], lru_b_i[l], lru_lambda[l],
                    w_up_a[l], w_up_b[l], w_out[l])
        h = h + mix.astype(h.dtype)
        ffn = hier_moe(rmsnorm(h, norm2_g[l]), w_group[l], b_group[l], w_router[l], b_router[l],
                       w_gate[l], w_up[l], w_down[l])
        h = h + ffn.astype(h.dtype)
    return rmsnorm(h, final_g)[:, N_META:]


def setup_inputs(seed=0):
    out = dict(first_inputs(seed))
    for name, value in second_inputs(seed + 1).items():
        if name != "x":
            out[name + "_2"] = value
    return out


def reference(
    x, p, positions, attn_norm, w_in, da_q_norm, da_k_norm, da_lambda_q1, da_lambda_k1,
    da_lambda_q2, da_lambda_k2, da_sub_norm, ssd_conv_w, ssd_conv_b, ssd_dt_bias, ssd_a_log,
    ssd_d, ssd_norm, gla_w_gate2, gla_b_gate, gla_norm, w_out, ffn_norm, w_ffn_gate, w_ffn_up,
    w_ffn_down, ple_w_proj, ple_w_gate, meta_tokens_2, norm1_g_2, w_in_2, hg_lower_bounds_2,
    hg_norm_g_2, conv_w_2, conv_b_2, lru_w_r_2, lru_b_r_2, lru_w_i_2, lru_b_i_2, lru_lambda_2,
    w_up_a_2, w_up_b_2, w_out_2, norm2_g_2, w_group_2, b_group_2, w_router_2, b_router_2,
    w_gate_2, w_up_2, w_down_2, final_g_2,
):
    x = first_block(
        x, p, positions, attn_norm, w_in, da_q_norm, da_k_norm, da_lambda_q1, da_lambda_k1,
        da_lambda_q2, da_lambda_k2, da_sub_norm, ssd_conv_w, ssd_conv_b, ssd_dt_bias, ssd_a_log,
        ssd_d, ssd_norm, gla_w_gate2, gla_b_gate, gla_norm, w_out, ffn_norm, w_ffn_gate,
        w_ffn_up, w_ffn_down, ple_w_proj, ple_w_gate,
    )
    return second_block(
        x, meta_tokens_2, norm1_g_2, w_in_2, hg_lower_bounds_2, hg_norm_g_2, conv_w_2, conv_b_2,
        lru_w_r_2, lru_b_r_2, lru_w_i_2, lru_b_i_2, lru_lambda_2, w_up_a_2, w_up_b_2, w_out_2,
        norm2_g_2, w_group_2, b_group_2, w_router_2, b_router_2, w_gate_2, w_up_2, w_down_2,
        final_g_2,
    )


_drawn_inputs = setup_inputs


def setup_inputs(seed=0):
    import zlib

    import numpy as np

    out = dict(_drawn_inputs(seed))
    spreads = {}
    factors = {'da_q_norm': 3.383,
     'da_k_norm': 4.221,
     'da_lambda_q1': 2.843,
     'da_sub_norm': 3.709,
     'ssd_norm': 2.718,
     'gla_b_gate': 5.251,
     'gla_norm': 3.696,
     'norm1_g_2': 3.499,
     'hg_lower_bounds_2': 3.283,
     'hg_norm_g_2': 5.91,
     'conv_b_2': 3.985,
     'lru_b_r_2': 8.0,
     'lru_b_i_2': 7.051,
     'norm2_g_2': 3.295,
     'b_group_2': 4.441,
     'b_router_2': 5.323,
     'final_g_2': 2.818}
    for name, (base, spread) in spreads.items():
        noise = np.random.default_rng([zlib.crc32(name.encode()), seed]).standard_normal(out[name].shape)
        drawn = base * np.exp(spread * noise) if base else spread * noise
        out[name] = __import__('jax').numpy.asarray(drawn.astype(out[name].dtype))
    for name, factor in factors.items():
        out[name] = (out[name] * factor).astype(out[name].dtype)
    return out
```

```python
import math
from contextlib import ExitStack

import concourse.bass as bass
from concourse import mybir
import numpy as np

F32 = mybir.dt.float32
I32 = mybir.dt.int32
ACT = mybir.ActivationFunctionType
ALU = mybir.AluOpType
AX = mybir.AxisListType

P = 128
D = 1024
KD = D // P
SEQ = 256
NT = SEQ // P
DEPTH = 2
EPS = 1e-6
SLOT = 4096
NB = 4
NPS = 8

DA_H, DQK, DV, ROT = 4, 64, 128, 16
ROPE_THETA = 500000.0
SSD_H, SSD_P, SSD_N, SSD_G, CONV = 8, 64, 128, 2, 4
GLA_H, GLA_DK, GLA_DV, GLA_C, GLA_RANK = 4, 64, 128, 64, 16
D_FF = 2816
KF = D_FF // P
MIX = 1536
KM = MIX // P
COL = dict(q=0, k=512, v=1024, z=1536, xbc=2048, dt=3072, gq=3080, gk=3336, gv=3592, gg=4104, lr=4616)

NM = 16
NTOK = NM + SEQ
HG_H = 4
LB = 8
NG, EPG = 4, 8
NE = NG * EPG
DE = 512
KE = DE // P
LEVELS = [64, 32, 16, 8, 4, 2, 1]

LAYER_TILES = [
    ("n1", 4), ("q", 2), ("k", 2), ("lr", 1), ("dt", 1), ("xbc", 4), ("gqk", 2), ("v", 2), ("z", 2), ("gv", 2), ("gg", 2),
    ("qkT", 4), ("sc", 8), ("at", 3), ("pv", 2),
    ("xbT", 3), ("cumc", 1), ("cumb", 4), ("cb", 1), ("yd", 2), ("st", 1), ("yo", 1),
    ("gk", 1), ("keT", 1), ("gst", 3), ("gat", 2), ("go", 2),
    ("mixT", 6), ("wo", 4), ("n2", 4), ("ffn", KF), ("dn", 4), ("n3", 4), ("pT", 1), ("pg", 4), ("pp", 4),
]
SECOND_TILES = [
    ("m1", 4), ("mm", 1), ("hf", 4), ("hq", 2), ("hi", 3), ("hog", 2), ("lx", 8), ("ly", 4), ("ga", 4), ("gb", 4),
    ("hkm", 1), ("hk0", 1), ("hsm", 1), ("hs0", 1), ("lev", 16), ("ho", 2), ("oaT", 2),
    ("lr_r", 8), ("lr_i", 8), ("ua", 4), ("ub", 4), ("wo2", 4), ("m2", 4), ("rt", 1),
]


def number_tiles():
    first, n = {}, 0
    for name, count in [("cp", 2)]:
        first[name] = n
        n += count
    for layer in range(DEPTH):
        for name, count in LAYER_TILES:
            first[name, layer] = n
            n += count
    for name, count in SECOND_TILES:
        first[name] = n
        n += count
    return first, n


TILE, N_TILES = number_tiles()

ROWS1 = 58
CP1 = dict(an=0, fn=8, cw=16, cb=48, gb=56)
CP2 = dict(n1=0, lb=8, cw=16, cb=48, br=56, bi=64, lam=72)
BC1 = dict(gq=(0, 64), gk=(64, 64), lq1=(128, 64), lk1=(192, 64), lq2=(256, 64), lk2=(320, 64),
           gsub=(384, 128), dtb=(512, 8), alog=(520, 8), dsk=(528, 8), ssdn=(536, 512), glan=(1048, 128))
NBC1 = 1176
BC2 = dict(hgn=(0, 512), n2=(512, 1024), fin=(1536, 1024), bg=(2560, 4), brt=(2564, 32))
NBC2 = 2596


def lambda_init(layer):
    return 0.8 - 0.6 * math.exp(-0.3 * layer)


def first_loads(d, layer):
    w = d["w_in"][layer].rearrange("(k p) n -> p k n", p=P)
    T = lambda name: TILE[name, layer]
    out = []

    def cols(c0, n, tile):
        out.append(([(0, KD, n, w[:, :, c0:c0 + n])], ("full", tile)))
    cols(COL["q"], 512, T("q") + 1)
    cols(COL["k"], 512, T("k") + 1)
    out.append(([(0, KD, 16, w[:, :, COL["lr"]:COL["lr"] + 16]), (KD * 16, KD, 8, w[:, :, COL["dt"]:COL["dt"] + 8])],
                ("full", T("dt"))))
    cols(COL["xbc"], 512, T("xbc") + 1)
    cols(COL["xbc"] + 512, 512, T("xbc") + 3)
    cols(COL["gq"], 512, T("gqk") + 1)
    cols(COL["v"], 512, T("v") + 1)
    cols(COL["z"], 512, T("z") + 1)
    cols(COL["gv"], 512, T("gv") + 1)
    cols(COL["gg"], 512, T("gg") + 1)
    rows(out, d["w_out"][layer], KM, T("wo") + 3)
    g = d["w_ffn_gate"][layer].rearrange("(k p) n -> p k n", p=P)
    u = d["w_ffn_up"][layer].rearrange("(k p) n -> p k n", p=P)
    for f in range(KF // 2):
        out.append(([(0, KD, 256, g[:, :, 256 * f:256 * f + 256]), (2048, KD, 256, u[:, :, 256 * f:256 * f + 256])],
                    ("full", T("ffn") + 2 * f + 1)))
    rows(out, d["w_ffn_down"][layer], KF, T("dn") + 3)
    rows(out, d["ple_w_gate"][layer], KD, T("pg") + 3)
    rows(out, d["ple_w_proj"][layer], 2, T("pp") + 3)
    return out


def rows(out, w, k_chunks, last_tile):
    v = w.rearrange("(k p) n -> p k n", p=P)
    for k in range(0, k_chunks, 4):
        n = min(4, k_chunks - k)
        out.append(([(0, n, D, v[:, k:k + n, :])], ("full", last_tile) if k + n == k_chunks else ("used",)))


def second_loads(d):
    w = d["w_in_2"][0].rearrange("(k p) n -> p k n", p=P)
    out = []
    for c0, tile in ((512, TILE["hf"] + 3), (0, TILE["hq"] + 1), (1024, TILE["hi"] + 2), (1536, TILE["hog"] + 1),
                     (2048, TILE["lx"] + 3), (2560, TILE["lx"] + 7), (3072, TILE["ly"] + 1), (3584, TILE["ly"] + 3),
                     (4096, TILE["ga"] + 1), (4608, TILE["ga"] + 3), (5120, TILE["gb"] + 1), (5632, TILE["gb"] + 3)):
        out.append(([(0, KD, 512, w[:, :, c0:c0 + 512])], ("full", tile)))
    r = [(0, LB, P, d["lru_w_r_2"][0].rearrange("n i j -> i n j")), (1024, LB, P, d["lru_w_i_2"][0].rearrange("n i j -> i n j"))]
    out.append((r, ("full", TILE["lr_i"] + 7)))
    rows(out, d["w_up_a_2"][0], 4, TILE["ua"] + 3)
    v = d["w_up_b_2"][0].rearrange("(k p) n -> p k n", p=P)
    out.append(([(0, 4, D, v[:, 0:4, :])], ("full", TILE["ub"] + 3)))
    out.append(([(0, 4, D, v[:, 4:8, :])], ("full", TILE["ub"] + 3)))
    rows(out, d["w_out_2"][0], KD, TILE["wo2"] + 3)
    return out


def program(nc, d, out):
    LOADS = first_loads(d, 0) + first_loads(d, 1) + second_loads(d)
    n, freed = 0, []
    for _, by in LOADS:
        if by[0] == "used":
            n += 1
            freed.append(("used", n))
        else:
            freed.append(by)
    N_LOADS = len(LOADS)
    full_at, filled = [], [0] * NB
    for c, (parts, _) in enumerate(LOADS):
        filled[c % NB] += 16 * len(parts)
        full_at.append(filled[c % NB])

    with ExitStack() as ctx:
        def sb(name, shape, dt=F32):
            return ctx.enter_context(nc.sbuf_tensor(name, shape, dt))

        sems = {}

        def sem(name):
            if name not in sems:
                sems[name] = ctx.enter_context(nc.semaphore(name))
            return sems[name]

        ring = sb("weights", [P, NB, SLOT])
        h = sb("h", [P, NT, D])
        hmeta = sb("h_meta", [P, D])
        xT = sb("xT", [P, KM, NTOK])
        xn = sb("xn", [P, NT, D])
        mix = sb("mix", [P, NT, MIX])
        bc = sb("bc", [P, NBC2])
        prow1 = mix[:, 0, 0:P]
        prow2 = mix[:, 0, P:2 * P]
        cp1 = sb("cp1", [P, DEPTH * ROWS1])
        cp2 = sb("cp2", [P, 80])
        gw2 = sb("gw2", [GLA_RANK, DEPTH, 256])
        wrt = sb("wrt", [P, KD, NG + NE])
        ident = sb("ident", [P, P])
        tri = sb("tri", [P, P])
        tri64 = sb("tri64", [P, P])
        ones = sb("ones", [P, P])
        neg = sb("neg", [P, P])
        lev = sb("lev", [P, 8, P])
        xi = sb("xi", [P, P], I32)
        xs_ = sb("xs_", [P, P], I32)
        xf = sb("xf", [P, P])
        pos = sb("pos", [P, NT], I32)
        posf = sb("posf", [P, NT])
        ang = sb("ang", [P, NT, 8])
        angk = sb("angk", [P, NT, 8])
        angi = sb("angi", [P, NT, 8], I32)
        cos = sb("cos", [P, NT, 8])
        sin = sb("sin", [P, NT, 8])
        frq = sb("frq", [P, 8])
        st1 = sb("st1", [P, 64])
        st2 = sb("st2", [P, 64])
        mhalf = sb("mhalf", [P, 64])
        s8 = sb("s8", [P, 32, 32])
        arena = sb("arena", [P, 18304])
        psum = [ctx.enter_context(nc.psum_tensor(f"bank{i}", [P, 512], F32)) for i in range(NPS)]

        class Carve:
            def __init__(self, at):
                self.at = at

            def take(self, *shape):
                n = int(np.prod(shape))
                v = arena[:, self.at:self.at + n]
                self.at += n
                assert self.at <= 18304, self.at
                if len(shape) == 2:
                    v = v.rearrange("p (a b) -> p a b", a=shape[0])
                elif len(shape) == 3:
                    v = v.rearrange("p (a b c) -> p a b c", a=shape[0], b=shape[1])
                elif len(shape) == 4:
                    v = v.rearrange("p (a b c e) -> p a b c e", a=shape[0], b=shape[1], c=shape[2])
                return v

        c = Carve(0)
        tm = c.take(NT, 3072)
        xbc = c.take(KD, SEQ + CONV - 1)
        gqk = c.take(4, SEQ)
        kz = c.take(3, 256)
        Sh = arena[:, NT * 3072:NT * 3072 + 2048].rearrange("p (a b e) -> p a b e", a=4, b=2)
        lrT = c.take(256)
        scratch = c.at
        qkT = c.take(2, DA_H, SEQ)
        sc = c.take(8, SEQ)
        attn = c.take(DA_H, SEQ)
        attnT = c.take(DA_H, 2, P)
        c = Carve(scratch)
        cx = c.take(KD, SEQ)
        xh = c.take(NT, 512)
        B0 = c.take(2, P)
        xdt = c.take(NT, 512)
        decay = c.take(NT, SSD_H, P)
        cbm = c.take(4, P)
        sst = cx[:, 0:2, :]
        xdte = cx[:, 2:4, :]
        c = Carve(scratch)
        gcum = c.take(2, SEQ)
        eb = c.take(2, SEQ)
        enb = c.take(2, SEQ)
        qd = c.take(2, SEQ)
        ki = c.take(2, SEQ)
        ke = c.take(2, SEQ)
        attm = c.take(NT, GLA_H, P)
        gtmp = c.take(2, SEQ)
        c = Carve(0)
        hid = c.take(KF, SEQ)
        sil = c.take(2, SEQ)
        sg = c.take(NT, D)
        ptm = c.take(NT, 256)
        pT = c.take(2, SEQ)
        c = Carve(0)
        lx = c.take(KD, NTOK + CONV - 1)
        ly = c.take(KD, SEQ)
        ga = c.take(KD, SEQ)
        gb = c.take(KD, SEQ)
        og = c.take(NT, 512)
        R = c.at
        fT = c.take(HG_H, NTOK)
        kT = c.take(HG_H, NTOK)
        qT = c.take(HG_H, SEQ)
        vt = c.take(3, 512)
        G = c.take(HG_H, SEQ)
        ke0 = c.take(HG_H, P)
        acc = c.take(NT, HG_H, P)
        S = c.take(2, HG_H, P)
        Gm = s8[:, 0:2, :].rearrange("p a (b e) -> p (a b) e", e=NM)
        c = Carve(R)
        xc = c.take(KD, NTOK)
        ra = c.take(KD, NTOK)
        iu = c.take(KD, NTOK)
        th = c.take(KD, NTOK)
        mflat = mix[:, :, :].rearrange("p a b -> p (a b)")
        wlev = mflat[:, 0:1024].rearrange("p (a b) -> p a b", a=HG_H)
        qlev = mflat[:, 1024:2048].rearrange("p (a b) -> p a b", a=HG_H)
        klev = mflat[:, 2048:3072].rearrange("p (a b) -> p a b", a=HG_H)
        oaT = mflat[:, 0:1024].rearrange("p (a b) -> p a b", a=4)
        mTt = mflat[:, 1024:3072].rearrange("p (a b) -> p a b", a=KD)
        oa = xn[:, 0, :].rearrange("p (a b) -> p a b", a=NT)
        c = Carve(0)
        hidE = c.take(2, KE, SEQ)
        silE = c.take(2, SEQ)
        gate = c.take(NT, NE)

        def bc1v(layer, name):
            o, n = BC1[name]
            return bc[:, layer * NBC1 + o:layer * NBC1 + o + n]

        def bc2v(name):
            o, n = BC2[name]
            return bc[:, o:o + n]

        def slot(ch, k, n, off=0):
            return ring[:, ch % NB, off:off + k * n].rearrange("p (k n) -> p k n", k=k)

        class Counts:

            def __init__(self):
                self.seen = {}

            def next(self, name, by=1):
                self.seen[name] = self.seen.get(name, 0) + by
                return self.seen[name]

        def psum_full(tile):
            return sem(f"psum_full{tile % NPS}")

        def psum_free(tile):
            return sem(f"psum_free{tile % NPS}")

        def fills(tile):
            return tile // NPS + 1

        def chunk_full(ch):
            return sem(f"chunk_full{ch % NB}")

        block = ctx.enter_context(nc.Block())

        E0 = N_LOADS
        LE = 4

        @block.sync
        def _(sp):
            sp.dma_start(h[:, :, :], d["x"][0].rearrange("(t p) n -> p t n", p=P)).then_inc(sem("x_loaded"), 16)
            for ch, (parts, _) in enumerate(LOADS):
                if ch >= NB:
                    kind, at = freed[ch - NB]
                    if kind == "used":
                        sp.wait_ge(sem("chunks_used"), at)
                    else:
                        sp.wait_ge(psum_full(at), fills(at))
                for off, k, nn, src in parts:
                    sp.dma_start(slot(ch, k, nn, off), src).then_inc(sem(f"chunk_full{ch % NB}"), 16)
            wg = d["w_gate_2"][0].rearrange("e (k p) n -> e p k n", p=P)
            wu = d["w_up_2"][0].rearrange("e (k p) n -> e p k n", p=P)
            wd = d["w_down_2"][0].rearrange("e (k p) n -> e p k n", p=P)

            def expert_load(e, j, c3):
                src, k = ((wg, KD), (wu, KD), (wd, KE))[c3]
                s = (E0 + 3 * j + c3) % NB
                if isinstance(e, int):
                    v = src[e]
                else:
                    v = src[bass.ds(e, 1)].rearrange("e p k n -> (e p) k n")
                sp.dma_start(ring[:, s, :].rearrange("p (k n) -> p k n", k=k), v).then_inc(sem(f"chunk_full{s}"), 16)

            for q in range(NB):
                kind, at = freed[E0 - NB + q]
                if kind == "used":
                    sp.wait_ge(sem("chunks_used"), at)
                else:
                    sp.wait_ge(psum_full(at), fills(at))
                expert_load(q // 3, q // 3, q % 3)

            def chunk_used(i, q):
                done = "down_done" if q % 3 == 2 else "gate_up_done"
                sp.wait_ge(sem(done), i * (4 * LE) + (4 * (q // 3) + 4))

            for q in range(NB, 3 * LE):
                chunk_used(0, q - NB)
                expert_load(q // 3, q // 3, q % 3)
            with sp.Fori(1, NE // LE) as i:
                for q in range(3 * LE):
                    chunk_used(i, q - NB)
                    expert_load(i * LE + q // 3, q // 3, q % 3)
            sp.wait_ge(sem("xn_ready"), 2 * DEPTH + 3)
            sp.dma_start(out[0].rearrange("(t p) n -> p t n", p=P), xn[:, :, :]).then_inc(sem("out_stored"), 16)
            sp.wait_ge(sem("out_stored"), 16)

        @block.gpsimd
        def _(g):
            n = Counts()
            g.memset(ident[:, :], 0.0).then_inc(sem("g_zero"), 1)
            g.memset(ones[:, :], 1.0).then_inc(sem("g_zero"), 1)
            g.memset(neg[:, :], 0.0).then_inc(sem("g_zero"), 1)
            g.memset(tri64[:, :], 0.0).then_inc(sem("g_zero"), 1)
            g.wait_ge(sem("g_zero"), n.next("g_zero", 4))
            g.memset(tri64[0:64, 0:64], 1.0).then_inc(sem("g_zero"), 1)
            g.wait_ge(sem("g_zero"), n.next("g_zero"))
            g.memset(tri64[64:P, 64:P], 1.0).then_inc(sem("g_zero"), 1)
            g.wait_ge(sem("g_zero"), n.next("g_zero"))
            g.affine_select(out=ident[:, :], in_=ident[:, :], compare_op=ALU.not_equal, fill=1.0, base=0,
                            pattern=[[-1, P]], channel_multiplier=1).then_inc(sem("masks"), 1)
            g.affine_select(out=tri[:, :], in_=ones[:, :], compare_op=ALU.is_ge, fill=0.0, base=0,
                            pattern=[[1, P]], channel_multiplier=-1).then_inc(sem("masks"), 1)
            g.affine_select(out=tri64[:, :], in_=tri64[:, :], compare_op=ALU.is_ge, fill=0.0, base=0,
                            pattern=[[1, P]], channel_multiplier=-1).then_inc(sem("masks"), 1)
            g.affine_select(out=neg[:, :], in_=neg[:, :], compare_op=ALU.is_ge, fill=-1e30, base=0,
                            pattern=[[-1, P]], channel_multiplier=1).then_inc(sem("masks"), 1)
            g.iota(xi[:, :], pattern=[[1, P]], base=0, channel_multiplier=0).then_inc(sem("iotas"), 1)
            g.iota(xs_[:, :], pattern=[[0, P]], base=0, channel_multiplier=1).then_inc(sem("iotas"), 1)
            for i in range(8):
                g.memset(frq[:, i:i + 1], float(np.float32(ROPE_THETA) ** np.float32(-2.0 * i / ROT)))
            g.memset(mhalf[:, :], -0.5).then_inc(sem("consts"), 1)
            for layer in range(DEPTH):
                r0 = ROWS1 * layer
                for name, key, cnt in (("an", "attn_norm", 8), ("fn", "ffn_norm", 8), ("cb", "ssd_conv_b", 8), ("gb", "gla_b_gate", 2)):
                    g.dma_start(prow1[r0 + CP1[name]:r0 + CP1[name] + cnt, :],
                                d[key][layer].rearrange("(c p) -> c p", p=P)).then_inc(sem("rows_loaded"), 16)
                g.dma_start(prow1[r0 + 16:r0 + 48, :],
                            d["ssd_conv_w"][layer].rearrange("j (c p) -> (j c) p", p=P)).then_inc(sem("rows_loaded"), 16)
            for name, key, cnt in (("n1", "norm1_g_2", 8), ("cb", "conv_b_2", 8), ("br", "lru_b_r_2", 8),
                                   ("bi", "lru_b_i_2", 8), ("lam", "lru_lambda_2", 8)):
                g.dma_start(prow2[CP2[name]:CP2[name] + cnt, :],
                            d[key][0].rearrange("(c p) -> c p", p=P)).then_inc(sem("rows_loaded"), 16)
            g.dma_start(prow2[16:48, :], d["conv_w_2"][0].rearrange("j (c p) -> (j c) p", p=P)).then_inc(sem("rows_loaded"), 16)
            g.dma_start(prow2[8:16, :], d["hg_lower_bounds_2"].rearrange("j (c p) -> (j c) p", p=P)).then_inc(sem("rows_loaded"), 16)
            g.dma_start(pos[:, :], d["positions"][0].rearrange("(t p) -> p t", p=P),
                        allow_slow_non_contiguous=True).then_inc(sem("bc_loaded"), 16)
            for layer in range(DEPTH):
                for name, key in (("gq", "da_q_norm"), ("gk", "da_k_norm"), ("lq1", "da_lambda_q1"), ("lk1", "da_lambda_k1"),
                                  ("lq2", "da_lambda_q2"), ("lk2", "da_lambda_k2"), ("gsub", "da_sub_norm"),
                                  ("dtb", "ssd_dt_bias"), ("alog", "ssd_a_log"), ("dsk", "ssd_d"), ("ssdn", "ssd_norm"),
                                  ("glan", "gla_norm")):
                    g.dma_start(bc1v(layer, name), d[key][layer].partition_broadcast(P)).then_inc(sem("bc_loaded"), 16)
                g.dma_start(gw2[:, layer, :], d["gla_w_gate2"][layer]).then_inc(sem("bc_loaded"), 16)
            g.dma_start(hmeta[0:NM, :], d["meta_tokens_2"]).then_inc(sem("bc2_loaded"), 16)
            g.dma_start(wrt[:, :, 0:NG], d["w_group_2"][0].rearrange("(k p) n -> p k n", p=P),
                        allow_slow_non_contiguous=True).then_inc(sem("bc2_loaded"), 16)
            for q in range(NG):
                g.dma_start(wrt[:, :, NG + EPG * q:NG + EPG * q + EPG], d["w_router_2"][0, q].rearrange("(k p) n -> p k n", p=P),
                            allow_slow_non_contiguous=True).then_inc(sem("bc2_loaded"), 16)

            def rsqrt(cols):
                g.wait_ge(sem("power_asked"), n.next("power_asked"))
                g.tensor_tensor(st2[:, 0:cols], st1[:, 0:cols], mhalf[:, 0:cols], ALU.pow).then_inc(sem("power_done"), 1)

            for layer in range(DEPTH):
                rsqrt(2)
                if layer:
                    g.wait_ge(sem("layer_done"), n.next("layer_done"))
                g.memset(kz[:, :, :], 0.0)
                g.memset(xbc[:, :, 0:CONV - 1], 0.0).then_inc(sem("zeros"), 1)
                rsqrt(32)
                rsqrt(8)
                g.wait_ge(sem("conv_sum"), n.next("conv_sum"))
                g.memset(Sh[:, :, :, :], 0.0).then_inc(sem("states_zero"), 1)
                rsqrt(4)
                rsqrt(8)
                rsqrt(2)
                g.wait_ge(sem("ptm_free"), n.next("ptm_free"))
                g.dma_start(ptm[:, :, :], d["p"][layer, 0].rearrange("(t p) n -> p t n", p=P)).then_inc(sem("p_loaded"), 16)
            g.wait_ge(sem("layer_done"), n.next("layer_done"))
            for name, key in (("hgn", "hg_norm_g_2"), ("n2", "norm2_g_2"), ("bg", "b_group_2")):
                g.dma_start(bc2v(name), d[key][0].partition_broadcast(P)).then_inc(sem("bc2_loaded"), 16)
            g.dma_start(bc2v("fin"), d["final_g_2"].partition_broadcast(P)).then_inc(sem("bc2_loaded"), 16)
            g.dma_start(bc2v("brt"), d["b_router_2"][0].rearrange("g e -> (g e)").partition_broadcast(P)).then_inc(sem("bc2_loaded"), 16)
            g.memset(lx[:, :, 0:CONV - 1], 0.0).then_inc(sem("zeros"), 1)
            rsqrt(3)
            for i in range(len(LEVELS)):
                g.wait_ge(sem("w_ready"), n.next("w_ready"))
                if i:
                    g.wait_ge(psum_full(TILE["lev"] + 2 * i - 1), fills(TILE["lev"] + 2 * i - 1))
                else:
                    g.wait_ge(sem("h_norm"), n.next("h_norm"))
                g.tensor_tensor(klev, kT[:, :, NM:NTOK], wlev, ALU.mult).then_inc(sem("klev_ready"), 1)
            rsqrt(8)
            rsqrt(2)
            rsqrt(2)

        @block.tensor
        def _(pe):
            n = Counts()
            mm = nc.tensor.matmul

            def claim(tile):
                if tile >= NPS:
                    pe.wait_ge(psum_free(tile - NPS), fills(tile - NPS))
                return psum[tile % NPS]

            def tokens_out(tile, ch, t0=NM):
                pe.wait_ge(chunk_full(ch), full_at[ch])
                w = slot(ch, KD, 512)
                for t in range(NT):
                    b = claim(tile + t)
                    for k in range(KD):
                        ins = mm(b[:, :], xT[:, k, t0 + P * t:t0 + P * t + P], w[:, k, :], start=(k == 0), stop=(k == KD - 1))
                    ins.then_inc(psum_full(tile + t), 1)

            def channels_out(tile, ch, n0, nt, per):
                pe.wait_ge(chunk_full(ch), full_at[ch])
                w = slot(ch, KD, 512)
                for m in range(4):
                    b = claim(tile + m // per)
                    o = (m % per) * nt
                    for k in range(KD):
                        ins = mm(b[:, o:o + nt], w[:, k, P * m:P * m + P], xT[:, k, n0:n0 + nt], start=(k == 0), stop=(k == KD - 1))
                    if m % per == per - 1:
                        ins.then_inc(psum_full(tile + m // per), 1)

            def transposes(tile, src, cols, q=P):
                b = claim(tile)
                for j, at in enumerate(cols):
                    ins = nc.tensor.transpose(b[:, q * j:q * j + q], src[0:q, at:at + P], ident[0:q, 0:q])
                ins.then_inc(psum_full(tile), 1)

            def norm_turns(tile, src):
                for t in range(NT):
                    for half in range(2):
                        transposes(tile + 2 * t + half, src[:, t, :], [512 * half + P * j for j in range(4)])

            def rows_out(tile, ch, k_chunks, lhs, mark):
                banks = [claim(tile + i) for i in range(4)]
                for k in range(k_chunks):
                    if k % 4 == 0:
                        pe.wait_ge(chunk_full(ch), full_at[ch])
                    kn = min(4, k_chunks - (k - k % 4))
                    w = slot(ch, kn, D)
                    last = k == k_chunks - 1
                    for i in range(4):
                        t, half = divmod(i, 2)
                        ins = mm(banks[i][:, :], lhs(k, t), w[:, k % 4, 512 * half:512 * half + 512], start=(k == 0), stop=last)
                        if last:
                            ins.then_inc(psum_full(tile + i), 1)
                    if k % 4 == 3 and not last:
                        ins.then_inc(sem("chunks_used"), 1)
                    if k % 4 == 3:
                        ch += 1
                return ch

            pe.wait_ge(sem("rows_loaded"), 16 * 17)
            pe.wait_ge(sem("masks"), 4)
            for i, (src, r) in enumerate(((prow1, DEPTH * ROWS1), (prow2, 80))):
                b = claim(i)
                nc.tensor.transpose(b[:, 0:r], src[0:r, :], ident[0:r, 0:r]).then_inc(psum_full(i), 1)

            ch = 0
            for layer in range(DEPTH):
                T = lambda name: TILE[name, layer]
                pe.wait_ge(sem("xn_ready"), n.next("xn_ready"))
                norm_turns(T("n1"), xn)
                for i in range(4):
                    pe.wait_ge(psum_free(T("n1") + i), fills(T("n1") + i))
                tokens_out(T("q"), ch)
                tokens_out(T("k"), ch + 1)
                pe.wait_ge(chunk_full(ch + 2), full_at[ch + 2])
                b = claim(T("lr"))
                w = slot(ch + 2, KD, 16)
                for k in range(KD):
                    ins = mm(b[0:16, 0:SEQ], w[:, k, :], xT[:, k, NM:NTOK], start=(k == 0), stop=(k == KD - 1))
                ins.then_inc(psum_full(T("lr")), 1)
                b = claim(T("dt"))
                w = slot(ch + 2, KD, 8, KD * 16)
                for t in range(NT):
                    for k in range(KD):
                        ins = mm(b[:, 8 * t:8 * t + 8], xT[:, k, NM + P * t:NM + P * t + P], w[:, k, :], start=(k == 0), stop=(k == KD - 1))
                ins.then_inc(psum_full(T("dt")), 1)
                channels_out(T("xbc"), ch + 3, NM, SEQ, 2)
                channels_out(T("xbc") + 2, ch + 4, NM, SEQ, 2)
                channels_out(T("gqk"), ch + 5, NM, SEQ, 2)
                tokens_out(T("v"), ch + 6)
                tokens_out(T("z"), ch + 7)
                tokens_out(T("gv"), ch + 8)
                tokens_out(T("gg"), ch + 9)
                ch += 10
                pe.wait_ge(sem("qk_ready"), n.next("qk_ready"))
                for t in range(NT):
                    for j in range(2):
                        transposes(T("qkT") + 2 * t + j, tm[:, t, :], [512 * j + P * q for q in range(4)])
                for i in range(4):
                    pe.wait_ge(psum_free(T("qkT") + i), fills(T("qkT") + i))
                for t in range(NT):
                    for comp in range(2):
                        for hp in range(2):
                            tile = T("sc") + 4 * t + 2 * comp + hp
                            b = claim(tile)
                            for j in range(2):
                                hh = 2 * hp + j
                                lo = 64 * comp
                                ins = mm(b[:, 256 * j:256 * j + P * (t + 1)], qkT[lo:lo + 64, 0, hh, P * t:P * t + P],
                                         qkT[lo:lo + 64, 1, hh, 0:P * (t + 1)], start=True, stop=True)
                            ins.then_inc(psum_full(tile), 1)
                at = T("at")
                for t in range(NT):
                    pe.wait_ge(sem("attn_ready"), n.next("attn_ready"))
                    for kt in range(t + 1):
                        transposes(at + t + kt, attn.rearrange("p a b -> p (a b)"), [256 * q + P * kt for q in range(4)])
                    for kt in range(t + 1):
                        pe.wait_ge(psum_free(at + t + kt), fills(at + t + kt))
                    b = claim(T("pv") + t)
                    for hh in range(DA_H):
                        for kt in range(t + 1):
                            ins = mm(b[:, P * hh:P * hh + P], attnT[:, hh, kt, :], tm[:, kt, 1024 + P * hh:1024 + P * hh + P],
                                     start=(kt == 0), stop=(kt == t))
                    ins.then_inc(psum_full(T("pv") + t), 1)
                pe.wait_ge(sem("conv_ready"), n.next("conv_ready"))
                for i in range(3):
                    tile = T("xbT") + i
                    b = claim(tile)
                    for j in range(4 if i < 2 else 2):
                        src = cx[:, j, P * i:P * i + P] if i < 2 else cx[:, 4 + j, 0:P]
                        ins = nc.tensor.transpose(b[:, P * j:P * j + P], src, ident[:, :])
                    ins.then_inc(psum_full(tile), 1)
                pe.wait_ge(sem("da_ready"), n.next("da_ready"))
                b = claim(T("cumc"))
                dA = s8[:, 2:4, 0:8]
                for t in range(NT):
                    mm(b[:, 16 * t:16 * t + 8], tri[:, :], dA[:, t, :], start=True, stop=True)
                    ins = mm(b[:, 16 * t + 8:16 * t + 16], ones[:, :], dA[:, t, :], start=True, stop=True)
                ins.then_inc(psum_full(T("cumc")), 1)
                for t in range(NT):
                    for q in range(2):
                        tile = T("cumb") + 2 * t + q
                        b = claim(tile)
                        for j in range(4):
                            hh = 4 * q + j
                            ins = mm(b[:, P * j:P * j + P], dA[:, t, hh:hh + 1].to_broadcast([P, P]), tri[:, :], start=True, stop=True)
                        ins.then_inc(psum_full(tile), 1)
                b = claim(T("cb"))
                for t in range(NT):
                    for gg in range(2):
                        o = P * (2 * t + gg)
                        ins = mm(b[:, o:o + P], cx[:, 4 + gg, P * t:P * t + P], cx[:, 6 + gg, P * t:P * t + P], start=True, stop=True)
                ins.then_inc(psum_full(T("cb")), 1)
                pe.wait_ge(sem("ssd_ready"), n.next("ssd_ready"))
                for t in range(NT):
                    b = claim(T("yd") + t)
                    for hh in range(SSD_H):
                        ins = mm(b[:, 64 * hh:64 * hh + 64], decay[:, t, hh, :], xdt[:, t, 64 * hh:64 * hh + 64], start=True, stop=True)
                    ins.then_inc(psum_full(T("yd") + t), 1)
                b = claim(T("st"))
                xe = xdte.rearrange("p a b -> p (a b)")
                for gg in range(2):
                    ins = mm(b[:, 256 * gg:256 * gg + 256], B0[:, gg, :], xe[:, 256 * gg:256 * gg + 256], start=True, stop=True)
                ins.then_inc(psum_full(T("st")), 1)
                pe.wait_ge(psum_free(T("st")), fills(T("st")))
                b = claim(T("yo"))
                for gg in range(2):
                    ins = mm(b[:, 256 * gg:256 * gg + 256], cx[:, 6 + gg, P:2 * P], sst[:, gg, :], start=True, stop=True)
                ins.then_inc(psum_full(T("yo")), 1)
                b = claim(T("gk"))
                if layer == 0:
                    pe.wait_ge(sem("bc_loaded"), 16 * 27)
                for j in range(2):
                    ins = mm(b[:, 256 * j:256 * j + 256], gw2[:, layer, P * j:P * j + P], lrT[0:GLA_RANK, :], start=True, stop=True)
                ins.then_inc(psum_full(T("gk")), 1)
                pe.wait_ge(sem("gla_ready"), n.next("gla_ready"))
                b = claim(T("keT"))
                for t in range(NT):
                    for j in range(2):
                        o = P * (2 * t + j)
                        ins = nc.tensor.transpose(b[:, o:o + P], ke[:, j, P * t:P * t + P], ident[:, :])
                ins.then_inc(psum_full(T("keT")), 1)
                pe.wait_ge(psum_free(T("keT")), fills(T("keT")))
                for cc in range(3):
                    b = claim(T("gst") + cc)
                    for j in range(2):
                        ins = mm(b[:, 256 * j:256 * j + 256], kz[:, cc, P * j:P * j + P],
                                 tm[:, cc // 2, 2048 + 256 * j:2048 + 256 * j + 256], start=True, stop=True)
                    ins.then_inc(psum_full(T("gst") + cc), 1)
                for par in range(2):
                    b = claim(T("gat") + par)
                    lo = 64 * par
                    for t in range(NT):
                        for j in range(2):
                            o = P * (2 * t + j)
                            ins = mm(b[:, o:o + P], ki[lo:lo + 64, j, P * t:P * t + P], qd[lo:lo + 64, j, P * t:P * t + P], start=True, stop=True)
                    ins.then_inc(psum_full(T("gat") + par), 1)
                for par in range(2):
                    pe.wait_ge(psum_free(T("gat") + par), fills(T("gat") + par))
                pe.wait_ge(psum_free(T("gst") + 2), fills(T("gst") + 2))
                for t in range(NT):
                    b = claim(T("go") + t)
                    for j in range(2):
                        for half in range(2):
                            cc = 2 * t + half
                            mm(b[64 * half:64 * half + 64, 256 * j:256 * j + 256], qd[:, j, 64 * cc:64 * cc + 64], Sh[:, cc, j, :],
                               start=True, stop=False, skip_group_check=True)
                        for par in range(2):
                            o = P * (2 * j + par)
                            ins = mm(b[:, o:o + P], attm[:, t, 2 * j + par, :], tm[:, t, 2048 + o:2048 + o + P],
                                     start=False, stop=True, skip_group_check=True)
                    ins.then_inc(psum_full(T("go") + t), 1)
                pe.wait_ge(sem("mix_ready"), n.next("mix_ready"))
                for t in range(NT):
                    for q in range(3):
                        transposes(T("mixT") + 3 * t + q, mix[:, t, :], [512 * q + P * j for j in range(4)])
                for i in range(6):
                    pe.wait_ge(psum_free(T("mixT") + i), fills(T("mixT") + i))
                xcols = lambda k, t: xT[:, k, NM + P * t:NM + P * t + P]
                ch = rows_out(T("wo"), ch, KM, xcols, True)
                pe.wait_ge(sem("xn_ready"), n.next("xn_ready"))
                norm_turns(T("n2"), xn)
                for i in range(4):
                    pe.wait_ge(psum_free(T("n2") + i), fills(T("n2") + i))
                for f in range(KF):
                    if f % 2 == 0:
                        pe.wait_ge(chunk_full(ch + f // 2), full_at[ch + f // 2])
                    b = claim(T("ffn") + f)
                    for q in range(2):
                        w = slot(ch + f // 2, KD, 256, 2048 * q)
                        for k in range(KD):
                            ins = mm(b[:, 256 * q:256 * q + 256], w[:, k, P * (f % 2):P * (f % 2) + P], xT[:, k, NM:NTOK], start=(k == 0), stop=(k == KD - 1))
                    ins.then_inc(psum_full(T("ffn") + f), 1)
                ch += KF // 2
                for i in range(NPS):
                    pe.wait_ge(psum_free(T("ffn") + KF - NPS + i), fills(T("ffn") + KF - NPS + i))
                ch = rows_out(T("dn"), ch, KF, lambda k, t: hid[:, k, P * t:P * t + P], True) + 1
                pe.wait_ge(sem("h_ready"), n.next("h_ready"))
                norm_turns(T("n3"), h)
                pe.wait_ge(sem("p_loaded"), 16 * (layer + 1))
                b = claim(T("pT"))
                for j in range(2):
                    for t in range(NT):
                        o = 256 * j + P * t
                        ins = nc.tensor.transpose(b[:, o:o + P], ptm[:, t, P * j:P * j + P], ident[:, :])
                ins.then_inc(psum_full(T("pT")), 1)
                for i in range(4):
                    pe.wait_ge(psum_free(T("n3") + i), fills(T("n3") + i))
                pe.wait_ge(psum_free(T("pT")), fills(T("pT")))
                ch = rows_out(T("pg"), ch, KD, xcols, True)
                ch = rows_out(T("pp"), ch, 2, lambda k, t: pT[:, k, P * t:P * t + P], True) + 1

            pe.wait_ge(sem("xn_ready"), n.next("xn_ready"))
            norm_turns(TILE["m1"], xn)
            b = claim(TILE["mm"])
            for k in range(KD):
                ins = nc.tensor.transpose(b[:, NM * k:NM * k + NM], hmeta[0:NM, P * k:P * k + P], ident[0:NM, 0:NM])
            ins.then_inc(psum_full(TILE["mm"]), 1)
            for i in range(5):
                pe.wait_ge(psum_free(TILE["m1"] + i), fills(TILE["m1"] + i))
            channels_out(TILE["hf"], ch, 0, NTOK, 1)
            channels_out(TILE["hq"], ch + 1, NM, SEQ, 2)
            tokens_out(TILE["hi"], ch + 2)
            b = claim(TILE["hi"] + 2)
            w = slot(ch + 2, KD, 512)
            for k in range(KD):
                ins = mm(b[0:NM, :], xT[:, k, 0:NM], w[:, k, :], start=(k == 0), stop=(k == KD - 1))
            ins.then_inc(psum_full(TILE["hi"] + 2), 1)
            tokens_out(TILE["hog"], ch + 3)
            channels_out(TILE["lx"], ch + 4, 0, NTOK, 1)
            channels_out(TILE["lx"] + 4, ch + 5, 0, NTOK, 1)
            for i, name in enumerate(("ly", "ga", "gb")):
                channels_out(TILE[name], ch + 6 + 2 * i, NM, SEQ, 2)
                channels_out(TILE[name] + 2, ch + 7 + 2 * i, NM, SEQ, 2)
            ch += 12
            pe.wait_ge(sem("ke_ready"), n.next("ke_ready"))
            b = claim(TILE["hkm"])
            for hh in range(HG_H):
                ins = nc.tensor.transpose(b[0:NM, P * hh:P * hh + P], fT[:, hh, 0:NM], ident[:, :])
            ins.then_inc(psum_full(TILE["hkm"]), 1)
            b = claim(TILE["hk0"])
            for hh in range(HG_H):
                ins = nc.tensor.transpose(b[:, P * hh:P * hh + P], klev[:, hh, 0:P], ident[:, :])
            ins.then_inc(psum_full(TILE["hk0"]), 1)
            pe.wait_ge(psum_free(TILE["hkm"]), fills(TILE["hkm"]))
            pe.wait_ge(psum_free(TILE["hk0"]), fills(TILE["hk0"]))
            b = claim(TILE["hsm"])
            kem = wlev[0:NM, :, 0:P]
            for hh in range(HG_H):
                ins = mm(b[:, P * hh:P * hh + P], kem[:, hh, :], vt[0:NM, 2, P * hh:P * hh + P], start=True, stop=True)
            ins.then_inc(psum_full(TILE["hsm"]), 1)
            b = claim(TILE["hs0"])
            for hh in range(HG_H):
                ins = mm(b[:, P * hh:P * hh + P], ke0[:, hh, :], vt[:, 0, P * hh:P * hh + P], start=True, stop=True)
            ins.then_inc(psum_full(TILE["hs0"]), 1)
            for i in range(len(LEVELS) + 1):
                if i < len(LEVELS):
                    pe.wait_ge(sem("klev_ready"), n.next("klev_ready"))
                    pe.wait_ge(sem("qlev_ready"), n.next("qlev_ready"))
                    ka, qa = klev, qlev
                else:
                    ka, qa = kT[:, :, NM:NTOK], qT
                for t in range(NT):
                    tile = TILE["lev"] + 2 * i + t
                    b = claim(tile)
                    for hh in range(HG_H):
                        ins = mm(b[:, P * hh:P * hh + P], ka[:, hh, P * t:P * t + P], qa[:, hh, P * t:P * t + P], start=True, stop=True)
                    ins.then_inc(psum_full(tile), 1)
            pe.wait_ge(sem("inter_ready"), n.next("inter_ready"))
            for t in range(NT):
                b = claim(TILE["ho"] + t)
                for hh in range(HG_H):
                    mm(b[:, P * hh:P * hh + P], qlev[:, hh, P * t:P * t + P], S[:, t, hh, :], start=True, stop=False)
                    ins = mm(b[:, P * hh:P * hh + P], acc[:, t, hh, :], vt[:, t, P * hh:P * hh + P], start=False, stop=True)
                ins.then_inc(psum_full(TILE["ho"] + t), 1)
            pe.wait_ge(sem("oa_ready"), n.next("oa_ready"))
            for t in range(NT):
                transposes(TILE["oaT"] + t, oa[:, t, :], [P * j for j in range(4)])
            pe.wait_ge(sem("xc_ready"), n.next("xc_ready"))
            pe.wait_ge(chunk_full(ch), full_at[ch])
            for i, name in enumerate(("lr_r", "lr_i")):
                w = slot(ch, LB, P, 1024 * i)
                for m in range(LB):
                    b = claim(TILE[name] + m)
                    mm(b[:, 0:NTOK], w[:, m, :], xc[:, m, :], start=True, stop=True).then_inc(psum_full(TILE[name] + m), 1)
            ch += 1
            for i in range(2):
                pe.wait_ge(psum_free(TILE["oaT"] + i), fills(TILE["oaT"] + i))
            pe.wait_ge(chunk_full(ch), full_at[ch])
            for m in range(KD):
                b = claim(TILE["ua"] + m // 2)
                o = 256 * (m % 2)
                for k in range(4):
                    ins = mm(b[:, o:o + 256], slot(ch, 4, D)[:, k, P * m:P * m + P], oaT[:, k, :], start=(k == 0), stop=(k == 3))
                if m % 2:
                    ins.then_inc(psum_full(TILE["ua"] + m // 2), 1)
            pe.wait_ge(sem("lru_ready"), n.next("lru_ready"))
            pe.wait_ge(chunk_full(ch + 1), full_at[ch + 1])
            pe.wait_ge(chunk_full(ch + 2), full_at[ch + 2])
            for m in range(KD):
                b = claim(TILE["ub"] + m // 2)
                o = 256 * (m % 2)
                for k in range(KD):
                    ins = mm(b[:, o:o + 256], slot(ch + 1 + k // 4, 4, D)[:, k % 4, P * m:P * m + P], th[:, k, NM:NTOK], start=(k == 0), stop=(k == KD - 1))
                if m % 2:
                    ins.then_inc(psum_full(TILE["ub"] + m // 2), 1)
            ch += 3
            pe.wait_ge(sem("merged_ready"), n.next("merged_ready"))
            ch = rows_out(TILE["wo2"], ch, KD, lambda k, t: mTt[:, k, P * t:P * t + P], True)
            pe.wait_ge(sem("xn_ready"), n.next("xn_ready"))
            norm_turns(TILE["m2"], xn)
            for i in range(4):
                pe.wait_ge(psum_free(TILE["m2"] + i), fills(TILE["m2"] + i))
            pe.wait_ge(sem("bc2_loaded"), 16 * 11)
            b = claim(TILE["rt"])
            for t in range(NT):
                for k in range(KD):
                    ins = mm(b[:, 64 * t:64 * t + NG + NE], xT[:, k, NM + P * t:NM + P * t + P], wrt[:, k, :], start=(k == 0), stop=(k == KD - 1))
            ins.then_inc(psum_full(TILE["rt"]), 1)
            assert ch == E0, (ch, E0)
            for i in range(NPS):
                pe.wait_ge(psum_free(N_TILES - NPS + i), fills(N_TILES - NPS + i))

            slot_base = list(filled)

            def expert(e, j, first):
                s = [(E0 + 3 * j + c3) % NB for c3 in range(3)]

                def arrived(c3):
                    q = 3 * j + c3
                    turn = sum(1 for r in range(q + 1) if (E0 + r) % NB == s[c3])
                    base = slot_base[s[c3]] + 16 * turn
                    step = e if isinstance(e, int) else e
                    pe.wait_ge(sem(f"chunk_full{s[c3]}"), base if isinstance(e, int) else step * (16 * 3) + base)

                arrived(0)
                arrived(1)
                for m in range(KE):
                    b = psum[m]
                    if not (isinstance(e, int) and j == 0):
                        pe.wait_ge(sem("hidden_ready"), KE * j + m + 1 - KE if isinstance(e, int) else e * (KE * LE) + (KE * j + m + 1 - KE))
                    for q in range(2):
                        w = ring[:, s[q], :].rearrange("p (k n) -> p k n", k=KD)
                        for k in range(KD):
                            ins = mm(b[:, 256 * q:256 * q + 256], w[:, k, P * m:P * m + P], xT[:, k, NM:NTOK], start=(k == 0), stop=(k == KD - 1))
                    ins.then_inc(sem("gate_up_done"), 1)
                arrived(2)
                pe.wait_ge(sem("hidden_ready"), KE * (j + 1) if isinstance(e, int) else e * (KE * LE) + KE * (j + 1))
                if not (isinstance(e, int) and j == 0):
                    pe.wait_ge(sem("experts_added"), 4 * j if isinstance(e, int) else e * (4 * LE) + 4 * j)
                w = ring[:, s[2], :].rearrange("p (k n) -> p k n", k=KE)
                for i in range(4):
                    t, half = divmod(i, 2)
                    for k in range(KE):
                        ins = mm(psum[4 + i][:, :], hidE[:, j % 2, k, P * t:P * t + P], w[:, k, 512 * half:512 * half + 512], start=(k == 0), stop=(k == KE - 1))
                    ins.then_inc(sem("down_done"), 1)

            for j in range(LE):
                expert(0, j, j == 0)
            with pe.Fori(1, NE // LE) as i:
                for j in range(LE):
                    expert(i, j, False)

        @block.scalar
        def _(act):
            n = Counts()

            def copy(dst, tile, src, func=ACT.Copy, **kw):
                act.wait_ge(psum_full(tile), fills(tile))
                act.activation(dst, src, func, **kw).then_inc(psum_free(tile), 1)

            for i, (dst, r) in enumerate(((cp1, DEPTH * ROWS1), (cp2, 80))):
                copy(dst[:, :], i, psum[i][:, 0:r])
            act.wait_ge(sem("angle_ready"), n.next("angle_ready"))
            act.activation(sin[:, :, :], ang[:, :, :], ACT.Sin).then_inc(sem("sin_done"), 1)
            act.activation(cos[:, :, :], ang[:, :, :], ACT.Sin, scale=0.5).then_inc(sem("sin_done"), 1)

            for layer in range(DEPTH):
                T = lambda name: TILE[name, layer]

                def tokens(name, col):
                    for t in range(NT):
                        copy(tm[:, t, col:col + 512], T(name) + t, psum[(T(name) + t) % NPS][:, :])
                if layer:
                    act.wait_ge(sem("arena_free"), n.next("arena_free"))
                tokens("q", 0)
                tokens("k", 512)
                copy(lrT[0:GLA_RANK, :], T("lr"), psum[T("lr") % NPS][0:GLA_RANK, 0:SEQ])
                copy(s8[:, 0:2, 0:8], T("dt"), psum[T("dt") % NPS][:, 0:16].rearrange("p (t e) -> p t e", t=2))
                for i in range(4):
                    b = psum[(T("xbc") + i) % NPS]
                    copy(xbc[:, 2 * i:2 * i + 2, CONV - 1:], T("xbc") + i, b[:, :].rearrange("p (m t) -> p m t", m=2))
                for i in range(2):
                    b = psum[(T("gqk") + i) % NPS]
                    copy(gqk[:, 2 * i:2 * i + 2, :], T("gqk") + i, b[:, :].rearrange("p (m t) -> p m t", m=2))
                tokens("v", 1024)
                tokens("z", 1536)
                tokens("gv", 2048)
                tokens("gg", 2560)
                act.wait_ge(sem("lam_dots"), n.next("lam_dots"))
                act.activation(s8[:, 4, 0:2], s8[:, 5, 0:2], ACT.Exp).then_inc(sem("lam_exp"), 1)
                for t in range(NT):
                    act.wait_ge(sem("scores_ready"), n.next("scores_ready"))
                    v = sc[:, :, 0:P * (t + 1)]
                    act.activation(v, v, ACT.Exp).then_inc(sem("exp_done"), 1)
                act.wait_ge(sem("conv_sum"), n.next("conv_sum"))
                act.activation(cx[:, :, :], cx[:, :, :], ACT.Silu).then_inc(sem("conv_ready"), 1)
                act.wait_ge(sem("dt_ready"), n.next("dt_ready"))
                act.activation(s8[:, 6:8, 0:8], s8[:, 0:2, 0:8], ACT.Abs).then_inc(sem("act_step"), 1)
                act.wait_ge(sem("act_step"), n.next("act_step"))
                act.activation(s8[:, 6:8, 0:8], s8[:, 6:8, 0:8], ACT.Exp, scale=-1.0).then_inc(sem("act_step"), 1)
                act.wait_ge(sem("act_step"), n.next("act_step"))
                act.activation(s8[:, 6:8, 0:8], s8[:, 6:8, 0:8], ACT.Ln, bias=1.0).then_inc(sem("softplus_ln"), 1)
                act.activation(s8[:, 8, 0:8], bc1v(layer, "alog"), ACT.Exp).then_inc(sem("softplus_ln"), 1)
                act.wait_ge(sem("cum_ready"), n.next("cum_ready"))
                act.activation(s8[:, 13:15, 0:16], s8[:, 11:13, 0:16], ACT.Exp).then_inc(sem("cum_exp"), 1)
                for t in range(NT):
                    act.wait_ge(sem("seg_ready"), n.next("seg_ready"))
                    act.activation(decay[:, t], decay[:, t], ACT.Exp).then_inc(sem("decay_exp"), 1)
                copy(sst.rearrange("p a b -> p (a b)"), T("st"), psum[T("st") % NPS][:, :])
                act.wait_ge(sem("z_asked"), n.next("z_asked"))
                act.activation(tm[:, :, 1536:2048], tm[:, :, 1536:2048], ACT.Silu)
                act.activation(tm[:, :, 2560:3072], tm[:, :, 2560:3072], ACT.Silu).then_inc(sem("z_silu"), 1)
                act.wait_ge(sem("gate_ready"), n.next("gate_ready"))
                act.activation(gtmp, gcum, ACT.Abs).then_inc(sem("act_step"), 1)
                act.wait_ge(sem("act_step"), n.next("act_step"))
                act.activation(gtmp, gtmp, ACT.Exp, scale=-1.0).then_inc(sem("act_step"), 1)
                act.wait_ge(sem("act_step"), n.next("act_step"))
                act.activation(gtmp, gtmp, ACT.Ln, bias=1.0).then_inc(sem("gate_ln"), 1)
                act.wait_ge(sem("gcum_ready"), n.next("gcum_ready"))
                act.activation(eb, gcum, ACT.Exp)
                act.activation(enb, gcum, ACT.Exp, scale=-1.0)
                act.activation(ke, gtmp, ACT.Exp).then_inc(sem("gla_exp"), 1)
                for t in range(NT):
                    for q in range(3):
                        tile = T("mixT") + 3 * t + q
                        copy(xT[:, 4 * q:4 * q + 4, NM + P * t:NM + P * t + P], tile,
                             psum[tile % NPS][:, :].rearrange("p (j t) -> p j t", j=4))
                for f in range(KF):
                    tile = T("ffn") + f
                    act.wait_ge(psum_full(tile), fills(tile))
                    if f >= 2:
                        act.wait_ge(psum_free(tile - 2), fills(tile - 2))
                    act.activation(sil[:, f % 2, :], psum[tile % NPS][:, 0:SEQ], ACT.Silu).then_inc(sem("silu_done"), 1)
                for t in range(NT):
                    for half in range(2):
                        tile = T("n3") + 2 * t + half
                        copy(xT[:, 4 * half:4 * half + 4, NM + P * t:NM + P * t + P], tile,
                             psum[tile % NPS][:, :].rearrange("p (j t) -> p j t", j=4))
                copy(pT.rearrange("p a b -> p (a b)"), T("pT"), psum[T("pT") % NPS][:, :])
                for i in range(4):
                    copy(sg[:, i // 2, 512 * (i % 2):512 * (i % 2) + 512], T("pg") + i, psum[(T("pg") + i) % NPS][:, :], ACT.Sigmoid)

            act.wait_ge(sem("layer_done"), n.next("layer_done"))
            act.wait_ge(sem("layer_done"), n.next("layer_done"))
            for m in range(4):
                copy(fT[:, m, :], TILE["hf"] + m, psum[(TILE["hf"] + m) % NPS][:, 0:NTOK])
            for i in range(2):
                copy(qT[:, 2 * i:2 * i + 2, :], TILE["hq"] + i, psum[(TILE["hq"] + i) % NPS][:, :].rearrange("p (m t) -> p m t", m=2))
            for t in range(NT):
                copy(vt[:, t, :], TILE["hi"] + t, psum[(TILE["hi"] + t) % NPS][:, :])
            copy(vt[0:NM, 2, :], TILE["hi"] + 2, psum[(TILE["hi"] + 2) % NPS][0:NM, :])
            for t in range(NT):
                copy(og[:, t, :], TILE["hog"] + t, psum[(TILE["hog"] + t) % NPS][:, :], ACT.Sigmoid)
            for m in range(KD):
                copy(lx[:, m, CONV - 1:], TILE["lx"] + m, psum[(TILE["lx"] + m) % NPS][:, 0:NTOK])
            for name, dst, func in (("ly", ly, ACT.Copy), ("ga", ga, ACT.Sigmoid), ("gb", gb, ACT.Sigmoid)):
                for i in range(4):
                    copy(dst[:, 2 * i:2 * i + 2, :], TILE[name] + i,
                         psum[(TILE[name] + i) % NPS][:, :].rearrange("p (m t) -> p m t", m=2), func)
            act.activation(kT, fT, ACT.Sigmoid, scale=-1.0).then_inc(sem("act_step"), 1)
            act.wait_ge(sem("act_step"), n.next("act_step"))
            act.activation(fT, fT, ACT.Sigmoid).then_inc(sem("f_sig"), 1)
            act.wait_ge(sem("lbd_ready"), n.next("lbd_ready"))
            act.activation(s8[:, 17, 0:4], s8[:, 16, 0:4], ACT.Sigmoid).then_inc(sem("lb_sig"), 1)
            act.wait_ge(sem("f_ready"), n.next("f_ready"))
            act.activation(fT, fT, ACT.Ln).then_inc(sem("f_ln"), 1)
            act.wait_ge(sem("gend_ready"), n.next("gend_ready"))
            act.activation(fT[:, :, 0:NM], fT[:, :, 0:NM], ACT.Exp)
            act.activation(klev[:, :, 0:P], klev[:, :, 0:P], ACT.Exp).then_inc(sem("gend_exp"), 1)
            copy(wlev[0:NM, :, 0:P], TILE["hkm"], psum[TILE["hkm"] % NPS][0:NM, :].rearrange("p (h d) -> p h d", h=4))
            copy(ke0, TILE["hk0"], psum[TILE["hk0"] % NPS][:, :].rearrange("p (h d) -> p h d", h=4))
            for i in range(len(LEVELS)):
                act.wait_ge(sem("diff_ready"), n.next("diff_ready"))
                act.activation(wlev, wlev, ACT.Abs).then_inc(sem("act_step"), 1)
                act.wait_ge(sem("act_step"), n.next("act_step"))
                act.activation(wlev, wlev, ACT.Exp, scale=-1.0).then_inc(sem("w_ready"), 1)
            act.wait_ge(sem("qexp_asked"), n.next("qexp_asked"))
            act.activation(wlev, G, ACT.Exp).then_inc(sem("qexp_done"), 1)
            act.wait_ge(sem("xc_ready"), n.next("xc_ready"))
            for name, dst, o in (("lr_r", ra, CP2["br"]), ("lr_i", iu, CP2["bi"])):
                for m in range(LB):
                    copy(dst[:, m, :], TILE[name] + m, psum[(TILE[name] + m) % NPS][:, 0:NTOK], ACT.Sigmoid, bias=cp2[:, o + m:o + m + 1])
            act.wait_ge(sem("lam_ready"), n.next("lam_ready"))
            act.activation(s8[:, 20, 0:8], cp2[:, 72:80], ACT.Abs).then_inc(sem("act_step"), 1)
            act.wait_ge(sem("act_step"), n.next("act_step"))
            act.activation(s8[:, 20, 0:8], s8[:, 20, 0:8], ACT.Exp, scale=-1.0).then_inc(sem("act_step"), 1)
            act.wait_ge(sem("act_step"), n.next("act_step"))
            act.activation(s8[:, 20, 0:8], s8[:, 20, 0:8], ACT.Ln, bias=1.0).then_inc(sem("lam_ln"), 1)
            act.wait_ge(sem("loga_ready"), n.next("loga_ready"))
            act.activation(th, ra, ACT.Tanh, scale=-1.0).then_inc(sem("act_step"), 1)
            act.wait_ge(sem("act_step"), n.next("act_step"))
            act.activation(ra, ra, ACT.Exp).then_inc(sem("a_ready"), 1)
            act.wait_ge(sem("gelu_asked"), n.next("gelu_asked"))
            act.activation(iu[:, :, NM:], iu[:, :, NM:], ACT.Tanh, scale=math.sqrt(2 / math.pi)).then_inc(sem("gelu_tanh"), 1)
            act.wait_ge(sem("sq_ready"), n.next("sq_ready"))
            act.activation(th, th, ACT.Sqrt).then_inc(sem("sq_done"), 1)
            act.wait_ge(sem("route_exp_asked"), n.next("route_exp_asked"))
            act.activation(s8[:, 2:4, 0:NG], s8[:, 2:4, 0:NG], ACT.Exp)
            act.activation(s8[:, 4, 0:2], s8[:, 4, 0:2], ACT.Exp).then_inc(sem("route_exp"), 1)

            def expert(i, j):
                for m in range(KE):
                    at = KE * j + m + 1
                    first = isinstance(i, int)
                    act.wait_ge(sem("gate_up_done"), at if first else i * (KE * LE) + at)
                    if not (first and at <= 2):
                        act.wait_ge(sem("hidden_ready"), at - 2 if first else i * (KE * LE) + (at - 2))
                    act.activation(silE[:, m % 2, :], psum[m][:, 0:SEQ], ACT.Silu).then_inc(sem("expert_silu"), 1)
            for j in range(LE):
                expert(0, j)
            with act.Fori(1, NE // LE) as i:
                for j in range(LE):
                    expert(i, j)

        @block.vector
        def _(v):
            n = Counts()
            TT, TS, STT = nc.vector.tensor_tensor, nc.vector.tensor_scalar, nc.vector.scalar_tensor_tensor

            def bank(tile):
                return psum[tile % NPS]

            def rsqrt(cols, width):
                TS(st1[:, 0:cols], st1[:, 0:cols], 1.0 / width, EPS, ALU.mult, ALU.add).then_inc(sem("power_asked"), 1)
                v.wait_ge(sem("power_done"), n.next("power_done"))

            def norm_rows(layer_gain=None, gain_row=None, meta=False):
                for t in range(NT):
                    nc.vector.tensor_tensor_reduce(out=xn[:, t, :], in0=h[:, t, :], in1=h[:, t, :], scale=1.0, scalar=0.0,
                                                        op0=ALU.mult, op1=ALU.add, accum_out=st1[:, t:t + 1]).then_inc(sem("dve_step"), 1)
                    v.wait_ge(sem("dve_step"), n.next("dve_step"))
                if meta:
                    v.memset(st1[:, 2:3], 1.0).then_inc(sem("dve_step"), 1)
                    v.wait_ge(sem("dve_step"), n.next("dve_step"))
                    nc.vector.tensor_tensor_reduce(out=mflat[0:NM, 0:D], in0=hmeta[0:NM, :], in1=hmeta[0:NM, :], scale=1.0, scalar=0.0,
                                                        op0=ALU.mult, op1=ALU.add, accum_out=st1[0:NM, 2:3]).then_inc(sem("dve_step"), 1)
                    v.wait_ge(sem("dve_step"), n.next("dve_step"))
                rsqrt(3 if meta else 2, D)
                if meta:
                    TS(hmeta[0:NM, :], hmeta[0:NM, :], st2[0:NM, 2:3], None, ALU.mult).then_inc(sem("dve_step"), 1)
                    v.wait_ge(sem("dve_step"), n.next("dve_step"))
                for t in range(NT):
                    ins = TS(xn[:, t, :], h[:, t, :], st2[:, t:t + 1], None, ALU.mult)
                    if gain_row is not None:
                        ins.then_inc(sem("dve_step"), 1)
                        v.wait_ge(sem("dve_step"), n.next("dve_step"))
                        ins = TT(xn[:, t, :], xn[:, t, :], gain_row, ALU.mult)
                    if t == NT - 1:
                        ins.then_inc(sem("xn_ready"), 1)
                    else:
                        ins.then_inc(sem("dve_step"), 1)
                        v.wait_ge(sem("dve_step"), n.next("dve_step"))

            def norm_evac(tile, gain):
                for t in range(NT):
                    for half in range(2):
                        k = tile + 2 * t + half
                        v.wait_ge(psum_full(k), fills(k))
                        src = bank(k)[:, :].rearrange("p (j t) -> p j t", j=4)
                        dst = xT[:, 4 * half:4 * half + 4, NM + P * t:NM + P * t + P]
                        if gain is None:
                            nc.vector.tensor_copy(dst, src).then_inc(psum_free(k), 1)
                        else:
                            TT(dst, src, gain[:, 4 * half:4 * half + 4].unsqueeze(2).to_broadcast([P, 4, P]), ALU.mult).then_inc(psum_free(k), 1)

            def add_rows(tile):
                for i in range(4):
                    k = tile + i
                    dst = h[:, i // 2, 512 * (i % 2):512 * (i % 2) + 512]
                    v.wait_ge(psum_full(k), fills(k))
                    TT(dst, dst, bank(k)[:, :], ALU.add).then_inc(psum_free(k), 1)
                    v.wait_ge(psum_free(k), fills(k))

            v.wait_ge(sem("iotas"), n.next("iotas", 2))
            TT(xi[:, :], xi[:, :], xs_[:, :], ALU.bitwise_xor).then_inc(sem("dve_step"), 1)
            v.wait_ge(sem("dve_step"), n.next("dve_step"))
            nc.vector.tensor_copy(xf[:, :], xi[:, :]).then_inc(sem("dve_step"), 1)
            v.wait_ge(sem("dve_step"), n.next("dve_step"))
            v.wait_ge(sem("masks"), 4)
            TT(xf[:, :], xf[:, :], tri[:, :], ALU.mult).then_inc(sem("dve_step"), 1)
            v.wait_ge(sem("dve_step"), n.next("dve_step"))
            for i, b in enumerate(LEVELS):
                TS(lev[:, i, :], xf[:, :], float(b), None, ALU.is_ge).then_inc(sem("dve_step"), 1)
                v.wait_ge(sem("dve_step"), n.next("dve_step"))
                STT(lev[:, i, :], xf[:, :], float(2 * b), lev[:, i, :], ALU.is_lt, ALU.mult).then_inc(sem("dve_step"), 1)
                v.wait_ge(sem("dve_step"), n.next("dve_step"))
            nc.vector.tensor_copy(lev[:, 7, :], ident[:, :]).then_inc(sem("dve_step"), 1)
            v.wait_ge(sem("dve_step"), n.next("dve_step"))
            v.wait_ge(sem("bc_loaded"), 16 * 27)
            v.wait_ge(sem("consts"), 1)
            nc.vector.tensor_copy(posf[:, :], pos[:, :]).then_inc(sem("dve_step"), 1)
            v.wait_ge(sem("dve_step"), n.next("dve_step"))
            TT(ang[:, :, :], posf[:, :].unsqueeze(2).to_broadcast([P, NT, 8]), frq[:, :].unsqueeze(1).to_broadcast([P, NT, 8]), ALU.mult).then_inc(sem("dve_step"), 1)
            v.wait_ge(sem("dve_step"), n.next("dve_step"))
            TS(angk[:, :, :], ang[:, :, :], 1.0 / (2 * math.pi), None, ALU.mult).then_inc(sem("dve_step"), 1)
            v.wait_ge(sem("dve_step"), n.next("dve_step"))
            TS(angk[:, :, :], angk[:, :, :], 12582912.0, None, ALU.add).then_inc(sem("dve_step"), 1)
            v.wait_ge(sem("dve_step"), n.next("dve_step"))
            TS(angk[:, :, :], angk[:, :, :], 12582912.0, None, ALU.subtract).then_inc(sem("dve_step"), 1)
            v.wait_ge(sem("dve_step"), n.next("dve_step"))
            for part in (6.28125, 0.0019350051879882812, 3.0199158e-07):
                STT(ang[:, :, :], angk[:, :, :], -part, ang[:, :, :], ALU.mult, ALU.add).then_inc(sem("dve_step"), 1)
                v.wait_ge(sem("dve_step"), n.next("dve_step"))
            TS(ang[:, :, :], ang[:, :, :], 3.1415925, -3.1415925, ALU.min, ALU.max).then_inc(sem("angle_ready"), 1)
            v.wait_ge(sem("sin_done"), n.next("sin_done", 2))
            TT(cos[:, :, :], cos[:, :, :], cos[:, :, :], ALU.mult).then_inc(sem("dve_step"), 1)
            v.wait_ge(sem("dve_step"), n.next("dve_step"))
            TS(cos[:, :, :], cos[:, :, :], -2.0, 1.0, ALU.mult, ALU.add).then_inc(sem("dve_step"), 1)
            v.wait_ge(sem("dve_step"), n.next("dve_step"))
            v.wait_ge(sem("x_loaded"), 16)
            v.wait_ge(psum_free(0), fills(0))
            v.wait_ge(psum_free(1), fills(1))

            for layer in range(DEPTH):
                T = lambda name: TILE[name, layer]
                cpl = cp1[:, ROWS1 * layer:ROWS1 * layer + ROWS1]
                norm_rows()
                norm_evac(T("n1"), cpl[:, 0:8])
                for i in range(2):
                    v.wait_ge(psum_free(T("q") + i), fills(T("q") + i))
                    v.wait_ge(psum_free(T("k") + i), fills(T("k") + i))
                qk = [tm[:, t, 0:1024].rearrange("p (h d) -> p h d", d=DQK) for t in range(NT)]
                for t in range(NT):
                    TT(xn[:, t, :], tm[:, t, 0:1024], tm[:, t, 0:1024], ALU.mult).then_inc(sem("dve_step"), 1)
                    v.wait_ge(sem("dve_step"), n.next("dve_step"))
                    nc.vector.reduce_sum(st1[:, 16 * t:16 * t + 16], xn[:, t, :].rearrange("p (h d) -> p h d", d=DQK), axis=AX.X).then_inc(sem("dve_step"), 1)
                    v.wait_ge(sem("dve_step"), n.next("dve_step"))
                rsqrt(32, DQK)
                for t in range(NT):
                    TT(qk[t], qk[t], st2[:, 16 * t:16 * t + 16].unsqueeze(2).to_broadcast([P, 16, DQK]), ALU.mult).then_inc(sem("dve_step"), 1)
                    v.wait_ge(sem("dve_step"), n.next("dve_step"))
                    for i, name in enumerate(("gq", "gk")):
                        TT(qk[t][:, 8 * i:8 * i + 8, :], qk[t][:, 8 * i:8 * i + 8, :],
                                bc1v(layer, name).unsqueeze(1).to_broadcast([P, 8, DQK]), ALU.mult).then_inc(sem("dve_step"), 1)
                        v.wait_ge(sem("dve_step"), n.next("dve_step"))
                    x1, x2 = qk[t][:, :, 0:8], qk[t][:, :, 8:16]
                    c_ = cos[:, t, :].unsqueeze(1).to_broadcast([P, 16, 8])
                    s_ = sin[:, t, :].unsqueeze(1).to_broadcast([P, 16, 8])
                    r = [xn[:, t, 128 * i:128 * i + 128].rearrange("p (h d) -> p h d", d=8) for i in range(4)]
                    TT(r[0], x1, c_, ALU.mult).then_inc(sem("dve_step"), 1)
                    v.wait_ge(sem("dve_step"), n.next("dve_step"))
                    TT(r[1], x2, s_, ALU.mult).then_inc(sem("dve_step"), 1)
                    v.wait_ge(sem("dve_step"), n.next("dve_step"))
                    TT(r[2], x2, c_, ALU.mult).then_inc(sem("dve_step"), 1)
                    v.wait_ge(sem("dve_step"), n.next("dve_step"))
                    TT(r[3], x1, s_, ALU.mult).then_inc(sem("dve_step"), 1)
                    v.wait_ge(sem("dve_step"), n.next("dve_step"))
                    TT(x1, r[0], r[1], ALU.subtract).then_inc(sem("dve_step"), 1)
                    v.wait_ge(sem("dve_step"), n.next("dve_step"))
                    ins = TT(x2, r[2], r[3], ALU.add)
                    if t:
                        ins.then_inc(sem("qk_ready"), 1)
                        v.wait_ge(sem("qk_ready"), n.next("qk_ready"))
                    else:
                        ins.then_inc(sem("dve_step"), 1)
                        v.wait_ge(sem("dve_step"), n.next("dve_step"))
                for t in range(NT):
                    for j in range(2):
                        k = T("qkT") + 2 * t + j
                        v.wait_ge(psum_full(k), fills(k))
                        nc.vector.tensor_copy(qkT[:, j, :, P * t:P * t + P], bank(k)[:, :].rearrange("p (h t) -> p h t", h=4)).then_inc(psum_free(k), 1)
                for i in range(2):
                    nc.vector.tensor_tensor_reduce(out=s8[:, 9:11, :].rearrange("p a b -> p (a b)"), in0=bc1v(layer, f"lq{i + 1}"),
                                                        in1=bc1v(layer, f"lk{i + 1}"), scale=1.0, scalar=0.0, op0=ALU.mult,
                                                        op1=ALU.add, accum_out=s8[:, 5, i:i + 1]).then_inc(sem("dve_step"), 1)
                    v.wait_ge(sem("dve_step"), n.next("dve_step"))
                v.sem_inc(sem("lam_dots"), 1)
                v.wait_ge(sem("lam_exp"), n.next("lam_exp"))
                lam = s8[:, 4, 2:3]
                TT(lam, s8[:, 4, 0:1], s8[:, 4, 1:2], ALU.subtract).then_inc(sem("dve_step"), 1)
                v.wait_ge(sem("dve_step"), n.next("dve_step"))
                TS(lam, lam, lambda_init(layer), None, ALU.add).then_inc(sem("dve_step"), 1)
                v.wait_ge(sem("dve_step"), n.next("dve_step"))
                for t in range(NT):
                    nk = P * (t + 1)
                    for i in range(4):
                        k = T("sc") + 4 * t + i
                        v.wait_ge(psum_full(k), fills(k))
                        src = bank(k)[:, :].rearrange("p (j t) -> p j t", j=2)
                        dst = sc[:, 2 * i:2 * i + 2, :]
                        if t:
                            TS(dst[:, :, 0:P], src[:, :, 0:P], DQK ** -0.5, None, ALU.mult).then_inc(sem("dve_step"), 1)
                            v.wait_ge(sem("dve_step"), n.next("dve_step"))
                        o = P * t
                        STT(dst[:, :, o:o + P], src[:, :, o:o + P], DQK ** -0.5,
                                    neg[:, :].unsqueeze(1).to_broadcast([P, 2, P]), ALU.mult, ALU.add).then_inc(psum_free(k), 1)
                        v.wait_ge(psum_free(k), fills(k))
                    s_ = sc[:, :, 0:nk]
                    nc.vector.reduce_max(s8[:, 9, 0:8], s_, axis=AX.X).then_inc(sem("dve_step"), 1)
                    v.wait_ge(sem("dve_step"), n.next("dve_step"))
                    TT(s_, s_, s8[:, 9, 0:8].unsqueeze(2).to_broadcast([P, 8, nk]), ALU.subtract).then_inc(sem("scores_ready"), 1)
                    v.wait_ge(sem("exp_done"), n.next("exp_done"))
                    nc.vector.reduce_sum(s8[:, 10, 0:8], s_, axis=AX.X).then_inc(sem("dve_step"), 1)
                    v.wait_ge(sem("dve_step"), n.next("dve_step"))
                    nc.vector.reciprocal(s8[:, 10, 0:8], s8[:, 10, 0:8]).then_inc(sem("dve_step"), 1)
                    v.wait_ge(sem("dve_step"), n.next("dve_step"))
                    TS(s8[:, 10, 4:8], s8[:, 10, 4:8], lam, None, ALU.mult).then_inc(sem("dve_step"), 1)
                    v.wait_ge(sem("dve_step"), n.next("dve_step"))
                    TT(s_, s_, s8[:, 10, 0:8].unsqueeze(2).to_broadcast([P, 8, nk]), ALU.mult).then_inc(sem("dve_step"), 1)
                    v.wait_ge(sem("dve_step"), n.next("dve_step"))
                    TT(attn[:, :, 0:nk], s_[:, 0:4, :], s_[:, 4:8, :], ALU.subtract).then_inc(sem("attn_ready"), 1)
                    v.wait_ge(sem("attn_ready"), n.next("attn_ready"))
                    for kt in range(t + 1):
                        k = T("at") + t + kt
                        v.wait_ge(psum_full(k), fills(k))
                        nc.vector.tensor_copy(attnT[:, :, kt, :], bank(k)[:, :].rearrange("p (h q) -> p h q", h=4)).then_inc(psum_free(k), 1)
                    k = T("pv") + t
                    v.wait_ge(psum_full(k), fills(k))
                    nc.vector.tensor_copy(mix[:, t, 0:512], bank(k)[:, :]).then_inc(psum_free(k), 1)
                    v.wait_ge(psum_free(k), fills(k))

                def head_norm(dst_t, heads, width, gain, factor):
                    per = heads // NT
                    for t in range(NT):
                        dd = dst_t(t)
                        sq = xn[:, t, 0:per * width]
                        TT(sq, dd, dd, ALU.mult).then_inc(sem("dve_step"), 1)
                        v.wait_ge(sem("dve_step"), n.next("dve_step"))
                        nc.vector.reduce_sum(st1[:, per * t:per * t + per], sq.rearrange("p (h d) -> p h d", d=width), axis=AX.X).then_inc(sem("dve_step"), 1)
                        v.wait_ge(sem("dve_step"), n.next("dve_step"))
                    rsqrt(heads, width)
                    for t in range(NT):
                        dd = dst_t(t).rearrange("p (h d) -> p h d", d=width)
                        TT(dd, dd, st2[:, per * t:per * t + per].unsqueeze(2).to_broadcast([P, per, width]), ALU.mult).then_inc(sem("dve_step"), 1)
                        v.wait_ge(sem("dve_step"), n.next("dve_step"))
                        STT(dd, dd, factor, gain, ALU.mult, ALU.mult).then_inc(sem("dve_step"), 1)
                        v.wait_ge(sem("dve_step"), n.next("dve_step"))

                head_norm(lambda t: mix[:, t, 0:512], 8, DV, bc1v(layer, "gsub").unsqueeze(1).to_broadcast([P, 4, DV]), 1.0 - lambda_init(layer))
                for i in range(4):
                    v.wait_ge(psum_free(T("xbc") + i), fills(T("xbc") + i))
                v.wait_ge(sem("zeros"), n.next("zeros"))
                for m in range(KD):
                    TS(cx[:, m, :], xbc[:, m, 0:SEQ], cpl[:, 16 + m:17 + m], cpl[:, 48 + m:49 + m], ALU.mult, ALU.add).then_inc(sem("dve_step"), 1)
                    v.wait_ge(sem("dve_step"), n.next("dve_step"))
                    for j in range(1, CONV):
                        STT(cx[:, m, :], xbc[:, m, j:j + SEQ], cpl[:, 16 + 8 * j + m:17 + 8 * j + m], cx[:, m, :], ALU.mult, ALU.add).then_inc(sem("dve_step"), 1)
                        v.wait_ge(sem("dve_step"), n.next("dve_step"))
                v.sem_inc(sem("conv_sum"), 1)
                v.wait_ge(psum_free(T("dt")), fills(T("dt")))
                dtr = s8[:, 0:2, 0:8]
                dtb = bc1v(layer, "dtb").unsqueeze(1).to_broadcast([P, NT, 8])
                TT(dtr, dtr, dtb, ALU.add).then_inc(sem("dt_ready"), 1)
                v.wait_ge(sem("dt_ready"), n.next("dt_ready"))
                v.wait_ge(sem("softplus_ln"), n.next("softplus_ln", 2))
                TS(dtr, dtr, 0.0, None, ALU.max).then_inc(sem("dve_step"), 1)
                v.wait_ge(sem("dve_step"), n.next("dve_step"))
                TT(dtr, dtr, s8[:, 6:8, 0:8], ALU.add).then_inc(sem("dve_step"), 1)
                v.wait_ge(sem("dve_step"), n.next("dve_step"))
                dA = s8[:, 2:4, 0:8]
                STT(dA, dtr, -1.0, s8[:, 8, 0:8].unsqueeze(1).to_broadcast([P, NT, 8]), ALU.mult, ALU.mult).then_inc(sem("dve_step"), 1)
                v.wait_ge(sem("dve_step"), n.next("dve_step"))
                v.sem_inc(sem("da_ready"), 1)
                for i in range(3):
                    k = T("xbT") + i
                    v.wait_ge(psum_full(k), fills(k))
                    if i < 2:
                        nc.vector.tensor_copy(xh[:, i, :], bank(k)[:, :]).then_inc(psum_free(k), 1)
                        v.wait_ge(psum_free(k), fills(k))
                    else:
                        nc.vector.tensor_copy(B0.rearrange("p a b -> p (a b)"), bank(k)[:, 0:256]).then_inc(psum_free(k), 1)
                        v.wait_ge(psum_free(k), fills(k))
                k = T("cumc")
                v.wait_ge(psum_full(k), fills(k))
                nc.vector.tensor_copy(s8[:, 11:13, 0:8], bank(k)[:, 0:32].rearrange("p (t e) -> p t e", t=2)[:, :, 0:8]).then_inc(sem("dve_step"), 1)
                v.wait_ge(sem("dve_step"), n.next("dve_step"))
                TT(s8[:, 11:13, 8:16], bank(k)[:, 0:32].rearrange("p (t e) -> p t e", t=2)[:, :, 8:16], s8[:, 11:13, 0:8], ALU.subtract).then_inc(psum_free(k), 1)
                v.wait_ge(psum_free(k), fills(k))
                v.sem_inc(sem("cum_ready"), 1)
                for t in range(NT):
                    for q in range(2):
                        k = T("cumb") + 2 * t + q
                        v.wait_ge(psum_full(k), fills(k))
                        for j in range(4):
                            hh = 4 * q + j
                            ins = TS(decay[:, t, hh, :], bank(k)[:, P * j:P * j + P], s8[:, 11 + t, hh:hh + 1], 0.0, ALU.subtract, ALU.min)
                            if j < 3:
                                ins.then_inc(sem("dve_step"), 1)
                                v.wait_ge(sem("dve_step"), n.next("dve_step"))
                        ins.then_inc(psum_free(k), 1)
                        v.wait_ge(psum_free(k), fills(k))
                    v.sem_inc(sem("seg_ready"), 1)
                k = T("cb")
                v.wait_ge(psum_full(k), fills(k))
                TT(cbm, bank(k)[:, :].rearrange("p (a b) -> p a b", a=4), tri[:, :].unsqueeze(1).to_broadcast([P, 4, P]), ALU.mult).then_inc(psum_free(k), 1)
                v.wait_ge(psum_free(k), fills(k))
                v.wait_ge(sem("cum_exp"), n.next("cum_exp"))
                for t in range(NT):
                    x3 = xh[:, t, :].rearrange("p (h d) -> p h d", d=SSD_P)
                    TT(xdt[:, t, :].rearrange("p (h d) -> p h d", d=SSD_P), x3, s8[:, t, 0:8].unsqueeze(2).to_broadcast([P, 8, SSD_P]), ALU.mult).then_inc(sem("dve_step"), 1)
                    v.wait_ge(sem("dve_step"), n.next("dve_step"))
                TT(xdte.rearrange("p a (b d) -> p (a b) d", d=SSD_P), xdt[:, 0, :].rearrange("p (h d) -> p h d", d=SSD_P),
                        s8[:, 13, 8:16].unsqueeze(2).to_broadcast([P, 8, SSD_P]), ALU.mult).then_inc(sem("dve_step"), 1)
                v.wait_ge(sem("dve_step"), n.next("dve_step"))
                v.wait_ge(sem("decay_exp"), n.next("decay_exp", 2))
                for t in range(NT):
                    for gg in range(2):
                        dd = decay[:, t, 4 * gg:4 * gg + 4, :]
                        TT(dd, dd, cbm[:, 2 * t + gg, :].unsqueeze(1).to_broadcast([P, 4, P]), ALU.mult).then_inc(sem("dve_step"), 1)
                        v.wait_ge(sem("dve_step"), n.next("dve_step"))
                v.sem_inc(sem("ssd_ready"), 1)
                v.sem_inc(sem("z_asked"), 1)
                for t in range(NT):
                    y = mix[:, t, 512:1024]
                    y3 = y.rearrange("p (h d) -> p h d", d=SSD_P)
                    x3 = xh[:, t, :].rearrange("p (h d) -> p h d", d=SSD_P)
                    TT(y3, x3, bc1v(layer, "dsk").unsqueeze(2).to_broadcast([P, 8, SSD_P]), ALU.mult).then_inc(sem("dve_step"), 1)
                    v.wait_ge(sem("dve_step"), n.next("dve_step"))
                    k = T("yd") + t
                    v.wait_ge(psum_full(k), fills(k))
                    TT(y, y, bank(k)[:, :], ALU.add).then_inc(psum_free(k), 1)
                    v.wait_ge(psum_free(k), fills(k))
                k = T("yo")
                v.wait_ge(psum_full(k), fills(k))
                TT(xdt[:, 1, :].rearrange("p (h d) -> p h d", d=SSD_P), bank(k)[:, :].rearrange("p (h d) -> p h d", d=SSD_P),
                           s8[:, 14, 0:8].unsqueeze(2).to_broadcast([P, 8, SSD_P]), ALU.mult).then_inc(psum_free(k), 1)
                v.wait_ge(psum_free(k), fills(k))
                TT(mix[:, 1, 512:1024], mix[:, 1, 512:1024], xdt[:, 1, :], ALU.add).then_inc(sem("dve_step"), 1)
                v.wait_ge(sem("dve_step"), n.next("dve_step"))
                v.wait_ge(sem("z_silu"), n.next("z_silu"))
                for t in range(NT):
                    TT(mix[:, t, 512:1024], mix[:, t, 512:1024], tm[:, t, 1536:2048], ALU.mult).then_inc(sem("dve_step"), 1)
                    v.wait_ge(sem("dve_step"), n.next("dve_step"))
                head_norm(lambda t: mix[:, t, 512:1024], 4, 256, bc1v(layer, "ssdn").rearrange("p (h d) -> p h d", d=256), 1.0)
                k = T("gk")
                v.wait_ge(psum_full(k), fills(k))
                TS(gcum[:, 0, :], bank(k)[:, 0:256], cpl[:, 56:57], None, ALU.add).then_inc(sem("dve_step"), 1)
                v.wait_ge(sem("dve_step"), n.next("dve_step"))
                TS(gcum[:, 1, :], bank(k)[:, 256:512], cpl[:, 57:58], None, ALU.add).then_inc(psum_free(k), 1)
                v.wait_ge(psum_free(k), fills(k))
                v.sem_inc(sem("gate_ready"), 1)
                v.wait_ge(sem("gate_ln"), n.next("gate_ln"))
                STT(gtmp, gcum, 0.0, gtmp, ALU.min, ALU.subtract).then_inc(sem("dve_step"), 1)
                v.wait_ge(sem("dve_step"), n.next("dve_step"))
                TS(gtmp, gtmp, 1.0 / 16.0, None, ALU.mult).then_inc(sem("dve_step"), 1)
                v.wait_ge(sem("dve_step"), n.next("dve_step"))
                one = ones[:, 0:GLA_C]
                for j in range(2):
                    for cc in range(4):
                        o = GLA_C * cc
                        nc.vector.tensor_tensor_scan(gcum[:, j, o:o + GLA_C], one, gtmp[:, j, o:o + GLA_C], 0.0, ALU.mult, ALU.add).then_inc(sem("dve_step"), 1)
                        v.wait_ge(sem("dve_step"), n.next("dve_step"))
                c3 = gcum.rearrange("p j (c t) -> p (j c) t", t=GLA_C)
                TT(gtmp.rearrange("p j (c t) -> p (j c) t", t=GLA_C), c3[:, :, GLA_C - 1:GLA_C].to_broadcast([P, 8, GLA_C]), c3, ALU.subtract).then_inc(sem("dve_step"), 1)
                v.wait_ge(sem("dve_step"), n.next("dve_step"))
                v.sem_inc(sem("gcum_ready"), 1)
                for i in range(2):
                    v.wait_ge(psum_free(T("gqk") + i), fills(T("gqk") + i))
                v.wait_ge(sem("gla_exp"), n.next("gla_exp"))
                STT(qd, gqk[:, 0:2, :], GLA_DK ** -0.5, eb, ALU.mult, ALU.mult).then_inc(sem("dve_step"), 1)
                v.wait_ge(sem("dve_step"), n.next("dve_step"))
                TT(ki, gqk[:, 2:4, :], enb, ALU.mult).then_inc(sem("dve_step"), 1)
                v.wait_ge(sem("dve_step"), n.next("dve_step"))
                TT(ke, gqk[:, 2:4, :], ke, ALU.mult).then_inc(sem("gla_ready"), 1)
                v.wait_ge(sem("gla_ready"), n.next("gla_ready"))
                k = T("keT")
                v.wait_ge(psum_full(k), fills(k))
                v.wait_ge(sem("states_zero"), n.next("states_zero"))
                bk = bank(k)[:, :].rearrange("p (t j) -> p t j", t=2)
                nc.vector.tensor_copy(kz[0:64, 0, :], bk[0:64, 0, :]).then_inc(sem("dve_step"), 1)
                v.wait_ge(sem("dve_step"), n.next("dve_step"))
                nc.vector.tensor_copy(kz[64:P, 1, :], bk[64:P, 0, :]).then_inc(sem("dve_step"), 1)
                v.wait_ge(sem("dve_step"), n.next("dve_step"))
                nc.vector.tensor_copy(kz[0:64, 2, :], bk[0:64, 1, :]).then_inc(psum_free(k), 1)
                v.wait_ge(psum_free(k), fills(k))
                for cc in range(3):
                    k = T("gst") + cc
                    v.wait_ge(psum_full(k), fills(k))
                    for j in range(2):
                        for par in range(2):
                            lo = 64 * par
                            ins = STT(Sh[lo:lo + 64, cc + 1, j, P * par:P * par + P], Sh[lo:lo + 64, cc, j, P * par:P * par + P],
                                      eb[lo:lo + 64, j, GLA_C * (cc + 1) - 1:GLA_C * (cc + 1)],
                                      bank(k)[lo:lo + 64, 256 * j + P * par:256 * j + P * par + P], ALU.mult, ALU.add)
                            if j + par < 2:
                                ins.then_inc(sem("dve_step"), 1)
                                v.wait_ge(sem("dve_step"), n.next("dve_step"))
                    ins.then_inc(psum_free(k), 1)
                    v.wait_ge(psum_free(k), fills(k))
                for par in range(2):
                    k = T("gat") + par
                    v.wait_ge(psum_full(k), fills(k))
                    for t in range(NT):
                        ins = TT(attm[:, t, par:4:2, :], bank(k)[:, 256 * t:256 * t + 256].rearrange("p (j l) -> p j l", j=2),
                                 tri64[:, :].unsqueeze(1).to_broadcast([P, 2, P]), ALU.mult)
                        if t == 0:
                            ins.then_inc(sem("dve_step"), 1)
                            v.wait_ge(sem("dve_step"), n.next("dve_step"))
                    ins.then_inc(psum_free(k), 1)
                    v.wait_ge(psum_free(k), fills(k))
                for t in range(NT):
                    k = T("go") + t
                    v.wait_ge(psum_full(k), fills(k))
                    nc.vector.tensor_copy(mix[:, t, 1024:1536], bank(k)[:, :]).then_inc(psum_free(k), 1)
                    v.wait_ge(psum_free(k), fills(k))
                head_norm(lambda t: mix[:, t, 1024:1536], 8, GLA_DV, bc1v(layer, "glan").unsqueeze(1).to_broadcast([P, 4, GLA_DV]), 1.0)
                TT(mix[:, 0, 1024:1536], mix[:, 0, 1024:1536], tm[:, 0, 2560:3072], ALU.mult).then_inc(sem("dve_step"), 1)
                v.wait_ge(sem("dve_step"), n.next("dve_step"))
                TT(mix[:, 1, 1024:1536], mix[:, 1, 1024:1536], tm[:, 1, 2560:3072], ALU.mult).then_inc(sem("mix_ready"), 1)
                v.wait_ge(sem("mix_ready"), n.next("mix_ready"))
                v.sem_inc(sem("ptm_free"), 1)
                add_rows(T("wo"))
                norm_rows()
                norm_evac(T("n2"), cpl[:, 8:16])
                for f in range(KF):
                    k = T("ffn") + f
                    v.wait_ge(sem("silu_done"), n.next("silu_done"))
                    TT(hid[:, f, :], sil[:, f % 2, :], bank(k)[:, SEQ:2 * SEQ], ALU.mult).then_inc(psum_free(k), 1)
                add_rows(T("dn"))
                v.sem_inc(sem("h_ready"), 1)
                for i in range(4):
                    v.wait_ge(psum_free(T("pg") + i), fills(T("pg") + i))
                for i in range(4):
                    k = T("pp") + i
                    o = 512 * (i % 2)
                    v.wait_ge(psum_full(k), fills(k))
                    s_ = sg[:, i // 2, o:o + 512]
                    TT(s_, s_, bank(k)[:, :], ALU.mult).then_inc(psum_free(k), 1)
                    v.wait_ge(psum_free(k), fills(k))
                    TT(h[:, i // 2, o:o + 512], h[:, i // 2, o:o + 512], s_, ALU.add).then_inc(sem("dve_step"), 1)
                    v.wait_ge(sem("dve_step"), n.next("dve_step"))
                v.sem_inc(sem("layer_done"), 1)
                if layer == 0:
                    v.sem_inc(sem("arena_free"), 1)

            v.wait_ge(sem("bc2_loaded"), 16 * 11)
            norm_rows(meta=True)
            norm_evac(TILE["m1"], cp2[:, 0:8])
            k = TILE["mm"]
            v.wait_ge(psum_full(k), fills(k))
            TT(xT[:, 0:8, 0:NM], bank(k)[:, 0:P].rearrange("p (k t) -> p k t", k=8),
                    cp2[:, 0:8].unsqueeze(2).to_broadcast([P, 8, NM]), ALU.mult).then_inc(psum_free(k), 1)
            TT(s8[:, 16, 0:4], cp2[:, 8:12], cp2[:, 12:16], ALU.subtract).then_inc(sem("lbd_ready"), 1)
            v.wait_ge(sem("lbd_ready"), n.next("lbd_ready"))
            v.wait_ge(sem("lb_sig"), n.next("lb_sig"))
            TS(s8[:, 18, 0:4], s8[:, 17, 0:4], -1.0, 1.0, ALU.mult, ALU.add).then_inc(sem("dve_step"), 1)
            v.wait_ge(sem("dve_step"), n.next("dve_step"))
            v.wait_ge(sem("f_sig"), n.next("f_sig"))
            oml = s8[:, 18, 0:4].unsqueeze(2).to_broadcast([P, 4, NTOK])
            TT(kT, kT, oml, ALU.mult).then_inc(sem("dve_step"), 1)
            v.wait_ge(sem("dve_step"), n.next("dve_step"))
            TT(fT, fT, oml, ALU.mult).then_inc(sem("dve_step"), 1)
            v.wait_ge(sem("dve_step"), n.next("dve_step"))
            TT(fT, fT, s8[:, 17, 0:4].unsqueeze(2).to_broadcast([P, 4, NTOK]), ALU.add).then_inc(sem("f_ready"), 1)
            v.wait_ge(sem("f_ready"), n.next("f_ready"))
            v.wait_ge(sem("f_ln"), n.next("f_ln"))
            for hh in range(HG_H):
                nc.vector.tensor_tensor_scan(Gm[:, hh, :], ones[:, 0:NM], fT[:, hh, 0:NM], 0.0, ALU.mult, ALU.add).then_inc(sem("dve_step"), 1)
                v.wait_ge(sem("dve_step"), n.next("dve_step"))
                for t in range(NT):
                    nc.vector.tensor_tensor_scan(G[:, hh, P * t:P * t + P], ones[:, :], fT[:, hh, NM + P * t:NM + P * t + P], 0.0, ALU.mult, ALU.add).then_inc(sem("dve_step"), 1)
                    v.wait_ge(sem("dve_step"), n.next("dve_step"))
            v.sem_inc(sem("h_norm"), 1)
            TT(fT[:, :, 0:NM], Gm[:, :, NM - 1:NM].to_broadcast([P, 4, NM]), Gm, ALU.subtract).then_inc(sem("dve_step"), 1)
            v.wait_ge(sem("dve_step"), n.next("dve_step"))
            TT(klev[:, :, 0:P], G[:, :, P - 1:P].to_broadcast([P, 4, P]), G[:, :, 0:P], ALU.subtract).then_inc(sem("dve_step"), 1)
            v.wait_ge(sem("dve_step"), n.next("dve_step"))
            v.sem_inc(sem("gend_ready"), 1)
            v.wait_ge(sem("gend_exp"), n.next("gend_exp"))
            TT(fT[:, :, 0:NM], fT[:, :, 0:NM], kT[:, :, 0:NM], ALU.mult).then_inc(sem("dve_step"), 1)
            v.wait_ge(sem("dve_step"), n.next("dve_step"))
            TT(klev[:, :, 0:P], klev[:, :, 0:P], kT[:, :, NM:NM + P], ALU.mult).then_inc(sem("ke_ready"), 1)
            v.wait_ge(sem("ke_ready"), n.next("ke_ready"))
            k = TILE["hsm"]
            v.wait_ge(psum_full(k), fills(k))
            nc.vector.tensor_copy(S[:, 0], bank(k)[:, :].rearrange("p (h d) -> p h d", h=4)).then_inc(psum_free(k), 1)
            v.wait_ge(psum_free(k), fills(k))
            k = TILE["hs0"]
            v.wait_ge(psum_full(k), fills(k))
            nc.vector.tensor_copy(S[:, 1], bank(k)[:, :].rearrange("p (h d) -> p h d", h=4)).then_inc(psum_free(k), 1)
            v.wait_ge(psum_free(k), fills(k))
            g2 = G.rearrange("p h t -> p (h t)")
            w2 = wlev.rearrange("p h t -> p (h t)")

            def level_diff(i):
                b2 = 2 * LEVELS[i]
                gv = g2.rearrange("p (n b) -> p n b", b=b2)
                TT(w2.rearrange("p (n b) -> p n b", b=b2), gv,
                          gv[:, :, b2 // 2 - 1:b2 // 2].to_broadcast([P, 1024 // b2, b2]), ALU.subtract).then_inc(sem("diff_ready"), 1)
                v.wait_ge(sem("diff_ready"), n.next("diff_ready"))
            level_diff(0)
            for i in range(len(LEVELS) + 1):
                if i < len(LEVELS):
                    v.wait_ge(sem("w_ready"), i + 1)
                    TT(qlev, qT, wlev, ALU.mult).then_inc(sem("qlev_ready"), 1)
                    v.wait_ge(sem("qlev_ready"), n.next("qlev_ready"))
                    v.wait_ge(sem("klev_ready"), i + 1)
                    if i + 1 < len(LEVELS):
                        level_diff(i + 1)
                for t in range(NT):
                    k = TILE["lev"] + 2 * i + t
                    v.wait_ge(psum_full(k), fills(k))
                    src = bank(k)[:, :].rearrange("p (h l) -> p h l", h=4)
                    mask = lev[:, i, :].unsqueeze(1).to_broadcast([P, 4, P])
                    if i == 0:
                        TT(acc[:, t], src, mask, ALU.mult).then_inc(psum_free(k), 1)
                        v.wait_ge(psum_free(k), fills(k))
                    else:
                        tmp = xn[:, t, 0:512].rearrange("p (h l) -> p h l", h=4)
                        TT(tmp, src, mask, ALU.mult).then_inc(psum_free(k), 1)
                        v.wait_ge(psum_free(k), fills(k))
                        TT(acc[:, t], acc[:, t], tmp, ALU.add).then_inc(sem("dve_step"), 1)
                        v.wait_ge(sem("dve_step"), n.next("dve_step"))
            v.sem_inc(sem("qexp_asked"), 1)
            v.wait_ge(sem("qexp_done"), n.next("qexp_done"))
            for hh in range(HG_H):
                STT(S[:, 1, hh, :], S[:, 0, hh, :], wlev[:, hh, P - 1:P], S[:, 1, hh, :], ALU.mult, ALU.add).then_inc(sem("dve_step"), 1)
                v.wait_ge(sem("dve_step"), n.next("dve_step"))
            TT(qlev, qT, wlev, ALU.mult).then_inc(sem("inter_ready"), 1)
            v.wait_ge(sem("inter_ready"), n.next("inter_ready"))
            for t in range(NT):
                k = TILE["ho"] + t
                v.wait_ge(psum_full(k), fills(k))
                nc.vector.tensor_copy(oa[:, t, :], bank(k)[:, :]).then_inc(psum_free(k), 1)
                v.wait_ge(psum_free(k), fills(k))
            for t in range(NT):
                sq = xn[:, 1, 0:512]
                TT(sq, oa[:, t, :], oa[:, t, :], ALU.mult).then_inc(sem("dve_step"), 1)
                v.wait_ge(sem("dve_step"), n.next("dve_step"))
                nc.vector.reduce_sum(st1[:, 4 * t:4 * t + 4], sq.rearrange("p (h d) -> p h d", d=P), axis=AX.X).then_inc(sem("dve_step"), 1)
                v.wait_ge(sem("dve_step"), n.next("dve_step"))
            rsqrt(8, P)
            for t in range(NT):
                o3 = oa[:, t, :].rearrange("p (h d) -> p h d", d=P)
                TT(o3, o3, st2[:, 4 * t:4 * t + 4].unsqueeze(2).to_broadcast([P, 4, P]), ALU.mult).then_inc(sem("dve_step"), 1)
                v.wait_ge(sem("dve_step"), n.next("dve_step"))
                TT(oa[:, t, :], oa[:, t, :], bc2v("hgn"), ALU.mult).then_inc(sem("dve_step"), 1)
                v.wait_ge(sem("dve_step"), n.next("dve_step"))
                TT(oa[:, t, :], oa[:, t, :], og[:, t, :], ALU.mult).then_inc(sem("dve_step"), 1)
                v.wait_ge(sem("dve_step"), n.next("dve_step"))
            v.sem_inc(sem("oa_ready"), 1)
            for t in range(NT):
                k = TILE["oaT"] + t
                v.wait_ge(psum_full(k), fills(k))
                nc.vector.tensor_copy(oaT[:, :, P * t:P * t + P], bank(k)[:, :].rearrange("p (j t) -> p j t", j=4)).then_inc(psum_free(k), 1)
            v.wait_ge(sem("zeros"), n.next("zeros"))
            for m in range(KD):
                TS(xc[:, m, :], lx[:, m, 0:NTOK], cp2[:, 16 + m:17 + m], cp2[:, 48 + m:49 + m], ALU.mult, ALU.add).then_inc(sem("dve_step"), 1)
                v.wait_ge(sem("dve_step"), n.next("dve_step"))
                for j in range(1, CONV):
                    STT(xc[:, m, :], lx[:, m, j:j + NTOK], cp2[:, 16 + 8 * j + m:17 + 8 * j + m], xc[:, m, :], ALU.mult, ALU.add).then_inc(sem("dve_step"), 1)
                    v.wait_ge(sem("dve_step"), n.next("dve_step"))
            v.sem_inc(sem("xc_ready"), 1)
            v.sem_inc(sem("xc_ready"), 1)
            v.sem_inc(sem("lam_ready"), 1)
            v.wait_ge(sem("lam_ln"), n.next("lam_ln"))
            lam8 = s8[:, 21, 0:8]
            TS(lam8, cp2[:, 72:80], -1.0, 0.0, ALU.mult, ALU.max).then_inc(sem("dve_step"), 1)
            v.wait_ge(sem("dve_step"), n.next("dve_step"))
            TT(lam8, lam8, s8[:, 20, 0:8], ALU.add).then_inc(sem("dve_step"), 1)
            v.wait_ge(sem("dve_step"), n.next("dve_step"))
            TS(lam8, lam8, -8.0, None, ALU.mult).then_inc(sem("dve_step"), 1)
            v.wait_ge(sem("dve_step"), n.next("dve_step"))
            TT(ra, ra, lam8.unsqueeze(2).to_broadcast([P, 8, NTOK]), ALU.mult).then_inc(sem("loga_ready"), 1)
            v.wait_ge(sem("loga_ready"), n.next("loga_ready"))
            TT(xc, xc, iu, ALU.mult).then_inc(sem("dve_step"), 1)
            v.wait_ge(sem("dve_step"), n.next("dve_step"))
            v.wait_ge(sem("a_ready"), n.next("a_ready"))
            iux = iu[:, :, NM:]
            TT(iux, ly, ly, ALU.mult).then_inc(sem("dve_step"), 1)
            v.wait_ge(sem("dve_step"), n.next("dve_step"))
            TS(iux, iux, 0.044715, 1.0, ALU.mult, ALU.add).then_inc(sem("dve_step"), 1)
            v.wait_ge(sem("dve_step"), n.next("dve_step"))
            TT(iux, iux, ly, ALU.mult).then_inc(sem("gelu_asked"), 1)
            v.wait_ge(sem("gelu_asked"), n.next("gelu_asked"))
            v.wait_ge(sem("gelu_tanh"), n.next("gelu_tanh"))
            STT(ly, iux, 1.0, ly, ALU.add, ALU.mult).then_inc(sem("dve_step"), 1)
            v.wait_ge(sem("dve_step"), n.next("dve_step"))
            TT(iu, ra, ra, ALU.mult).then_inc(sem("dve_step"), 1)
            v.wait_ge(sem("dve_step"), n.next("dve_step"))
            STT(th, iu, 1.0, th, ALU.add, ALU.mult).then_inc(sem("sq_ready"), 1)
            v.wait_ge(sem("sq_ready"), n.next("sq_ready"))
            v.wait_ge(sem("sq_done"), n.next("sq_done"))
            TT(xc, xc, th, ALU.mult).then_inc(sem("dve_step"), 1)
            v.wait_ge(sem("dve_step"), n.next("dve_step"))
            for m in range(KD):
                nc.vector.tensor_tensor_scan(th[:, m, :], ra[:, m, :], xc[:, m, :], 0.0, ALU.mult, ALU.add).then_inc(sem("dve_step"), 1)
                v.wait_ge(sem("dve_step"), n.next("dve_step"))
            STT(th[:, :, NM:], th[:, :, NM:], 0.5, ly, ALU.mult, ALU.mult).then_inc(sem("lru_ready"), 1)
            v.wait_ge(sem("lru_ready"), n.next("lru_ready"))
            for i in range(4):
                k = TILE["ua"] + i
                v.wait_ge(psum_full(k), fills(k))
                TT(ga[:, 2 * i:2 * i + 2, :], ga[:, 2 * i:2 * i + 2, :], bank(k)[:, :].rearrange("p (m t) -> p m t", m=2), ALU.mult).then_inc(psum_free(k), 1)
                v.wait_ge(psum_free(k), fills(k))
            for i in range(4):
                k = TILE["ub"] + i
                v.wait_ge(psum_full(k), fills(k))
                TT(gb[:, 2 * i:2 * i + 2, :], gb[:, 2 * i:2 * i + 2, :], bank(k)[:, :].rearrange("p (m t) -> p m t", m=2), ALU.mult).then_inc(psum_free(k), 1)
                v.wait_ge(psum_free(k), fills(k))
            TT(mTt, ga, gb, ALU.add).then_inc(sem("merged_ready"), 1)
            v.wait_ge(sem("merged_ready"), n.next("merged_ready"))
            add_rows(TILE["wo2"])
            norm_rows(gain_row=bc2v("n2"))
            norm_evac(TILE["m2"], None)
            k = TILE["rt"]
            v.wait_ge(psum_full(k), fills(k))
            lg = xn[:, 0, 0:72].rearrange("p (t e) -> p t e", t=2)
            bias = bc[:, 2560:2596].unsqueeze(1).to_broadcast([P, NT, NG + NE])
            TT(lg, bank(k)[:, 0:P].rearrange("p (t e) -> p t e", t=2)[:, :, 0:NG + NE], bias, ALU.add).then_inc(psum_free(k), 1)
            v.wait_ge(psum_free(k), fills(k))
            iof = s8[:, 15, 0:8]
            nc.vector.tensor_copy(iof, xs_[:, 0:8]).then_inc(sem("dve_step"), 1)
            v.wait_ge(sem("dve_step"), n.next("dve_step"))
            for i in range(8):
                v.memset(s8[:, 15, i:i + 1], float(i) - 64.0).then_inc(sem("dve_step"), 1)
                v.wait_ge(sem("dve_step"), n.next("dve_step"))

            def first_max(val, w, mx, hot, at):
                b3 = [P, NT, w]
                nc.vector.reduce_max(mx, val, axis=AX.X).then_inc(sem("dve_step"), 1)
                v.wait_ge(sem("dve_step"), n.next("dve_step"))
                TT(hot, val, mx.unsqueeze(2).to_broadcast(b3), ALU.is_equal).then_inc(sem("dve_step"), 1)
                v.wait_ge(sem("dve_step"), n.next("dve_step"))
                TT(hot, hot, iof[:, 0:w].unsqueeze(1).to_broadcast(b3), ALU.mult).then_inc(sem("dve_step"), 1)
                v.wait_ge(sem("dve_step"), n.next("dve_step"))
                nc.vector.tensor_reduce(at, hot, AX.X, ALU.min).then_inc(sem("dve_step"), 1)
                v.wait_ge(sem("dve_step"), n.next("dve_step"))
                TT(hot, iof[:, 0:w].unsqueeze(1).to_broadcast(b3), at.unsqueeze(2).to_broadcast(b3), ALU.is_equal).then_inc(sem("dve_step"), 1)
                v.wait_ge(sem("dve_step"), n.next("dve_step"))

            gl = lg[:, :, 0:NG]
            gmx, gat, ghot = s8[:, 5, 0:2], s8[:, 5, 2:4], s8[:, 6:8, 0:NG]
            first_max(gl, NG, gmx, ghot, gat)
            TT(s8[:, 2:4, 0:NG], gl, gmx.unsqueeze(2).to_broadcast([P, NT, NG]), ALU.subtract).then_inc(sem("dve_step"), 1)
            v.wait_ge(sem("dve_step"), n.next("dve_step"))
            sel = s8[:, 9:11, 0:8]
            tmp = s8[:, 11:13, 0:8]
            for g_ in range(NG):
                dst = sel if g_ == 0 else tmp
                TT(dst, lg[:, :, NG + EPG * g_:NG + EPG * g_ + EPG], ghot[:, :, g_:g_ + 1].to_broadcast([P, NT, EPG]), ALU.mult).then_inc(sem("dve_step"), 1)
                v.wait_ge(sem("dve_step"), n.next("dve_step"))
                if g_:
                    TT(sel, sel, tmp, ALU.add).then_inc(sem("dve_step"), 1)
                    v.wait_ge(sem("dve_step"), n.next("dve_step"))
            m1, a1, h1 = s8[:, 5, 4:6], s8[:, 5, 6:8], s8[:, 13:15, 0:8]
            m2, a2, h2 = s8[:, 5, 8:10], s8[:, 5, 10:12], s8[:, 16:18, 0:8]
            first_max(sel, EPG, m1, h1, a1)
            STT(sel, h1, -3e38, sel, ALU.mult, ALU.add).then_inc(sem("dve_step"), 1)
            v.wait_ge(sem("dve_step"), n.next("dve_step"))
            first_max(sel, EPG, m2, h2, a2)
            TT(s8[:, 4, 0:2], m2, m1, ALU.subtract).then_inc(sem("route_exp_asked"), 1)
            v.wait_ge(sem("route_exp_asked"), n.next("route_exp_asked"))
            v.wait_ge(sem("route_exp"), n.next("route_exp"))
            ps_, w1, w2_ = s8[:, 18, 0:2], s8[:, 18, 2:4], s8[:, 18, 4:6]
            nc.vector.reduce_sum(ps_, s8[:, 2:4, 0:NG], axis=AX.X).then_inc(sem("dve_step"), 1)
            v.wait_ge(sem("dve_step"), n.next("dve_step"))
            STT(ps_, s8[:, 4, 0:2], 1.0, ps_, ALU.add, ALU.mult).then_inc(sem("dve_step"), 1)
            v.wait_ge(sem("dve_step"), n.next("dve_step"))
            nc.vector.reciprocal(w1, ps_).then_inc(sem("dve_step"), 1)
            v.wait_ge(sem("dve_step"), n.next("dve_step"))
            TT(w2_, w1, s8[:, 4, 0:2], ALU.mult).then_inc(sem("dve_step"), 1)
            v.wait_ge(sem("dve_step"), n.next("dve_step"))
            TT(h1, h1, w1.unsqueeze(2).to_broadcast([P, NT, 8]), ALU.mult).then_inc(sem("dve_step"), 1)
            v.wait_ge(sem("dve_step"), n.next("dve_step"))
            TT(h2, h2, w2_.unsqueeze(2).to_broadcast([P, NT, 8]), ALU.mult).then_inc(sem("dve_step"), 1)
            v.wait_ge(sem("dve_step"), n.next("dve_step"))
            TT(h1, h1, h2, ALU.add).then_inc(sem("dve_step"), 1)
            v.wait_ge(sem("dve_step"), n.next("dve_step"))
            for g_ in range(NG):
                TT(gate[:, :, EPG * g_:EPG * g_ + EPG], h1, ghot[:, :, g_:g_ + 1].to_broadcast([P, NT, EPG]), ALU.mult).then_inc(sem("dve_step"), 1)
                v.wait_ge(sem("dve_step"), n.next("dve_step"))

            def expert(i, j):
                first = isinstance(i, int)
                for m in range(KE):
                    at = KE * j + m + 1
                    v.wait_ge(sem("expert_silu"), at if first else i * (KE * LE) + at)
                    if m == 0 and not (first and j < 2):
                        v.wait_ge(sem("down_done"), 4 * (j - 1) if first else i * (4 * LE) + 4 * (j - 1))
                    TT(hidE[:, j % 2, m, :], silE[:, m % 2, :], psum[m][:, SEQ:2 * SEQ], ALU.mult).then_inc(sem("hidden_ready"), 1)
                for q in range(4):
                    t, half = divmod(q, 2)
                    at = 4 * j + q + 1
                    v.wait_ge(sem("down_done"), at if first else i * (4 * LE) + at)
                    wt = gate[:, t, j:j + 1] if first else gate[:, t, bass.ds(i * LE + j, 1)]
                    dst = h[:, t, 512 * half:512 * half + 512]
                    STT(dst, psum[4 + q][:, :], wt, dst, ALU.mult, ALU.add).then_inc(sem("experts_added"), 1)
            for j in range(LE):
                expert(0, j)
            with v.Fori(1, NE // LE) as i:
                for j in range(LE):
                    expert(i, j)
            v.wait_ge(sem("experts_added"), 4 * NE)
            norm_rows(gain_row=bc2v("fin"))


_INS = ['x', 'p', 'positions', 'attn_norm', 'w_in', 'da_q_norm', 'da_k_norm', 'da_lambda_q1', 'da_lambda_k1',
        'da_lambda_q2', 'da_lambda_k2', 'da_sub_norm', 'ssd_conv_w', 'ssd_conv_b', 'ssd_dt_bias', 'ssd_a_log',
        'ssd_d', 'ssd_norm', 'gla_w_gate2', 'gla_b_gate', 'gla_norm', 'w_out', 'ffn_norm', 'w_ffn_gate', 'w_ffn_up',
        'w_ffn_down', 'ple_w_proj', 'ple_w_gate', 'meta_tokens_2', 'norm1_g_2', 'w_in_2', 'hg_lower_bounds_2',
        'hg_norm_g_2', 'conv_w_2', 'conv_b_2', 'lru_w_r_2', 'lru_b_r_2', 'lru_w_i_2', 'lru_b_i_2', 'lru_lambda_2',
        'w_up_a_2', 'w_up_b_2', 'w_out_2', 'norm2_g_2', 'w_group_2', 'b_group_2', 'w_router_2', 'b_router_2',
        'w_gate_2', 'w_up_2', 'w_down_2', 'final_g_2']


def kernel(**inputs):
    import numpy as _np
    import concourse.bacc as _bacc
    from concourse import mybir as _mybir
    from concourse.bass_utils import run_bass_kernel_spmd as _run

    nc = _bacc.Bacc("TRN2", target_bir_lowering=False, num_devices=1)
    arrays, d = {}, {}
    for name in _INS:
        a = _np.ascontiguousarray(inputs[name])
        arrays[f"in_{name}"] = a
        d[name] = nc.dram_tensor(f"in_{name}", a.shape, _mybir.dt.from_np(a.dtype), kind="ExternalInput").ap()
    out = nc.dram_tensor("out_0", (1, SEQ, D), _mybir.dt.float32, kind="ExternalOutput").ap()
    program(nc, d, out)
    r = _run(nc, [arrays], core_ids=[0])
    return r.results[0]["out_0"]
```

```python
import math
from contextlib import ExitStack

import concourse.bass as bass
from concourse import mybir
import numpy as np

F32 = mybir.dt.float32
I32 = mybir.dt.int32
ACT = mybir.ActivationFunctionType
ALU = mybir.AluOpType
AX = mybir.AxisListType

P = 128
D = 1024
KD = D // P
SEQ = 256
NT = SEQ // P
DEPTH = 2
EPS = 1e-6
SLOT = 4096
NB = 3
NPS = 8

DA_H, DQK, DV, ROT = 4, 64, 128, 16
ROPE_THETA = 500000.0
SSD_H, SSD_P, SSD_N, SSD_G, CONV = 8, 64, 128, 2, 4
GLA_H, GLA_DK, GLA_DV, GLA_C, GLA_RANK = 4, 64, 128, 64, 16
D_FF = 2816
KF = D_FF // P
MIX = 1536
KM = MIX // P
COL = dict(q=0, k=512, v=1024, z=1536, xbc=2048, dt=3072, gq=3080, gk=3336, gv=3592, gg=4104, lr=4616)

NM = 16
NTOK = NM + SEQ
HG_H = 4
LB = 8
NG, EPG = 4, 8
NE = NG * EPG
DE = 512
KE = DE // P
SL = 64
PAIRS = NE // 2
MAX_PASSES = SEQ // SL
LEVELS = [64, 32, 16, 8, 4, 2, 1]

LAYER_TILES = [
    ("n1", 4), ("q", 2), ("k", 2), ("lr", 1), ("dt", 1), ("xbc", 4), ("qkT", 4), ("v", 2), ("sc", 8), ("gqk", 2), ("xbT", 3),
    ("z", 2), ("at", 3), ("pv", 2), ("cumc", 1), ("cumb", 4), ("cb", 1), ("gv", 2), ("gk", 1), ("gg", 2), ("yd", 2), ("st", 1),
    ("yo", 1), ("keT", 1), ("gst", 3), ("gat", 2), ("go", 2),
    ("mixT", 6), ("wo", 4), ("n2", 4), ("ffn", KF), ("dn", 4), ("n3", 4), ("pT", 1), ("pg", 4), ("pp", 4),
]
N_LEVELS = len(LEVELS) + 1
UNITS = 12
UNITS_AFTER = [[0], [], [1], [], [2], [], [3], [4]]
UNITS_NORM, UNITS_CONV, UNITS_LRU = [5, 6], [7, 8, 9], [10, 11]


def unit_tiles(units):
    return [(("unit", u), 1) for u in units]


SECOND_TILES = (
    [("m1", 4), ("mm", 1), ("hf", 4), ("hq", 2), ("hi", 3), ("hog", 2), ("lx", 8), ("hkm", 1), ("hk0", 1), ("hsm", 1), ("hs0", 1)]
    + [tile for i in range(N_LEVELS) for tile in [(("lev", i), 2)] + unit_tiles(UNITS_AFTER[i])]
    + [("ho", 2)] + unit_tiles(UNITS_NORM) + [("oaT", 2)] + unit_tiles(UNITS_CONV) + [("lr_r", 8), ("lr_i", 8), ("ua", 4)]
    + unit_tiles(UNITS_LRU) + [("ub", 4), ("wo2", 4), ("m2", 4), ("rt", 1), ("rk", 1)]
)


def number_tiles():
    first, n = {}, 0
    for name, count in [("cp", 2)]:
        first[name] = n
        n += count
    for layer in range(DEPTH):
        for name, count in LAYER_TILES:
            first[name, layer] = n
            n += count
    for name, count in SECOND_TILES:
        first[name] = n
        n += count
    return first, n


TILE, N_TILES = number_tiles()

ROWS1 = 58
CP1 = dict(an=0, fn=8, cw=16, cb=48, gb=56)
CP2 = dict(n1=0, lb=8, cw=16, cb=48, br=56, bi=64, lam=72)
BC1 = dict(gq=(0, 64), gk=(64, 64), lq1=(128, 64), lk1=(192, 64), lq2=(256, 64), lk2=(320, 64),
           gsub=(384, 128), dtb=(512, 8), alog=(520, 8), dsk=(528, 8), ssdn=(536, 512), glan=(1048, 128))
NBC1 = 1176
BC2 = dict(hgn=(0, 512), n2=(512, 1024), fin=(1536, 1024), bg=(2560, 4), brt=(2564, 32))
NBC2 = 2596


def lambda_init(layer):
    return 0.8 - 0.6 * math.exp(-0.3 * layer)


def first_loads(d, layer):
    w = d["w_in"][layer].rearrange("(k p) n -> p k n", p=P)
    T = lambda name: TILE[name, layer]
    out = []

    def cols(c0, n, tile):
        out.append(([(0, KD, n, w[:, :, c0:c0 + n])], ("full", tile)))
    cols(COL["q"], 512, T("q") + 1)
    cols(COL["k"], 512, T("k") + 1)
    out.append(([(0, KD, 16, w[:, :, COL["lr"]:COL["lr"] + 16]), (KD * 16, KD, 8, w[:, :, COL["dt"]:COL["dt"] + 8])],
                ("full", T("dt"))))
    cols(COL["xbc"], 512, T("xbc") + 1)
    cols(COL["xbc"] + 512, 512, T("xbc") + 3)
    cols(COL["v"], 512, T("v") + 1)
    cols(COL["gq"], 512, T("gqk") + 1)
    cols(COL["z"], 512, T("z") + 1)
    cols(COL["gv"], 512, T("gv") + 1)
    cols(COL["gg"], 512, T("gg") + 1)
    rows(out, d["w_out"][layer], KM, T("wo") + 3)
    g = d["w_ffn_gate"][layer].rearrange("(k p) n -> p k n", p=P)
    u = d["w_ffn_up"][layer].rearrange("(k p) n -> p k n", p=P)
    for f in range(KF // 2):
        out.append(([(0, KD, 256, g[:, :, 256 * f:256 * f + 256]), (2048, KD, 256, u[:, :, 256 * f:256 * f + 256])],
                    ("full", T("ffn") + 2 * f + 1)))
    rows(out, d["w_ffn_down"][layer], KF, T("dn") + 3)
    rows(out, d["ple_w_gate"][layer], KD, T("pg") + 3)
    rows(out, d["ple_w_proj"][layer], 2, T("pp") + 3)
    return out


def rows(out, w, k_chunks, last_tile):
    v = w.rearrange("(k p) n -> p k n", p=P)
    for k in range(0, k_chunks, 4):
        n = min(4, k_chunks - k)
        out.append(([(0, n, D, v[:, k:k + n, :])], ("full", last_tile) if k + n == k_chunks else ("used",)))


def second_loads(d):
    w = d["w_in_2"][0].rearrange("(k p) n -> p k n", p=P)
    out = []
    for c0, tile in ((512, TILE["hf"] + 3), (0, TILE["hq"] + 1), (1024, TILE["hi"] + 2), (1536, TILE["hog"] + 1),
                     (2048, TILE["lx"] + 3), (2560, TILE["lx"] + 7), *[(3072 + 512 * i, TILE["unit", 2 * i + 1]) for i in range(UNITS // 2 - 1)]):
        out.append(([(0, KD, 512, w[:, :, c0:c0 + 512])], ("full", tile)))
    r = [(0, LB, P, d["lru_w_r_2"][0].rearrange("n i j -> i n j")), (1024, LB, P, d["lru_w_i_2"][0].rearrange("n i j -> i n j"))]
    out.append((r, ("full", TILE["lr_i"] + 7)))
    rows(out, d["w_up_a_2"][0], 4, TILE["ua"] + 3)
    out.append(([(0, KD, 512, w[:, :, 5632:6144])], ("full", TILE["unit", UNITS - 1])))
    v = d["w_up_b_2"][0].rearrange("(k p) n -> p k n", p=P)
    out.append(([(0, 4, D, v[:, 0:4, :])], ("full", TILE["ub"] + 3)))
    out.append(([(0, 4, D, v[:, 4:8, :])], ("full", TILE["ub"] + 3)))
    rows(out, d["w_out_2"][0], KD, TILE["wo2"] + 3)
    return out


def program(nc, d, out):
    LOADS = first_loads(d, 0) + first_loads(d, 1) + second_loads(d)
    n, freed = 0, []
    for _, by in LOADS:
        if by[0] == "used":
            n += 1
            freed.append(("used", n))
        else:
            freed.append(by)
    N_LOADS = len(LOADS)
    full_at, filled = [], [0] * NB
    for c, (parts, _) in enumerate(LOADS):
        filled[c % NB] += 16 * len(parts)
        full_at.append(filled[c % NB])

    with ExitStack() as ctx:
        def sb(name, shape, dt=F32):
            return ctx.enter_context(nc.sbuf_tensor(name, shape, dt))

        sems = {}

        def sem(name):
            if name not in sems:
                sems[name] = ctx.enter_context(nc.semaphore(name))
            return sems[name]

        ring = sb("weights", [P, NB, SLOT])
        h = sb("h", [P, NT, D])
        hmeta = sb("h_meta", [P, D])
        xT = sb("xT", [P, KM, NTOK])
        xn = sb("xn", [P, NT, D])
        mix = sb("mix", [P, NT, MIX])
        bc = sb("bc", [P, NBC2])
        prow1 = mix[:, 0, 0:P]
        prow2 = mix[:, 0, P:2 * P]
        cp1 = sb("cp1", [P, DEPTH * ROWS1])
        cp2 = sb("cp2", [P, 80])
        gw2 = sb("gw2", [GLA_RANK, DEPTH, 256])
        wrt = sb("wrt", [P, KD, NG + NE])
        ident = sb("ident", [P, P])
        tri = sb("tri", [P, P])
        tri64 = sb("tri64", [P, P])
        ones = sb("ones", [P, P])
        neg = sb("neg", [P, P])
        lev = sb("lev", [P, 8, P])
        xi = sb("xi", [P, P], I32)
        xs_ = sb("xs_", [P, P], I32)
        xf = sb("xf", [P, P])
        pos = sb("pos", [P, NT], I32)
        posf = sb("posf", [P, NT])
        ang = sb("ang", [P, NT, 8])
        angk = sb("angk", [P, NT, 8])
        angi = sb("angi", [P, NT, 8], I32)
        cos = sb("cos", [P, NT, 8])
        passes = sb("passes", [P, 1], I32)
        place_i = sb("place_i", [P, SL], I32)
        sin = sb("sin", [P, NT, 8])
        frq = sb("frq", [P, 8])
        st1 = sb("st1", [P, 64])
        st2 = sb("st2", [P, 64])
        mhalf = sb("mhalf", [P, 64])
        s8 = sb("s8", [P, 32, 32])
        arena = sb("arena", [P, 22400])
        psum = [ctx.enter_context(nc.psum_tensor(f"bank{i}", [P, 512], F32)) for i in range(NPS)]

        class Carve:
            def __init__(self, at):
                self.at = at

            def take(self, *shape):
                n = int(np.prod(shape))
                v = arena[:, self.at:self.at + n]
                self.at += n
                assert self.at <= 22400, self.at
                if len(shape) == 2:
                    v = v.rearrange("p (a b) -> p a b", a=shape[0])
                elif len(shape) == 3:
                    v = v.rearrange("p (a b c) -> p a b c", a=shape[0], b=shape[1])
                elif len(shape) == 4:
                    v = v.rearrange("p (a b c e) -> p a b c e", a=shape[0], b=shape[1], c=shape[2])
                return v

        c = Carve(0)
        tm = c.take(NT, 3072)
        xbc = c.take(KD, SEQ + CONV - 1)
        gqk = c.take(4, SEQ)
        kz = c.take(3, 256)
        Sh = arena[:, NT * 3072:NT * 3072 + 2048].rearrange("p (a b e) -> p a b e", a=4, b=2)
        lrT = c.take(256)
        scratch = c.at
        qkT = c.take(2, DA_H, SEQ)
        sc = [c.take(8, P), c.take(8, SEQ)]
        attn = c.take(DA_H, SEQ)
        attnT = c.take(DA_H, 2, P)
        c = Carve(scratch)
        decay = c.take(NT, SSD_H, P)
        cbm = c.take(4, P)
        gcum = c.take(2, SEQ)
        eb = c.take(2, SEQ)
        enb = c.take(2, SEQ)
        qd = c.take(2, SEQ)
        ki = c.take(2, SEQ)
        ke = c.take(2, SEQ)
        attm = c.take(NT, GLA_H, P)
        gtmp = c.take(2, SEQ)
        cx = c.take(KD, SEQ)
        xh = c.take(NT, 512)
        B0 = c.take(2, P)
        xdt = c.take(NT, 512)
        sst = cx[:, 0:2, :]
        xdte = cx[:, 2:4, :]
        c = Carve(0)
        hid = c.take(KF, SEQ)
        sil = c.take(2, SEQ)
        sg = c.take(NT, D)
        ptm = c.take(NT, 256)
        pT = c.take(2, SEQ)
        c = Carve(0)
        lx = c.take(KD, NTOK + CONV - 1)
        ly = c.take(KD, SEQ)
        ga = c.take(KD, SEQ)
        gb = c.take(KD, SEQ)
        og = c.take(NT, 512)
        R = c.at
        fT = c.take(HG_H, NTOK)
        kT = c.take(HG_H, NTOK)
        qT = c.take(HG_H, SEQ)
        vt = c.take(3, 512)
        G = c.take(HG_H, SEQ)
        ke0 = c.take(HG_H, P)
        acc = c.take(NT, HG_H, P)
        S = c.take(2, HG_H, P)
        Gm = s8[:, 0:2, :].rearrange("p a (b e) -> p (a b) e", e=NM)
        c = Carve(R)
        xc = c.take(KD, NTOK)
        ra = c.take(KD, NTOK)
        iu = c.take(KD, NTOK)
        th = c.take(KD, NTOK)
        mflat = mix[:, :, :].rearrange("p a b -> p (a b)")
        wlev = mflat[:, 0:1024].rearrange("p (a b) -> p a b", a=HG_H)
        qlev = mflat[:, 1024:2048].rearrange("p (a b) -> p a b", a=HG_H)
        klev = mflat[:, 2048:3072].rearrange("p (a b) -> p a b", a=HG_H)
        oaT = mflat[:, 0:1024].rearrange("p (a b) -> p a b", a=4)
        mTt = mflat[:, 1024:3072].rearrange("p (a b) -> p a b", a=KD)
        oa = xn[:, 0, :].rearrange("p (a b) -> p a b", a=NT)
        c = Carve(0)
        slots345 = c.take(3, SLOT)
        hidE = c.take(2, KE, SL)
        silE = c.take(2, KE * SL)
        xsE = c.take(KD, 2 * SL)
        yE = c.take(D)
        pick = c.take(NT, 2 * SL)
        pickw = c.take(NT, 2 * SL)
        pickT = c.take(NT * P)
        gate = c.take(NT, NE)
        chosen = c.take(NT, NE)
        rank = c.take(NT, NE)
        place = c.take(SL)
        expert_slot = [ring[:, i, :] for i in range(NB)] + [slots345[:, i, :] for i in range(3)]

        def bc1v(layer, name):
            o, n = BC1[name]
            return bc[:, layer * NBC1 + o:layer * NBC1 + o + n]

        def bc2v(name):
            o, n = BC2[name]
            return bc[:, o:o + n]

        def slot(ch, k, n, off=0):
            return ring[:, ch % NB, off:off + k * n].rearrange("p (k n) -> p k n", k=k)

        class Counts:

            def __init__(self):
                self.seen = {}

            def next(self, name, by=1):
                self.seen[name] = self.seen.get(name, 0) + by
                return self.seen[name]

        def psum_full(tile):
            return sem(f"psum_full{tile % NPS}")

        def psum_free(tile):
            return sem(f"psum_free{tile % NPS}")

        def fills(tile):
            return tile // NPS + 1

        def chunk_full(ch):
            return sem(f"chunk_full{ch % NB}")

        block = ctx.enter_context(nc.Block())

        def pair_full(b):
            return sem(f"pair_full{b}")

        def pair_free(b):
            return sem(f"pair_free{b}")

        @block.sync
        def _(sp):
            sp.dma_start(h[:, :, :], d["x"][0].rearrange("(t p) n -> p t n", p=P)).then_inc(sem("x_loaded"), 16)
            for ch, (parts, _) in enumerate(LOADS):
                if ch >= NB:
                    kind, at = freed[ch - NB]
                    if kind == "used":
                        sp.wait_ge(sem("chunks_used"), at)
                    else:
                        sp.wait_ge(psum_full(at), fills(at))
                for off, k, nn, src in parts:
                    sp.dma_start(slot(ch, k, nn, off), src).then_inc(sem(f"chunk_full{ch % NB}"), 16)
            wg = d["w_gate_2"][0].rearrange("e (k p) n -> e p k n", p=P)
            wu = d["w_up_2"][0].rearrange("e (k p) n -> e p k n", p=P)
            wd = d["w_down_2"][0].rearrange("e (k p) n -> e p k n", p=P)

            wsrc = [(wg, 0, KD), (wu, 0, KD), (wg, 1, KD), (wu, 1, KD), (wd, 0, KE), (wd, 1, KE)]

            def expert_load(pair, c6):
                src, odd, k = wsrc[c6]
                if isinstance(pair, int):
                    v = src[2 * pair + odd]
                else:
                    v = src[bass.ds(pair * 2 + odd, 1)].rearrange("e p k n -> (e p) k n")
                sp.dma_start(expert_slot[c6].rearrange("p (k n) -> p k n", k=k), v).then_inc(sem(f"expert_chunk{c6}"), 16)

            def pair_loads(n, pair):
                sp.wait_ge(pair_full(3), n)
                expert_load(pair, 0)
                expert_load(pair, 1)
                sp.wait_ge(pair_full(0), n * 2)
                expert_load(pair, 2)
                expert_load(pair, 3)
                sp.wait_ge(sem("down0_used"), n)
                expert_load(pair, 4)
                sp.wait_ge(pair_full(2), n * 2)
                expert_load(pair, 5)

            for q in range(NB):
                ch = N_LOADS - NB + q
                kind, at = freed[ch]
                if kind == "used":
                    sp.wait_ge(sem("chunks_used"), at)
                else:
                    sp.wait_ge(psum_full(at), fills(at))
                expert_load(0, ch % NB)
            for c6 in range(NB, 6):
                expert_load(0, c6)
            with sp.Fori(1, PAIRS) as i:
                pair_loads(i, i)
            sp.wait_ge(sem("passes_ready"), 1)
            n_passes = sp.value_load(passes[0:1, 0:1], min_val=1, max_val=MAX_PASSES)
            with sp.If(n_passes > 1):
                with sp.Fori(1, n_passes) as turn:
                    with sp.Fori(0, PAIRS) as i:
                        pair_loads(turn * PAIRS + i, i)
            sp.wait_ge(sem("xn_ready"), 2 * DEPTH + 3)
            sp.dma_start(out[0].rearrange("(t p) n -> p t n", p=P), xn[:, :, :]).then_inc(sem("out_stored"), 16)
            sp.wait_ge(sem("out_stored"), 16)

        @block.gpsimd
        def _(g):
            n = Counts()
            g.memset(ident[:, :], 0.0).then_inc(sem("g_zero"), 1)
            g.memset(ones[:, :], 1.0).then_inc(sem("g_zero"), 1)
            g.memset(neg[:, :], 0.0).then_inc(sem("g_zero"), 1)
            g.memset(tri64[:, :], 0.0).then_inc(sem("g_zero"), 1)
            g.wait_ge(sem("g_zero"), n.next("g_zero", 4))
            g.memset(tri64[0:64, 0:64], 1.0).then_inc(sem("g_zero"), 1)
            g.wait_ge(sem("g_zero"), n.next("g_zero"))
            g.memset(tri64[64:P, 64:P], 1.0).then_inc(sem("g_zero"), 1)
            g.wait_ge(sem("g_zero"), n.next("g_zero"))
            g.affine_select(out=ident[:, :], in_=ident[:, :], compare_op=ALU.not_equal, fill=1.0, base=0,
                            pattern=[[-1, P]], channel_multiplier=1).then_inc(sem("masks"), 1)
            g.affine_select(out=tri[:, :], in_=ones[:, :], compare_op=ALU.is_ge, fill=0.0, base=0,
                            pattern=[[1, P]], channel_multiplier=-1).then_inc(sem("masks"), 1)
            g.affine_select(out=tri64[:, :], in_=tri64[:, :], compare_op=ALU.is_ge, fill=0.0, base=0,
                            pattern=[[1, P]], channel_multiplier=-1).then_inc(sem("masks"), 1)
            g.affine_select(out=neg[:, :], in_=neg[:, :], compare_op=ALU.is_ge, fill=-1e30, base=0,
                            pattern=[[-1, P]], channel_multiplier=1).then_inc(sem("masks"), 1)
            g.iota(xi[:, :], pattern=[[1, P]], base=0, channel_multiplier=0).then_inc(sem("iotas"), 1)
            g.iota(xs_[:, :], pattern=[[0, P]], base=0, channel_multiplier=1).then_inc(sem("iotas"), 1)
            g.iota(place_i[:, :], pattern=[[1, SL]], base=0, channel_multiplier=0).then_inc(sem("iotas"), 1)
            for i in range(8):
                g.memset(frq[:, i:i + 1], float(np.float32(ROPE_THETA) ** np.float32(-2.0 * i / ROT)))
            g.memset(mhalf[:, :], -0.5).then_inc(sem("consts"), 1)
            def rsqrt(cols):
                g.wait_ge(sem("power_asked"), n.next("power_asked"))
                g.tensor_tensor(st2[:, 0:cols], st1[:, 0:cols], mhalf[:, 0:cols], ALU.pow).then_inc(sem("power_done"), 1)

            g.wait_ge(sem("consts"), 1)
            for layer in range(DEPTH):
                rsqrt(2)
                if layer:
                    g.wait_ge(sem("layer_done"), n.next("layer_done"))
                g.memset(kz[:, :, :], 0.0)
                g.memset(xbc[:, :, 0:CONV - 1], 0.0).then_inc(sem("zeros"), 1)
                rsqrt(32)
                g.wait_ge(sem("conv_sum"), n.next("conv_sum"))
                g.memset(Sh[:, :, :, :], 0.0).then_inc(sem("states_zero"), 1)
                rsqrt(8)
                rsqrt(4)
                rsqrt(8)
                rsqrt(2)
                g.wait_ge(sem("ptm_free"), n.next("ptm_free"))
                g.dma_start(ptm[:, :, :], d["p"][layer, 0].rearrange("(t p) n -> p t n", p=P)).then_inc(sem("p_loaded"), 16)
            g.wait_ge(sem("layer_done"), n.next("layer_done"))
            for name, key in (("hgn", "hg_norm_g_2"), ("n2", "norm2_g_2"), ("bg", "b_group_2")):
                g.dma_start(bc2v(name), d[key][0].partition_broadcast(P)).then_inc(sem("late_rows_loaded"), 16)
            g.dma_start(bc2v("fin"), d["final_g_2"].partition_broadcast(P)).then_inc(sem("late_rows_loaded"), 16)
            g.dma_start(bc2v("brt"), d["b_router_2"][0].rearrange("g e -> (g e)").partition_broadcast(P)).then_inc(sem("late_rows_loaded"), 16)
            g.memset(lx[:, :, 0:CONV - 1], 0.0).then_inc(sem("zeros"), 1)
            rsqrt(3)
            for i in range(len(LEVELS)):
                g.wait_ge(sem("w_ready"), n.next("w_ready"))
                if i:
                    g.wait_ge(psum_full(TILE["lev", i - 1] + 1), fills(TILE["lev", i - 1] + 1))
                else:
                    g.wait_ge(sem("h_norm"), n.next("h_norm"))
                g.tensor_tensor(klev, kT[:, :, NM:NTOK], wlev, ALU.mult).then_inc(sem("klev_ready"), 1)
            rsqrt(8)
            rsqrt(2)
            g.memset(yE, 0.0)
            g.memset(pickT, 0.0).then_inc(sem("moe_zero"), 1)
            rsqrt(2)

        @block.tensor
        def _(pe):
            n = Counts()
            mm = nc.tensor.matmul

            def claim(tile):
                if tile >= NPS:
                    pe.wait_ge(psum_free(tile - NPS), fills(tile - NPS))
                return psum[tile % NPS]

            def tokens_out(tile, ch, t0=NM):
                pe.wait_ge(chunk_full(ch), full_at[ch])
                w = slot(ch, KD, 512)
                for t in range(NT):
                    b = claim(tile + t)
                    for k in range(KD):
                        ins = mm(b[:, :], xT[:, k, t0 + P * t:t0 + P * t + P], w[:, k, :], start=(k == 0), stop=(k == KD - 1))
                    ins.then_inc(psum_full(tile + t), 1)

            def channels_out(tile, ch, n0, nt, per):
                pe.wait_ge(chunk_full(ch), full_at[ch])
                w = slot(ch, KD, 512)
                for m in range(4):
                    b = claim(tile + m // per)
                    o = (m % per) * nt
                    for k in range(KD):
                        ins = mm(b[:, o:o + nt], w[:, k, P * m:P * m + P], xT[:, k, n0:n0 + nt], start=(k == 0), stop=(k == KD - 1))
                    if m % per == per - 1:
                        ins.then_inc(psum_full(tile + m // per), 1)

            def transposes(tile, src, cols, q=P):
                b = claim(tile)
                for j, at in enumerate(cols):
                    ins = nc.tensor.transpose(b[:, q * j:q * j + q], src[0:q, at:at + P], ident[0:q, 0:q])
                ins.then_inc(psum_full(tile), 1)

            def norm_turns(tile, src):
                for t in range(NT):
                    for half in range(2):
                        transposes(tile + 2 * t + half, src[:, t, :], [512 * half + P * j for j in range(4)])

            def rows_out(tile, ch, k_chunks, lhs):
                banks = [claim(tile + i) for i in range(4)]
                for k in range(k_chunks):
                    if k % 4 == 0:
                        pe.wait_ge(chunk_full(ch), full_at[ch])
                    kn = min(4, k_chunks - (k - k % 4))
                    w = slot(ch, kn, D)
                    last = k == k_chunks - 1
                    for i in range(4):
                        t, half = divmod(i, 2)
                        ins = mm(banks[i][:, :], lhs(k, t), w[:, k % 4, 512 * half:512 * half + 512], start=(k == 0), stop=last)
                        if last:
                            ins.then_inc(psum_full(tile + i), 1)
                    if k % 4 == 3 and not last:
                        ins.then_inc(sem("chunks_used"), 1)
                    if k % 4 == 3:
                        ch += 1
                return ch

            pe.wait_ge(sem("rows_loaded"), 16 * 17)
            pe.wait_ge(sem("masks"), 4)
            for i, (src, r) in enumerate(((prow1, DEPTH * ROWS1), (prow2, 80))):
                b = claim(i)
                nc.tensor.transpose(b[:, 0:r], src[0:r, :], ident[0:r, 0:r]).then_inc(psum_full(i), 1)

            ch = 0
            for layer in range(DEPTH):
                T = lambda name: TILE[name, layer]
                pe.wait_ge(sem("xn_ready"), n.next("xn_ready"))
                norm_turns(T("n1"), xn)
                for i in range(4):
                    pe.wait_ge(psum_free(T("n1") + i), fills(T("n1") + i))
                tokens_out(T("q"), ch)
                tokens_out(T("k"), ch + 1)
                pe.wait_ge(chunk_full(ch + 2), full_at[ch + 2])
                b = claim(T("lr"))
                w = slot(ch + 2, KD, 16)
                for k in range(KD):
                    ins = mm(b[0:16, 0:SEQ], w[:, k, :], xT[:, k, NM:NTOK], start=(k == 0), stop=(k == KD - 1))
                ins.then_inc(psum_full(T("lr")), 1)
                b = claim(T("dt"))
                w = slot(ch + 2, KD, 8, KD * 16)
                for t in range(NT):
                    for k in range(KD):
                        ins = mm(b[:, 8 * t:8 * t + 8], xT[:, k, NM + P * t:NM + P * t + P], w[:, k, :], start=(k == 0), stop=(k == KD - 1))
                ins.then_inc(psum_full(T("dt")), 1)
                channels_out(T("xbc"), ch + 3, NM, SEQ, 2)
                channels_out(T("xbc") + 2, ch + 4, NM, SEQ, 2)
                pe.wait_ge(sem("qk_ready"), n.next("qk_ready"))
                for t in range(NT):
                    for j in range(2):
                        transposes(T("qkT") + 2 * t + j, tm[:, t, :], [512 * j + P * q for q in range(4)])
                tokens_out(T("v"), ch + 5)
                for i in range(4):
                    pe.wait_ge(psum_free(T("qkT") + i), fills(T("qkT") + i))
                for t in range(NT):
                    for comp in range(2):
                        for hp in range(2):
                            tile = T("sc") + 4 * t + 2 * comp + hp
                            b = claim(tile)
                            for j in range(2):
                                hh = 2 * hp + j
                                lo = 64 * comp
                                ins = mm(b[:, 256 * j:256 * j + P * (t + 1)], qkT[lo:lo + 64, 0, hh, P * t:P * t + P],
                                         qkT[lo:lo + 64, 1, hh, 0:P * (t + 1)], start=True, stop=True)
                            ins.then_inc(psum_full(tile), 1)
                channels_out(T("gqk"), ch + 6, NM, SEQ, 2)
                pe.wait_ge(sem("conv_ready"), n.next("conv_ready"))
                for i in range(3):
                    tile = T("xbT") + i
                    b = claim(tile)
                    for j in range(4 if i < 2 else 2):
                        src = cx[:, j, P * i:P * i + P] if i < 2 else cx[:, 4 + j, 0:P]
                        ins = nc.tensor.transpose(b[:, P * j:P * j + P], src, ident[:, :])
                    ins.then_inc(psum_full(tile), 1)
                tokens_out(T("z"), ch + 7)
                at = T("at")
                for t in range(NT):
                    pe.wait_ge(sem("attn_ready"), n.next("attn_ready"))
                    for kt in range(t + 1):
                        transposes(at + t + kt, attn.rearrange("p a b -> p (a b)"), [256 * q + P * kt for q in range(4)])
                    for kt in range(t + 1):
                        pe.wait_ge(psum_free(at + t + kt), fills(at + t + kt))
                    b = claim(T("pv") + t)
                    for hh in range(DA_H):
                        for kt in range(t + 1):
                            ins = mm(b[:, P * hh:P * hh + P], attnT[:, hh, kt, :], tm[:, kt, 1024 + P * hh:1024 + P * hh + P],
                                     start=(kt == 0), stop=(kt == t))
                    ins.then_inc(psum_full(T("pv") + t), 1)
                pe.wait_ge(sem("da_ready"), n.next("da_ready"))
                b = claim(T("cumc"))
                dA = s8[:, 2:4, 0:8]
                for t in range(NT):
                    mm(b[:, 16 * t:16 * t + 8], tri[:, :], dA[:, t, :], start=True, stop=True)
                    ins = mm(b[:, 16 * t + 8:16 * t + 16], ones[:, :], dA[:, t, :], start=True, stop=True)
                ins.then_inc(psum_full(T("cumc")), 1)
                for t in range(NT):
                    for q in range(2):
                        tile = T("cumb") + 2 * t + q
                        b = claim(tile)
                        for j in range(4):
                            hh = 4 * q + j
                            ins = mm(b[:, P * j:P * j + P], dA[:, t, hh:hh + 1].to_broadcast([P, P]), tri[:, :], start=True, stop=True)
                        ins.then_inc(psum_full(tile), 1)
                b = claim(T("cb"))
                for t in range(NT):
                    for gg in range(2):
                        o = P * (2 * t + gg)
                        ins = mm(b[:, o:o + P], cx[:, 4 + gg, P * t:P * t + P], cx[:, 6 + gg, P * t:P * t + P], start=True, stop=True)
                ins.then_inc(psum_full(T("cb")), 1)
                tokens_out(T("gv"), ch + 8)
                b = claim(T("gk"))
                if layer == 0:
                    pe.wait_ge(sem("bc_loaded"), 16 * 27)
                for j in range(2):
                    ins = mm(b[:, 256 * j:256 * j + 256], gw2[:, layer, P * j:P * j + P], lrT[0:GLA_RANK, :], start=True, stop=True)
                ins.then_inc(psum_full(T("gk")), 1)
                tokens_out(T("gg"), ch + 9)
                ch += 10
                pe.wait_ge(sem("ssd_ready"), n.next("ssd_ready"))
                for t in range(NT):
                    b = claim(T("yd") + t)
                    for hh in range(SSD_H):
                        ins = mm(b[:, 64 * hh:64 * hh + 64], decay[:, t, hh, :], xdt[:, t, 64 * hh:64 * hh + 64], start=True, stop=True)
                    ins.then_inc(psum_full(T("yd") + t), 1)
                b = claim(T("st"))
                xe = xdte.rearrange("p a b -> p (a b)")
                for gg in range(2):
                    ins = mm(b[:, 256 * gg:256 * gg + 256], B0[:, gg, :], xe[:, 256 * gg:256 * gg + 256], start=True, stop=True)
                ins.then_inc(psum_full(T("st")), 1)
                pe.wait_ge(psum_free(T("st")), fills(T("st")))
                b = claim(T("yo"))
                for gg in range(2):
                    ins = mm(b[:, 256 * gg:256 * gg + 256], cx[:, 6 + gg, P:2 * P], sst[:, gg, :], start=True, stop=True)
                ins.then_inc(psum_full(T("yo")), 1)
                pe.wait_ge(sem("gla_ready"), n.next("gla_ready"))
                b = claim(T("keT"))
                for t in range(NT):
                    for j in range(2):
                        o = P * (2 * t + j)
                        ins = nc.tensor.transpose(b[:, o:o + P], ke[:, j, P * t:P * t + P], ident[:, :])
                ins.then_inc(psum_full(T("keT")), 1)
                pe.wait_ge(psum_free(T("keT")), fills(T("keT")))
                for cc in range(3):
                    b = claim(T("gst") + cc)
                    for j in range(2):
                        ins = mm(b[:, 256 * j:256 * j + 256], kz[:, cc, P * j:P * j + P],
                                 tm[:, cc // 2, 2048 + 256 * j:2048 + 256 * j + 256], start=True, stop=True)
                    ins.then_inc(psum_full(T("gst") + cc), 1)
                for par in range(2):
                    b = claim(T("gat") + par)
                    lo = 64 * par
                    for t in range(NT):
                        for j in range(2):
                            o = P * (2 * t + j)
                            ins = mm(b[:, o:o + P], ki[lo:lo + 64, j, P * t:P * t + P], qd[lo:lo + 64, j, P * t:P * t + P], start=True, stop=True)
                    ins.then_inc(psum_full(T("gat") + par), 1)
                for par in range(2):
                    pe.wait_ge(psum_free(T("gat") + par), fills(T("gat") + par))
                pe.wait_ge(psum_free(T("gst") + 2), fills(T("gst") + 2))
                for t in range(NT):
                    b = claim(T("go") + t)
                    for j in range(2):
                        for half in range(2):
                            cc = 2 * t + half
                            mm(b[64 * half:64 * half + 64, 256 * j:256 * j + 256], qd[:, j, 64 * cc:64 * cc + 64], Sh[:, cc, j, :],
                               start=True, stop=False, skip_group_check=True)
                        for par in range(2):
                            o = P * (2 * j + par)
                            ins = mm(b[:, o:o + P], attm[:, t, 2 * j + par, :], tm[:, t, 2048 + o:2048 + o + P],
                                     start=False, stop=True, skip_group_check=True)
                    ins.then_inc(psum_full(T("go") + t), 1)
                pe.wait_ge(sem("mix_ready"), n.next("mix_ready"))
                for t in range(NT):
                    for q in range(3):
                        transposes(T("mixT") + 3 * t + q, mix[:, t, :], [512 * q + P * j for j in range(4)])
                for i in range(6):
                    pe.wait_ge(psum_free(T("mixT") + i), fills(T("mixT") + i))
                xcols = lambda k, t: xT[:, k, NM + P * t:NM + P * t + P]
                ch = rows_out(T("wo"), ch, KM, xcols)
                pe.wait_ge(sem("xn_ready"), n.next("xn_ready"))
                norm_turns(T("n2"), xn)
                for i in range(4):
                    pe.wait_ge(psum_free(T("n2") + i), fills(T("n2") + i))
                for f in range(KF):
                    if f % 2 == 0:
                        pe.wait_ge(chunk_full(ch + f // 2), full_at[ch + f // 2])
                    b = claim(T("ffn") + f)
                    for q in range(2):
                        w = slot(ch + f // 2, KD, 256, 2048 * q)
                        for k in range(KD):
                            ins = mm(b[:, 256 * q:256 * q + 256], w[:, k, P * (f % 2):P * (f % 2) + P], xT[:, k, NM:NTOK], start=(k == 0), stop=(k == KD - 1))
                    ins.then_inc(psum_full(T("ffn") + f), 1)
                ch += KF // 2
                for i in range(NPS):
                    pe.wait_ge(psum_free(T("ffn") + KF - NPS + i), fills(T("ffn") + KF - NPS + i))
                ch = rows_out(T("dn"), ch, KF, lambda k, t: hid[:, k, P * t:P * t + P]) + 1
                pe.wait_ge(sem("h_ready"), n.next("h_ready"))
                norm_turns(T("n3"), h)
                pe.wait_ge(sem("p_loaded"), 16 * (layer + 1))
                b = claim(T("pT"))
                for j in range(2):
                    for t in range(NT):
                        o = 256 * j + P * t
                        ins = nc.tensor.transpose(b[:, o:o + P], ptm[:, t, P * j:P * j + P], ident[:, :])
                ins.then_inc(psum_full(T("pT")), 1)
                for i in range(4):
                    pe.wait_ge(psum_free(T("n3") + i), fills(T("n3") + i))
                pe.wait_ge(psum_free(T("pT")), fills(T("pT")))
                ch = rows_out(T("pg"), ch, KD, xcols)
                ch = rows_out(T("pp"), ch, 2, lambda k, t: pT[:, k, P * t:P * t + P]) + 1

            pe.wait_ge(sem("xn_ready"), n.next("xn_ready"))
            norm_turns(TILE["m1"], xn)
            b = claim(TILE["mm"])
            for k in range(KD):
                ins = nc.tensor.transpose(b[:, NM * k:NM * k + NM], hmeta[0:NM, P * k:P * k + P], ident[0:NM, 0:NM])
            ins.then_inc(psum_full(TILE["mm"]), 1)
            for i in range(5):
                pe.wait_ge(psum_free(TILE["m1"] + i), fills(TILE["m1"] + i))
            channels_out(TILE["hf"], ch, 0, NTOK, 1)
            channels_out(TILE["hq"], ch + 1, NM, SEQ, 2)
            tokens_out(TILE["hi"], ch + 2)
            b = claim(TILE["hi"] + 2)
            w = slot(ch + 2, KD, 512)
            for k in range(KD):
                ins = mm(b[0:NM, :], xT[:, k, 0:NM], w[:, k, :], start=(k == 0), stop=(k == KD - 1))
            ins.then_inc(psum_full(TILE["hi"] + 2), 1)
            tokens_out(TILE["hog"], ch + 3)
            channels_out(TILE["lx"], ch + 4, 0, NTOK, 1)
            channels_out(TILE["lx"] + 4, ch + 5, 0, NTOK, 1)
            pe.wait_ge(sem("ke_ready"), n.next("ke_ready"))
            b = claim(TILE["hkm"])
            for hh in range(HG_H):
                ins = nc.tensor.transpose(b[0:NM, P * hh:P * hh + P], fT[:, hh, 0:NM], ident[:, :])
            ins.then_inc(psum_full(TILE["hkm"]), 1)
            b = claim(TILE["hk0"])
            for hh in range(HG_H):
                ins = nc.tensor.transpose(b[:, P * hh:P * hh + P], klev[:, hh, 0:P], ident[:, :])
            ins.then_inc(psum_full(TILE["hk0"]), 1)
            pe.wait_ge(psum_free(TILE["hkm"]), fills(TILE["hkm"]))
            pe.wait_ge(psum_free(TILE["hk0"]), fills(TILE["hk0"]))
            b = claim(TILE["hsm"])
            kem = wlev[0:NM, :, 0:P]
            for hh in range(HG_H):
                ins = mm(b[:, P * hh:P * hh + P], kem[:, hh, :], vt[0:NM, 2, P * hh:P * hh + P], start=True, stop=True)
            ins.then_inc(psum_full(TILE["hsm"]), 1)
            b = claim(TILE["hs0"])
            for hh in range(HG_H):
                ins = mm(b[:, P * hh:P * hh + P], ke0[:, hh, :], vt[:, 0, P * hh:P * hh + P], start=True, stop=True)
            ins.then_inc(psum_full(TILE["hs0"]), 1)
            unit_chunk = {u: ch + 6 + u // 2 for u in range(UNITS - 2)}
            unit_chunk.update({u: ch + 6 + UNITS // 2 - 1 + 2 for u in UNITS_LRU})
            ch += 6 + UNITS // 2 - 1

            def units_out(units):
                for u in units:
                    uc = unit_chunk[u]
                    pe.wait_ge(chunk_full(uc), full_at[uc])
                    b = claim(TILE["unit", u])
                    for m in range(2):
                        for k in range(KD):
                            ins = mm(b[:, 256 * m:256 * m + 256], slot(uc, KD, 512)[:, k, P * (2 * (u % 2) + m):P * (2 * (u % 2) + m) + P],
                                     xT[:, k, NM:NTOK], start=(k == 0), stop=(k == KD - 1))
                    ins.then_inc(psum_full(TILE["unit", u]), 1)

            for i in range(N_LEVELS):
                if i < len(LEVELS):
                    pe.wait_ge(sem("klev_ready"), n.next("klev_ready"))
                    pe.wait_ge(sem("qlev_ready"), n.next("qlev_ready"))
                    ka, qa = klev, qlev
                else:
                    ka, qa = kT[:, :, NM:NTOK], qT
                for t in range(NT):
                    tile = TILE["lev", i] + t
                    b = claim(tile)
                    for hh in range(HG_H):
                        ins = mm(b[:, P * hh:P * hh + P], ka[:, hh, P * t:P * t + P], qa[:, hh, P * t:P * t + P], start=True, stop=True)
                    ins.then_inc(psum_full(tile), 1)
                units_out(UNITS_AFTER[i])
            pe.wait_ge(sem("inter_ready"), n.next("inter_ready"))
            for t in range(NT):
                b = claim(TILE["ho"] + t)
                for hh in range(HG_H):
                    mm(b[:, P * hh:P * hh + P], qlev[:, hh, P * t:P * t + P], S[:, t, hh, :], start=True, stop=False)
                    ins = mm(b[:, P * hh:P * hh + P], acc[:, t, hh, :], vt[:, t, P * hh:P * hh + P], start=False, stop=True)
                ins.then_inc(psum_full(TILE["ho"] + t), 1)
            units_out(UNITS_NORM)
            pe.wait_ge(sem("oa_ready"), n.next("oa_ready"))
            for t in range(NT):
                transposes(TILE["oaT"] + t, oa[:, t, :], [P * j for j in range(4)])
            units_out(UNITS_CONV)
            pe.wait_ge(sem("xc_ready"), n.next("xc_ready"))
            pe.wait_ge(chunk_full(ch), full_at[ch])
            for i, name in enumerate(("lr_r", "lr_i")):
                w = slot(ch, LB, P, 1024 * i)
                for m in range(LB):
                    b = claim(TILE[name] + m)
                    mm(b[:, 0:NTOK], w[:, m, :], xc[:, m, :], start=True, stop=True).then_inc(psum_full(TILE[name] + m), 1)
            ch += 1
            for i in range(2):
                pe.wait_ge(psum_free(TILE["oaT"] + i), fills(TILE["oaT"] + i))
            pe.wait_ge(chunk_full(ch), full_at[ch])
            for m in range(KD):
                b = claim(TILE["ua"] + m // 2)
                o = 256 * (m % 2)
                for k in range(4):
                    ins = mm(b[:, o:o + 256], slot(ch, 4, D)[:, k, P * m:P * m + P], oaT[:, k, :], start=(k == 0), stop=(k == 3))
                if m % 2:
                    ins.then_inc(psum_full(TILE["ua"] + m // 2), 1)
            ch += 1
            units_out(UNITS_LRU)
            pe.wait_ge(sem("lru_ready"), n.next("lru_ready"))
            pe.wait_ge(chunk_full(ch + 1), full_at[ch + 1])
            pe.wait_ge(chunk_full(ch + 2), full_at[ch + 2])
            for m in range(KD):
                b = claim(TILE["ub"] + m // 2)
                o = 256 * (m % 2)
                for k in range(KD):
                    ins = mm(b[:, o:o + 256], slot(ch + 1 + k // 4, 4, D)[:, k % 4, P * m:P * m + P], th[:, k, NM:NTOK], start=(k == 0), stop=(k == KD - 1))
                if m % 2:
                    ins.then_inc(psum_full(TILE["ub"] + m // 2), 1)
            ch += 3
            pe.wait_ge(sem("merged_ready"), n.next("merged_ready"))
            ch = rows_out(TILE["wo2"], ch, KD, lambda k, t: mTt[:, k, P * t:P * t + P])
            pe.wait_ge(sem("xn_ready"), n.next("xn_ready"))
            norm_turns(TILE["m2"], xn)
            for i in range(4):
                pe.wait_ge(psum_free(TILE["m2"] + i), fills(TILE["m2"] + i))
            pe.wait_ge(sem("route_weights_loaded"), 16 * 6)
            pe.wait_ge(sem("late_rows_loaded"), 16 * 5)
            b = claim(TILE["rt"])
            for t in range(NT):
                for k in range(KD):
                    ins = mm(b[:, 64 * t:64 * t + NG + NE], xT[:, k, NM + P * t:NM + P * t + P], wrt[:, k, :], start=(k == 0), stop=(k == KD - 1))
            ins.then_inc(psum_full(TILE["rt"]), 1)
            assert ch == N_LOADS, (ch, N_LOADS)
            pe.wait_ge(sem("chosen_ready"), n.next("chosen_ready"))
            b = claim(TILE["rk"])
            mm(b[:, 0:NE], tri[:, :], chosen[:, 0, :], start=True, stop=True)
            mm(b[:, NE:2 * NE], tri[:, :], chosen[:, 1, :], start=True, stop=False)
            mm(b[:, NE:2 * NE], ones[:, :], chosen[:, 0, :], start=False, stop=True)
            mm(b[:, 2 * NE:3 * NE], ones[:, :], chosen[:, 0, :], start=True, stop=False)
            mm(b[:, 2 * NE:3 * NE], ones[:, :], chosen[:, 1, :], start=False, stop=True).then_inc(psum_full(TILE["rk"]), 1)
            for i in range(NPS):
                pe.wait_ge(psum_free(N_TILES - NPS + i), fills(N_TILES - NPS + i))

            def sum_up(start=False):
                for q in range(4):
                    t, half = divmod(q, 2)
                    ins = mm(psum[4 + q][:, :], pickT[:, P * t:P * t + P], yE[:, 512 * half:512 * half + 512],
                             start=start, stop=True, skip_group_check=True)
                return ins

            def pair(n):
                pe.wait_ge(sem("pick_ready"), n + 1)
                for q in range(2):
                    pe.wait_ge(pair_free(q), n * 2 + 2)
                    for c4 in range(4):
                        for t in range(NT):
                            ins = mm(psum[q][:, P * c4:P * c4 + P], xn[:, t, 512 * q + P * c4:512 * q + P * c4 + P], pick[:, t, :],
                                     start=(t == 0), stop=(t == NT - 1))
                    ins.then_inc(pair_full(q), 1)
                pe.wait_ge(pair_free(2), n * 2 + 2)
                sum_up()
                for t in range(NT):
                    ins = nc.tensor.transpose(psum[2][:, P * t:P * t + P], pickw[:, t, :], ident[:, :])
                ins.then_inc(pair_full(2), 1)
                for q in range(2):
                    pe.wait_ge(pair_free(q), n * 2 + 3)
                for e in range(2):
                    b = psum[3] if e == 0 else psum[0]
                    if e == 0:
                        pe.wait_ge(pair_free(3), n + 2)
                    for q in range(2):
                        pe.wait_ge(sem(f"expert_chunk{2 * e + q}"), n * 16 + 16)
                        w = expert_slot[2 * e + q].rearrange("p (k n) -> p k n", k=KD)
                        for m in range(KE):
                            o = (KE * q + m) * SL
                            for k in range(KD):
                                ins = mm(b[:, o:o + SL], w[:, k, P * m:P * m + P], xsE[:, k, SL * e:SL * e + SL], start=(k == 0), stop=(k == KD - 1))
                    ins.then_inc(pair_full(3 if e == 0 else 0), 1)
                pe.wait_ge(pair_free(2), n * 2 + 3)
                for e in range(2):
                    if e == 0:
                        pe.wait_ge(pair_free(3), n + 3)
                    else:
                        pe.wait_ge(pair_free(0), n * 2 + 4)
                    pe.wait_ge(sem(f"expert_chunk{4 + e}"), n * 16 + 16)
                    w = expert_slot[4 + e].rearrange("p (k n) -> p k n", k=KE)
                    for half in range(2):
                        for k in range(KE):
                            ins = mm(psum[1 + half][SL * e:SL * e + SL, :], hidE[:, e, k, :], w[:, k, 512 * half:512 * half + 512],
                                     start=(k == 0), stop=(k == KE - 1), skip_group_check=True)
                        if e:
                            ins.then_inc(pair_full(1 + half), 1)
                    if e == 0:
                        ins.then_inc(sem("down0_used"), 1)

            pe.wait_ge(sem("moe_zero"), 1)
            sum_up(start=True)
            pe.wait_ge(sem("passes_ready"), 1)
            n_passes = pe.value_load(passes[0:1, 0:1], min_val=1, max_val=MAX_PASSES)
            with pe.Fori(0, n_passes) as turn:
                with pe.Fori(0, PAIRS) as i:
                    pair(turn * PAIRS + i)
            for q in range(1, 3):
                pe.wait_ge(pair_free(q), n_passes * (2 * PAIRS) + 2)
            sum_up().then_inc(sem("sum_done"), 1)

        @block.scalar
        def _(act):
            n = Counts()

            def copy(dst, tile, src, func=ACT.Copy, **kw):
                act.wait_ge(psum_full(tile), fills(tile))
                act.activation(dst, src, func, **kw).then_inc(psum_free(tile), 1)

            for layer in range(DEPTH):
                r0 = ROWS1 * layer
                for name, key, cnt in (("an", "attn_norm", 8), ("fn", "ffn_norm", 8), ("cb", "ssd_conv_b", 8), ("gb", "gla_b_gate", 2)):
                    act.dma_start(prow1[r0 + CP1[name]:r0 + CP1[name] + cnt, :],
                                d[key][layer].rearrange("(c p) -> c p", p=P)).then_inc(sem("rows_loaded"), 16)
                act.dma_start(prow1[r0 + 16:r0 + 48, :],
                            d["ssd_conv_w"][layer].rearrange("j (c p) -> (j c) p", p=P)).then_inc(sem("rows_loaded"), 16)
            for name, key, cnt in (("n1", "norm1_g_2", 8), ("cb", "conv_b_2", 8), ("br", "lru_b_r_2", 8),
                                   ("bi", "lru_b_i_2", 8), ("lam", "lru_lambda_2", 8)):
                act.dma_start(prow2[CP2[name]:CP2[name] + cnt, :],
                            d[key][0].rearrange("(c p) -> c p", p=P)).then_inc(sem("rows_loaded"), 16)
            act.dma_start(prow2[16:48, :], d["conv_w_2"][0].rearrange("j (c p) -> (j c) p", p=P)).then_inc(sem("rows_loaded"), 16)
            act.dma_start(prow2[8:16, :], d["hg_lower_bounds_2"].rearrange("j (c p) -> (j c) p", p=P)).then_inc(sem("rows_loaded"), 16)
            act.dma_start(pos[:, :], d["positions"][0].rearrange("(t p) -> p t", p=P),
                        allow_slow_non_contiguous=True).then_inc(sem("bc_loaded"), 16)
            for layer in range(DEPTH):
                for name, key in (("gq", "da_q_norm"), ("gk", "da_k_norm"), ("lq1", "da_lambda_q1"), ("lk1", "da_lambda_k1"),
                                  ("lq2", "da_lambda_q2"), ("lk2", "da_lambda_k2"), ("gsub", "da_sub_norm"),
                                  ("dtb", "ssd_dt_bias"), ("alog", "ssd_a_log"), ("dsk", "ssd_d"), ("ssdn", "ssd_norm"),
                                  ("glan", "gla_norm")):
                    act.dma_start(bc1v(layer, name), d[key][layer].partition_broadcast(P)).then_inc(sem("bc_loaded"), 16)
                act.dma_start(gw2[:, layer, :], d["gla_w_gate2"][layer]).then_inc(sem("bc_loaded"), 16)
            act.dma_start(hmeta[0:NM, :], d["meta_tokens_2"]).then_inc(sem("route_weights_loaded"), 16)
            act.dma_start(wrt[:, :, 0:NG], d["w_group_2"][0].rearrange("(k p) n -> p k n", p=P),
                        allow_slow_non_contiguous=True).then_inc(sem("route_weights_loaded"), 16)
            for q in range(NG):
                act.dma_start(wrt[:, :, NG + EPG * q:NG + EPG * q + EPG], d["w_router_2"][0, q].rearrange("(k p) n -> p k n", p=P),
                            allow_slow_non_contiguous=True).then_inc(sem("route_weights_loaded"), 16)

            for i, (dst, r) in enumerate(((cp1, DEPTH * ROWS1), (cp2, 80))):
                copy(dst[:, :], i, psum[i][:, 0:r])
            for layer in range(DEPTH):
                T = lambda name: TILE[name, layer]

                def tokens(name, col, func=ACT.Copy):
                    for t in range(NT):
                        copy(tm[:, t, col:col + 512], T(name) + t, psum[(T(name) + t) % NPS][:, :], func)
                if layer:
                    act.wait_ge(sem("arena_free"), n.next("arena_free"))
                tokens("q", 0)
                tokens("k", 512)
                copy(lrT[0:GLA_RANK, :], T("lr"), psum[T("lr") % NPS][0:GLA_RANK, 0:SEQ])
                copy(s8[:, 0:2, 0:8], T("dt"), psum[T("dt") % NPS][:, 0:16].rearrange("p (t e) -> p t e", t=2))
                if layer == 0:
                    act.wait_ge(sem("angle_ready"), n.next("angle_ready"))
                    act.activation(sin[:, :, :], ang[:, :, :], ACT.Sin).then_inc(sem("sin_done"), 1)
                    act.activation(cos[:, :, :], ang[:, :, :], ACT.Sin, scale=0.5).then_inc(sem("sin_done"), 1)
                for i in range(4):
                    b = psum[(T("xbc") + i) % NPS]
                    copy(xbc[:, 2 * i:2 * i + 2, CONV - 1:], T("xbc") + i, b[:, :].rearrange("p (m t) -> p m t", m=2))
                act.wait_ge(sem("conv_sum"), n.next("conv_sum"))
                act.activation(cx[:, :, :], cx[:, :, :], ACT.Silu).then_inc(sem("conv_ready"), 1)
                act.wait_ge(sem("dt_ready"), n.next("dt_ready"))
                act.activation(s8[:, 6:8, 0:8], s8[:, 0:2, 0:8], ACT.Abs).then_inc(sem("act_step"), 1)
                act.wait_ge(sem("act_step"), n.next("act_step"))
                act.activation(s8[:, 6:8, 0:8], s8[:, 6:8, 0:8], ACT.Exp, scale=-1.0).then_inc(sem("act_step"), 1)
                act.wait_ge(sem("act_step"), n.next("act_step"))
                act.activation(s8[:, 6:8, 0:8], s8[:, 6:8, 0:8], ACT.Ln, bias=1.0).then_inc(sem("softplus_ln"), 1)
                act.activation(s8[:, 8, 0:8], bc1v(layer, "alog"), ACT.Exp).then_inc(sem("softplus_ln"), 1)
                act.wait_ge(sem("lam_dots"), n.next("lam_dots"))
                act.activation(s8[:, 4, 0:2], s8[:, 5, 0:2], ACT.Exp).then_inc(sem("lam_exp"), 1)
                tokens("v", 1024)
                for t in range(NT):
                    act.wait_ge(sem("scores_ready"), n.next("scores_ready"))
                    act.activation(sc[t], sc[t], ACT.Exp).then_inc(sem("exp_done"), 1)
                for i in range(2):
                    b = psum[(T("gqk") + i) % NPS]
                    copy(gqk[:, 2 * i:2 * i + 2, :], T("gqk") + i, b[:, :].rearrange("p (m t) -> p m t", m=2))
                tokens("z", 1536, ACT.Silu)
                act.wait_ge(sem("cum_ready"), n.next("cum_ready"))
                act.activation(s8[:, 13:15, 0:16], s8[:, 11:13, 0:16], ACT.Exp).then_inc(sem("cum_exp"), 1)
                for t in range(NT):
                    act.wait_ge(sem("seg_ready"), n.next("seg_ready"))
                    act.activation(decay[:, t], decay[:, t], ACT.Exp).then_inc(sem("decay_exp"), 1)
                tokens("gv", 2048)
                act.wait_ge(sem("gate_ready"), n.next("gate_ready"))
                act.activation(gtmp, gcum, ACT.Abs).then_inc(sem("act_step"), 1)
                act.wait_ge(sem("act_step"), n.next("act_step"))
                act.activation(gtmp, gtmp, ACT.Exp, scale=-1.0).then_inc(sem("act_step"), 1)
                act.wait_ge(sem("act_step"), n.next("act_step"))
                act.activation(gtmp, gtmp, ACT.Ln, bias=1.0).then_inc(sem("gate_ln"), 1)
                tokens("gg", 2560, ACT.Silu)
                copy(sst.rearrange("p a b -> p (a b)"), T("st"), psum[T("st") % NPS][:, :])
                act.wait_ge(sem("gcum_ready"), n.next("gcum_ready"))
                act.activation(eb, gcum, ACT.Exp)
                act.activation(enb, gcum, ACT.Exp, scale=-1.0)
                act.activation(ke, gtmp, ACT.Exp).then_inc(sem("gla_exp"), 1)
                for t in range(NT):
                    for q in range(3):
                        tile = T("mixT") + 3 * t + q
                        copy(xT[:, 4 * q:4 * q + 4, NM + P * t:NM + P * t + P], tile,
                             psum[tile % NPS][:, :].rearrange("p (j t) -> p j t", j=4))
                for f in range(KF):
                    tile = T("ffn") + f
                    act.wait_ge(psum_full(tile), fills(tile))
                    if f >= 2:
                        act.wait_ge(psum_free(tile - 2), fills(tile - 2))
                    act.activation(sil[:, f % 2, :], psum[tile % NPS][:, 0:SEQ], ACT.Silu).then_inc(sem("silu_done"), 1)
                for t in range(NT):
                    for half in range(2):
                        tile = T("n3") + 2 * t + half
                        copy(xT[:, 4 * half:4 * half + 4, NM + P * t:NM + P * t + P], tile,
                             psum[tile % NPS][:, :].rearrange("p (j t) -> p j t", j=4))
                copy(pT.rearrange("p a b -> p (a b)"), T("pT"), psum[T("pT") % NPS][:, :])
                for i in range(4):
                    copy(sg[:, i // 2, 512 * (i % 2):512 * (i % 2) + 512], T("pg") + i, psum[(T("pg") + i) % NPS][:, :], ACT.Sigmoid)

            act.wait_ge(sem("layer_done"), n.next("layer_done"))
            act.wait_ge(sem("layer_done"), n.next("layer_done"))
            for m in range(4):
                copy(fT[:, m, :], TILE["hf"] + m, psum[(TILE["hf"] + m) % NPS][:, 0:NTOK])
            act.wait_ge(psum_free(TILE["hf"] + 3), fills(TILE["hf"] + 3))
            act.activation(kT, fT, ACT.Sigmoid, scale=-1.0).then_inc(sem("act_step"), 1)
            act.wait_ge(sem("act_step"), n.next("act_step"))
            act.activation(fT, fT, ACT.Sigmoid).then_inc(sem("f_sig"), 1)
            act.wait_ge(sem("lbd_ready"), n.next("lbd_ready"))
            act.activation(s8[:, 17, 0:4], s8[:, 16, 0:4], ACT.Sigmoid).then_inc(sem("lb_sig"), 1)
            for i in range(2):
                copy(qT[:, 2 * i:2 * i + 2, :], TILE["hq"] + i, psum[(TILE["hq"] + i) % NPS][:, :].rearrange("p (m t) -> p m t", m=2))
            act.wait_ge(sem("f_ready"), n.next("f_ready"))
            act.activation(fT, fT, ACT.Ln).then_inc(sem("f_ln"), 1)
            for t in range(NT):
                copy(vt[:, t, :], TILE["hi"] + t, psum[(TILE["hi"] + t) % NPS][:, :])
            copy(vt[0:NM, 2, :], TILE["hi"] + 2, psum[(TILE["hi"] + 2) % NPS][0:NM, :])
            for t in range(NT):
                copy(og[:, t, :], TILE["hog"] + t, psum[(TILE["hog"] + t) % NPS][:, :], ACT.Sigmoid)
            act.wait_ge(sem("gend_ready"), n.next("gend_ready"))
            act.activation(fT[:, :, 0:NM], fT[:, :, 0:NM], ACT.Exp)
            act.activation(klev[:, :, 0:P], klev[:, :, 0:P], ACT.Exp).then_inc(sem("gend_exp"), 1)
            for m in range(KD):
                copy(lx[:, m, CONV - 1:], TILE["lx"] + m, psum[(TILE["lx"] + m) % NPS][:, 0:NTOK])
            copy(wlev[0:NM, :, 0:P], TILE["hkm"], psum[TILE["hkm"] % NPS][0:NM, :].rearrange("p (h d) -> p h d", h=4))
            copy(ke0, TILE["hk0"], psum[TILE["hk0"] % NPS][:, :].rearrange("p (h d) -> p h d", h=4))
            def copy_unit(u):
                dst, func = ((ly, ACT.Copy), (ga, ACT.Sigmoid), (gb, ACT.Sigmoid))[u // 4]
                copy(dst[:, 2 * (u % 4):2 * (u % 4) + 2, :], TILE["unit", u],
                     psum[TILE["unit", u] % NPS][:, :].rearrange("p (m t) -> p m t", m=2), func)

            for i in range(N_LEVELS):
                if i < len(LEVELS):
                    act.wait_ge(sem("diff_ready"), n.next("diff_ready"))
                    act.activation(wlev, wlev, ACT.Abs).then_inc(sem("act_step"), 1)
                    act.wait_ge(sem("act_step"), n.next("act_step"))
                    act.activation(wlev, wlev, ACT.Exp, scale=-1.0).then_inc(sem("w_ready"), 1)
                for u in UNITS_AFTER[i - 1] if i else ():
                    copy_unit(u)
            for u in UNITS_AFTER[-1] + UNITS_NORM + UNITS_CONV:
                if u == UNITS_NORM[0]:
                    act.wait_ge(sem("qexp_asked"), n.next("qexp_asked"))
                    act.activation(wlev, G, ACT.Exp).then_inc(sem("qexp_done"), 1)
                copy_unit(u)
            act.wait_ge(sem("xc_ready"), n.next("xc_ready"))
            for name, dst, o in (("lr_r", ra, CP2["br"]), ("lr_i", iu, CP2["bi"])):
                for m in range(LB):
                    copy(dst[:, m, :], TILE[name] + m, psum[(TILE[name] + m) % NPS][:, 0:NTOK], ACT.Sigmoid, bias=cp2[:, o + m:o + m + 1])
            act.wait_ge(sem("lam_ready"), n.next("lam_ready"))
            act.activation(s8[:, 20, 0:8], cp2[:, 72:80], ACT.Abs).then_inc(sem("act_step"), 1)
            act.wait_ge(sem("act_step"), n.next("act_step"))
            act.activation(s8[:, 20, 0:8], s8[:, 20, 0:8], ACT.Exp, scale=-1.0).then_inc(sem("act_step"), 1)
            act.wait_ge(sem("act_step"), n.next("act_step"))
            act.activation(s8[:, 20, 0:8], s8[:, 20, 0:8], ACT.Ln, bias=1.0).then_inc(sem("lam_ln"), 1)
            act.wait_ge(sem("loga_ready"), n.next("loga_ready"))
            act.activation(th, ra, ACT.Tanh, scale=-1.0).then_inc(sem("act_step"), 1)
            act.wait_ge(sem("act_step"), n.next("act_step"))
            act.activation(ra, ra, ACT.Exp).then_inc(sem("a_ready"), 1)
            act.wait_ge(sem("gelu_asked"), n.next("gelu_asked"))
            act.activation(iu[:, :, NM:], iu[:, :, NM:], ACT.Tanh, scale=math.sqrt(2 / math.pi)).then_inc(sem("gelu_tanh"), 1)
            act.wait_ge(sem("sq_ready"), n.next("sq_ready"))
            act.activation(th, th, ACT.Sqrt).then_inc(sem("sq_done"), 1)
            for u in UNITS_LRU:
                copy_unit(u)
            act.wait_ge(sem("route_exp_asked"), n.next("route_exp_asked"))
            act.activation(s8[:, 2:4, 0:NG], s8[:, 2:4, 0:NG], ACT.Exp)
            act.activation(s8[:, 4, 0:2], s8[:, 4, 0:2], ACT.Exp).then_inc(sem("route_exp"), 1)

            act.wait_ge(sem("passes_ready"), 1)
            n_passes = act.value_load(passes[0:1, 0:1], min_val=1, max_val=MAX_PASSES)
            with act.Fori(0, n_passes) as turn:
                with act.Fori(0, PAIRS) as i:
                    n_ = turn * PAIRS + i
                    act.wait_ge(pair_full(1), n_ * 2 + 1)
                    act.activation(xsE[:, 4:8, :], psum[1][:, :].rearrange("p (k n) -> p k n", k=4), ACT.Copy).then_inc(pair_free(1), 1)
                    act.wait_ge(pair_full(3), n_ + 1)
                    act.activation(silE[:, 0, :], psum[3][:, 0:KE * SL], ACT.Silu).then_inc(sem("expert_silu"), 1)
                    act.wait_ge(pair_full(0), n_ * 2 + 2)
                    act.activation(silE[:, 1, :], psum[0][:, 0:KE * SL], ACT.Silu).then_inc(sem("expert_silu"), 1)
                    act.wait_ge(pair_full(1), n_ * 2 + 2)
                    act.activation(yE[:, 0:512], psum[1][:, :], ACT.Copy).then_inc(pair_free(1), 1)
                    act.wait_ge(pair_full(2), n_ * 2 + 2)
                    act.activation(yE[:, 512:D], psum[2][:, :], ACT.Copy).then_inc(pair_free(2), 1)

        @block.vector
        def _(v):
            n = Counts()
            TT, TS, STT = nc.vector.tensor_tensor, nc.vector.tensor_scalar, nc.vector.scalar_tensor_tensor

            def bank(tile):
                return psum[tile % NPS]

            def rsqrt(cols, width):
                TS(st1[:, 0:cols], st1[:, 0:cols], 1.0 / width, EPS, ALU.mult, ALU.add).then_inc(sem("power_asked"), 1)
                v.wait_ge(sem("power_done"), n.next("power_done"))

            def norm_rows(layer_gain=None, gain_row=None, meta=False):
                for t in range(NT):
                    nc.vector.tensor_tensor_reduce(out=xn[:, t, :], in0=h[:, t, :], in1=h[:, t, :], scale=1.0, scalar=0.0,
                                                        op0=ALU.mult, op1=ALU.add, accum_out=st1[:, t:t + 1]).then_inc(sem("dve_step"), 1)
                    v.wait_ge(sem("dve_step"), n.next("dve_step"))
                if meta:
                    v.memset(st1[:, 2:3], 1.0).then_inc(sem("dve_step"), 1)
                    v.wait_ge(sem("dve_step"), n.next("dve_step"))
                    nc.vector.tensor_tensor_reduce(out=mflat[0:NM, 0:D], in0=hmeta[0:NM, :], in1=hmeta[0:NM, :], scale=1.0, scalar=0.0,
                                                        op0=ALU.mult, op1=ALU.add, accum_out=st1[0:NM, 2:3]).then_inc(sem("dve_step"), 1)
                    v.wait_ge(sem("dve_step"), n.next("dve_step"))
                rsqrt(3 if meta else 2, D)
                if meta:
                    TS(hmeta[0:NM, :], hmeta[0:NM, :], st2[0:NM, 2:3], None, ALU.mult).then_inc(sem("dve_step"), 1)
                    v.wait_ge(sem("dve_step"), n.next("dve_step"))
                for t in range(NT):
                    ins = TS(xn[:, t, :], h[:, t, :], st2[:, t:t + 1], None, ALU.mult)
                    if gain_row is not None:
                        ins.then_inc(sem("dve_step"), 1)
                        v.wait_ge(sem("dve_step"), n.next("dve_step"))
                        ins = TT(xn[:, t, :], xn[:, t, :], gain_row, ALU.mult)
                    if t == NT - 1:
                        ins.then_inc(sem("xn_ready"), 1)
                    else:
                        ins.then_inc(sem("dve_step"), 1)
                        v.wait_ge(sem("dve_step"), n.next("dve_step"))

            def norm_evac(tile, gain):
                for t in range(NT):
                    for half in range(2):
                        k = tile + 2 * t + half
                        v.wait_ge(psum_full(k), fills(k))
                        src = bank(k)[:, :].rearrange("p (j t) -> p j t", j=4)
                        dst = xT[:, 4 * half:4 * half + 4, NM + P * t:NM + P * t + P]
                        if gain is None:
                            nc.vector.tensor_copy(dst, src).then_inc(psum_free(k), 1)
                        else:
                            TT(dst, src, gain[:, 4 * half:4 * half + 4].unsqueeze(2).to_broadcast([P, 4, P]), ALU.mult).then_inc(psum_free(k), 1)

            def add_rows(tile):
                for i in range(4):
                    k = tile + i
                    dst = h[:, i // 2, 512 * (i % 2):512 * (i % 2) + 512]
                    v.wait_ge(psum_full(k), fills(k))
                    TT(dst, dst, bank(k)[:, :], ALU.add).then_inc(psum_free(k), 1)
                    v.wait_ge(psum_free(k), fills(k))

            v.wait_ge(sem("x_loaded"), 16)
            v.wait_ge(psum_free(0), fills(0))
            v.wait_ge(psum_free(1), fills(1))

            for layer in range(DEPTH):
                T = lambda name: TILE[name, layer]
                cpl = cp1[:, ROWS1 * layer:ROWS1 * layer + ROWS1]
                norm_rows()
                norm_evac(T("n1"), cpl[:, 0:8])
                if layer == 0:
                    v.wait_ge(sem("iotas"), n.next("iotas", 3))
                    TT(xi[:, :], xi[:, :], xs_[:, :], ALU.bitwise_xor).then_inc(sem("dve_step"), 1)
                    v.wait_ge(sem("dve_step"), n.next("dve_step"))
                    nc.vector.tensor_copy(xf[:, :], xi[:, :]).then_inc(sem("dve_step"), 1)
                    v.wait_ge(sem("dve_step"), n.next("dve_step"))
                    v.wait_ge(sem("masks"), 4)
                    TT(xf[:, :], xf[:, :], tri[:, :], ALU.mult).then_inc(sem("dve_step"), 1)
                    v.wait_ge(sem("dve_step"), n.next("dve_step"))
                    for i, b in enumerate(LEVELS):
                        TS(lev[:, i, :], xf[:, :], float(b), None, ALU.is_ge).then_inc(sem("dve_step"), 1)
                        v.wait_ge(sem("dve_step"), n.next("dve_step"))
                        STT(lev[:, i, :], xf[:, :], float(2 * b), lev[:, i, :], ALU.is_lt, ALU.mult).then_inc(sem("dve_step"), 1)
                        v.wait_ge(sem("dve_step"), n.next("dve_step"))
                    nc.vector.tensor_copy(lev[:, 7, :], ident[:, :]).then_inc(sem("dve_step"), 1)
                    v.wait_ge(sem("dve_step"), n.next("dve_step"))
                    v.wait_ge(sem("bc_loaded"), 16 * 27)
                    v.wait_ge(sem("consts"), 1)
                    nc.vector.tensor_copy(posf[:, :], pos[:, :]).then_inc(sem("dve_step"), 1)
                    v.wait_ge(sem("dve_step"), n.next("dve_step"))
                    TT(ang[:, :, :], posf[:, :].unsqueeze(2).to_broadcast([P, NT, 8]), frq[:, :].unsqueeze(1).to_broadcast([P, NT, 8]), ALU.mult).then_inc(sem("dve_step"), 1)
                    v.wait_ge(sem("dve_step"), n.next("dve_step"))
                    TS(angk[:, :, :], ang[:, :, :], 1.0 / (2 * math.pi), None, ALU.mult).then_inc(sem("dve_step"), 1)
                    v.wait_ge(sem("dve_step"), n.next("dve_step"))
                    TS(angk[:, :, :], angk[:, :, :], 12582912.0, None, ALU.add).then_inc(sem("dve_step"), 1)
                    v.wait_ge(sem("dve_step"), n.next("dve_step"))
                    TS(angk[:, :, :], angk[:, :, :], 12582912.0, None, ALU.subtract).then_inc(sem("dve_step"), 1)
                    v.wait_ge(sem("dve_step"), n.next("dve_step"))
                    for part in (6.28125, 0.0019350051879882812, 3.0199158e-07):
                        STT(ang[:, :, :], angk[:, :, :], -part, ang[:, :, :], ALU.mult, ALU.add).then_inc(sem("dve_step"), 1)
                        v.wait_ge(sem("dve_step"), n.next("dve_step"))
                    TS(ang[:, :, :], ang[:, :, :], 3.1415925, -3.1415925, ALU.min, ALU.max).then_inc(sem("angle_ready"), 1)
                    v.wait_ge(sem("sin_done"), n.next("sin_done", 2))
                    TT(cos[:, :, :], cos[:, :, :], cos[:, :, :], ALU.mult).then_inc(sem("dve_step"), 1)
                    v.wait_ge(sem("dve_step"), n.next("dve_step"))
                    TS(cos[:, :, :], cos[:, :, :], -2.0, 1.0, ALU.mult, ALU.add).then_inc(sem("dve_step"), 1)
                    v.wait_ge(sem("dve_step"), n.next("dve_step"))
                for i in range(2):
                    v.wait_ge(psum_free(T("q") + i), fills(T("q") + i))
                    v.wait_ge(psum_free(T("k") + i), fills(T("k") + i))
                qk = [tm[:, t, 0:1024].rearrange("p (h d) -> p h d", d=DQK) for t in range(NT)]
                for t in range(NT):
                    TT(xn[:, t, :], tm[:, t, 0:1024], tm[:, t, 0:1024], ALU.mult).then_inc(sem("dve_step"), 1)
                    v.wait_ge(sem("dve_step"), n.next("dve_step"))
                    nc.vector.reduce_sum(st1[:, 16 * t:16 * t + 16], xn[:, t, :].rearrange("p (h d) -> p h d", d=DQK), axis=AX.X).then_inc(sem("dve_step"), 1)
                    v.wait_ge(sem("dve_step"), n.next("dve_step"))
                rsqrt(32, DQK)
                for t in range(NT):
                    TT(qk[t], qk[t], st2[:, 16 * t:16 * t + 16].unsqueeze(2).to_broadcast([P, 16, DQK]), ALU.mult).then_inc(sem("dve_step"), 1)
                    v.wait_ge(sem("dve_step"), n.next("dve_step"))
                    for i, name in enumerate(("gq", "gk")):
                        TT(qk[t][:, 8 * i:8 * i + 8, :], qk[t][:, 8 * i:8 * i + 8, :],
                                bc1v(layer, name).unsqueeze(1).to_broadcast([P, 8, DQK]), ALU.mult).then_inc(sem("dve_step"), 1)
                        v.wait_ge(sem("dve_step"), n.next("dve_step"))
                    x1, x2 = qk[t][:, :, 0:8], qk[t][:, :, 8:16]
                    c_ = cos[:, t, :].unsqueeze(1).to_broadcast([P, 16, 8])
                    s_ = sin[:, t, :].unsqueeze(1).to_broadcast([P, 16, 8])
                    r = [xn[:, t, 128 * i:128 * i + 128].rearrange("p (h d) -> p h d", d=8) for i in range(4)]
                    TT(r[0], x1, c_, ALU.mult).then_inc(sem("dve_step"), 1)
                    v.wait_ge(sem("dve_step"), n.next("dve_step"))
                    TT(r[1], x2, s_, ALU.mult).then_inc(sem("dve_step"), 1)
                    v.wait_ge(sem("dve_step"), n.next("dve_step"))
                    TT(r[2], x2, c_, ALU.mult).then_inc(sem("dve_step"), 1)
                    v.wait_ge(sem("dve_step"), n.next("dve_step"))
                    TT(r[3], x1, s_, ALU.mult).then_inc(sem("dve_step"), 1)
                    v.wait_ge(sem("dve_step"), n.next("dve_step"))
                    TT(x1, r[0], r[1], ALU.subtract).then_inc(sem("dve_step"), 1)
                    v.wait_ge(sem("dve_step"), n.next("dve_step"))
                    ins = TT(x2, r[2], r[3], ALU.add)
                    if t:
                        ins.then_inc(sem("qk_ready"), 1)
                        v.wait_ge(sem("qk_ready"), n.next("qk_ready"))
                    else:
                        ins.then_inc(sem("dve_step"), 1)
                        v.wait_ge(sem("dve_step"), n.next("dve_step"))
                for t in range(NT):
                    for j in range(2):
                        k = T("qkT") + 2 * t + j
                        v.wait_ge(psum_full(k), fills(k))
                        nc.vector.tensor_copy(qkT[:, j, :, P * t:P * t + P], bank(k)[:, :].rearrange("p (h t) -> p h t", h=4)).then_inc(psum_free(k), 1)
                for i in range(4):
                    v.wait_ge(psum_free(T("xbc") + i), fills(T("xbc") + i))
                v.wait_ge(sem("zeros"), n.next("zeros"))
                for m in range(KD):
                    TS(cx[:, m, :], xbc[:, m, 0:SEQ], cpl[:, 16 + m:17 + m], cpl[:, 48 + m:49 + m], ALU.mult, ALU.add).then_inc(sem("dve_step"), 1)
                    v.wait_ge(sem("dve_step"), n.next("dve_step"))
                    for j in range(1, CONV):
                        STT(cx[:, m, :], xbc[:, m, j:j + SEQ], cpl[:, 16 + 8 * j + m:17 + 8 * j + m], cx[:, m, :], ALU.mult, ALU.add).then_inc(sem("dve_step"), 1)
                        v.wait_ge(sem("dve_step"), n.next("dve_step"))
                v.sem_inc(sem("conv_sum"), 1)
                v.wait_ge(psum_free(T("dt")), fills(T("dt")))
                dtr = s8[:, 0:2, 0:8]
                dtb = bc1v(layer, "dtb").unsqueeze(1).to_broadcast([P, NT, 8])
                TT(dtr, dtr, dtb, ALU.add).then_inc(sem("dt_ready"), 1)
                v.wait_ge(sem("dt_ready"), n.next("dt_ready"))
                for i in range(2):
                    nc.vector.tensor_tensor_reduce(out=s8[:, 9:11, :].rearrange("p a b -> p (a b)"), in0=bc1v(layer, f"lq{i + 1}"),
                                                        in1=bc1v(layer, f"lk{i + 1}"), scale=1.0, scalar=0.0, op0=ALU.mult,
                                                        op1=ALU.add, accum_out=s8[:, 5, i:i + 1]).then_inc(sem("dve_step"), 1)
                    v.wait_ge(sem("dve_step"), n.next("dve_step"))
                v.sem_inc(sem("lam_dots"), 1)
                v.wait_ge(sem("lam_exp"), n.next("lam_exp"))
                lam = s8[:, 4, 2:3]
                TT(lam, s8[:, 4, 0:1], s8[:, 4, 1:2], ALU.subtract).then_inc(sem("dve_step"), 1)
                v.wait_ge(sem("dve_step"), n.next("dve_step"))
                TS(lam, lam, lambda_init(layer), None, ALU.add).then_inc(sem("dve_step"), 1)
                v.wait_ge(sem("dve_step"), n.next("dve_step"))
                v.wait_ge(sem("softplus_ln"), n.next("softplus_ln", 2))
                TS(dtr, dtr, 0.0, None, ALU.max).then_inc(sem("dve_step"), 1)
                v.wait_ge(sem("dve_step"), n.next("dve_step"))
                TT(dtr, dtr, s8[:, 6:8, 0:8], ALU.add).then_inc(sem("dve_step"), 1)
                v.wait_ge(sem("dve_step"), n.next("dve_step"))
                dA = s8[:, 2:4, 0:8]
                STT(dA, dtr, -1.0, s8[:, 8, 0:8].unsqueeze(1).to_broadcast([P, NT, 8]), ALU.mult, ALU.mult).then_inc(sem("dve_step"), 1)
                v.wait_ge(sem("dve_step"), n.next("dve_step"))
                v.sem_inc(sem("da_ready"), 1)
                for t in range(NT):
                    o = P * t
                    for i in range(4):
                        k = T("sc") + 4 * t + i
                        v.wait_ge(psum_full(k), fills(k))
                        src = bank(k)[:, :].rearrange("p (j t) -> p j t", j=2)
                        dst = sc[t][:, 2 * i:2 * i + 2, :]
                        if t:
                            TS(dst[:, :, 0:P], src[:, :, 0:P], DQK ** -0.5, None, ALU.mult).then_inc(sem("dve_step"), 1)
                            v.wait_ge(sem("dve_step"), n.next("dve_step"))
                        STT(dst[:, :, o:o + P], src[:, :, o:o + P], DQK ** -0.5,
                            neg[:, :].unsqueeze(1).to_broadcast([P, 2, P]), ALU.mult, ALU.add).then_inc(psum_free(k), 1)
                        v.wait_ge(psum_free(k), fills(k))
                    nc.vector.reduce_max(s8[:, 9, 0:8], sc[t], axis=AX.X).then_inc(sem("dve_step"), 1)
                    v.wait_ge(sem("dve_step"), n.next("dve_step"))
                    TT(sc[t], sc[t], s8[:, 9, 0:8].unsqueeze(2).to_broadcast([P, 8, o + P]), ALU.subtract).then_inc(sem("scores_ready"), 1)
                for i in range(3):
                    k = T("xbT") + i
                    v.wait_ge(psum_full(k), fills(k))
                    if i < 2:
                        nc.vector.tensor_copy(xh[:, i, :], bank(k)[:, :]).then_inc(psum_free(k), 1)
                        v.wait_ge(psum_free(k), fills(k))
                    else:
                        nc.vector.tensor_copy(B0.rearrange("p a b -> p (a b)"), bank(k)[:, 0:256]).then_inc(psum_free(k), 1)
                        v.wait_ge(psum_free(k), fills(k))
                for t in range(NT):
                    nk = P * (t + 1)
                    s_ = sc[t]
                    v.wait_ge(sem("exp_done"), n.next("exp_done"))
                    nc.vector.reduce_sum(s8[:, 10, 0:8], s_, axis=AX.X).then_inc(sem("dve_step"), 1)
                    v.wait_ge(sem("dve_step"), n.next("dve_step"))
                    nc.vector.reciprocal(s8[:, 10, 0:8], s8[:, 10, 0:8]).then_inc(sem("dve_step"), 1)
                    v.wait_ge(sem("dve_step"), n.next("dve_step"))
                    TS(s8[:, 10, 4:8], s8[:, 10, 4:8], lam, None, ALU.mult).then_inc(sem("dve_step"), 1)
                    v.wait_ge(sem("dve_step"), n.next("dve_step"))
                    TT(s_, s_, s8[:, 10, 0:8].unsqueeze(2).to_broadcast([P, 8, nk]), ALU.mult).then_inc(sem("dve_step"), 1)
                    v.wait_ge(sem("dve_step"), n.next("dve_step"))
                    TT(attn[:, :, 0:nk], s_[:, 0:4, :], s_[:, 4:8, :], ALU.subtract).then_inc(sem("attn_ready"), 1)
                    v.wait_ge(sem("attn_ready"), n.next("attn_ready"))
                    for kt in range(t + 1):
                        k = T("at") + t + kt
                        v.wait_ge(psum_full(k), fills(k))
                        nc.vector.tensor_copy(attnT[:, :, kt, :], bank(k)[:, :].rearrange("p (h q) -> p h q", h=4)).then_inc(psum_free(k), 1)
                    k = T("pv") + t
                    v.wait_ge(psum_full(k), fills(k))
                    nc.vector.tensor_copy(mix[:, t, 0:512], bank(k)[:, :]).then_inc(psum_free(k), 1)
                    v.wait_ge(psum_free(k), fills(k))

                def head_norm(dst_t, heads, width, gain, factor):
                    per = heads // NT
                    for t in range(NT):
                        dd = dst_t(t)
                        sq = xn[:, t, 0:per * width]
                        TT(sq, dd, dd, ALU.mult).then_inc(sem("dve_step"), 1)
                        v.wait_ge(sem("dve_step"), n.next("dve_step"))
                        nc.vector.reduce_sum(st1[:, per * t:per * t + per], sq.rearrange("p (h d) -> p h d", d=width), axis=AX.X).then_inc(sem("dve_step"), 1)
                        v.wait_ge(sem("dve_step"), n.next("dve_step"))
                    rsqrt(heads, width)
                    for t in range(NT):
                        dd = dst_t(t).rearrange("p (h d) -> p h d", d=width)
                        TT(dd, dd, st2[:, per * t:per * t + per].unsqueeze(2).to_broadcast([P, per, width]), ALU.mult).then_inc(sem("dve_step"), 1)
                        v.wait_ge(sem("dve_step"), n.next("dve_step"))
                        STT(dd, dd, factor, gain, ALU.mult, ALU.mult).then_inc(sem("dve_step"), 1)
                        v.wait_ge(sem("dve_step"), n.next("dve_step"))

                k = T("cumc")
                v.wait_ge(psum_full(k), fills(k))
                nc.vector.tensor_copy(s8[:, 11:13, 0:8], bank(k)[:, 0:32].rearrange("p (t e) -> p t e", t=2)[:, :, 0:8]).then_inc(sem("dve_step"), 1)
                v.wait_ge(sem("dve_step"), n.next("dve_step"))
                TT(s8[:, 11:13, 8:16], bank(k)[:, 0:32].rearrange("p (t e) -> p t e", t=2)[:, :, 8:16], s8[:, 11:13, 0:8], ALU.subtract).then_inc(psum_free(k), 1)
                v.wait_ge(psum_free(k), fills(k))
                v.sem_inc(sem("cum_ready"), 1)
                for t in range(NT):
                    for q in range(2):
                        k = T("cumb") + 2 * t + q
                        v.wait_ge(psum_full(k), fills(k))
                        for j in range(4):
                            hh = 4 * q + j
                            ins = TS(decay[:, t, hh, :], bank(k)[:, P * j:P * j + P], s8[:, 11 + t, hh:hh + 1], 0.0, ALU.subtract, ALU.min)
                            if j < 3:
                                ins.then_inc(sem("dve_step"), 1)
                                v.wait_ge(sem("dve_step"), n.next("dve_step"))
                        ins.then_inc(psum_free(k), 1)
                        v.wait_ge(psum_free(k), fills(k))
                    v.sem_inc(sem("seg_ready"), 1)
                k = T("cb")
                v.wait_ge(psum_full(k), fills(k))
                TT(cbm, bank(k)[:, :].rearrange("p (a b) -> p a b", a=4), tri[:, :].unsqueeze(1).to_broadcast([P, 4, P]), ALU.mult).then_inc(psum_free(k), 1)
                v.wait_ge(psum_free(k), fills(k))
                v.wait_ge(sem("cum_exp"), n.next("cum_exp"))
                for t in range(NT):
                    x3 = xh[:, t, :].rearrange("p (h d) -> p h d", d=SSD_P)
                    TT(xdt[:, t, :].rearrange("p (h d) -> p h d", d=SSD_P), x3, s8[:, t, 0:8].unsqueeze(2).to_broadcast([P, 8, SSD_P]), ALU.mult).then_inc(sem("dve_step"), 1)
                    v.wait_ge(sem("dve_step"), n.next("dve_step"))
                TT(xdte.rearrange("p a (b d) -> p (a b) d", d=SSD_P), xdt[:, 0, :].rearrange("p (h d) -> p h d", d=SSD_P),
                        s8[:, 13, 8:16].unsqueeze(2).to_broadcast([P, 8, SSD_P]), ALU.mult).then_inc(sem("dve_step"), 1)
                v.wait_ge(sem("dve_step"), n.next("dve_step"))
                v.wait_ge(sem("decay_exp"), n.next("decay_exp", 2))
                for t in range(NT):
                    for gg in range(2):
                        dd = decay[:, t, 4 * gg:4 * gg + 4, :]
                        TT(dd, dd, cbm[:, 2 * t + gg, :].unsqueeze(1).to_broadcast([P, 4, P]), ALU.mult).then_inc(sem("dve_step"), 1)
                        v.wait_ge(sem("dve_step"), n.next("dve_step"))
                v.sem_inc(sem("ssd_ready"), 1)
                head_norm(lambda t: mix[:, t, 0:512], 8, DV, bc1v(layer, "gsub").unsqueeze(1).to_broadcast([P, 4, DV]), 1.0 - lambda_init(layer))
                k = T("gk")
                v.wait_ge(psum_full(k), fills(k))
                TS(gcum[:, 0, :], bank(k)[:, 0:256], cpl[:, 56:57], None, ALU.add).then_inc(sem("dve_step"), 1)
                v.wait_ge(sem("dve_step"), n.next("dve_step"))
                TS(gcum[:, 1, :], bank(k)[:, 256:512], cpl[:, 57:58], None, ALU.add).then_inc(psum_free(k), 1)
                v.wait_ge(psum_free(k), fills(k))
                v.sem_inc(sem("gate_ready"), 1)
                v.wait_ge(sem("gate_ln"), n.next("gate_ln"))
                STT(gtmp, gcum, 0.0, gtmp, ALU.min, ALU.subtract).then_inc(sem("dve_step"), 1)
                v.wait_ge(sem("dve_step"), n.next("dve_step"))
                TS(gtmp, gtmp, 1.0 / 16.0, None, ALU.mult).then_inc(sem("dve_step"), 1)
                v.wait_ge(sem("dve_step"), n.next("dve_step"))
                one = ones[:, 0:GLA_C]
                for j in range(2):
                    for cc in range(4):
                        o = GLA_C * cc
                        nc.vector.tensor_tensor_scan(gcum[:, j, o:o + GLA_C], one, gtmp[:, j, o:o + GLA_C], 0.0, ALU.mult, ALU.add).then_inc(sem("dve_step"), 1)
                        v.wait_ge(sem("dve_step"), n.next("dve_step"))
                c3 = gcum.rearrange("p j (c t) -> p (j c) t", t=GLA_C)
                TT(gtmp.rearrange("p j (c t) -> p (j c) t", t=GLA_C), c3[:, :, GLA_C - 1:GLA_C].to_broadcast([P, 8, GLA_C]), c3, ALU.subtract).then_inc(sem("dve_step"), 1)
                v.wait_ge(sem("dve_step"), n.next("dve_step"))
                v.sem_inc(sem("gcum_ready"), 1)
                for t in range(NT):
                    y = mix[:, t, 512:1024]
                    y3 = y.rearrange("p (h d) -> p h d", d=SSD_P)
                    x3 = xh[:, t, :].rearrange("p (h d) -> p h d", d=SSD_P)
                    TT(y3, x3, bc1v(layer, "dsk").unsqueeze(2).to_broadcast([P, 8, SSD_P]), ALU.mult).then_inc(sem("dve_step"), 1)
                    v.wait_ge(sem("dve_step"), n.next("dve_step"))
                    k = T("yd") + t
                    v.wait_ge(psum_full(k), fills(k))
                    TT(y, y, bank(k)[:, :], ALU.add).then_inc(psum_free(k), 1)
                    v.wait_ge(psum_free(k), fills(k))
                k = T("yo")
                v.wait_ge(psum_full(k), fills(k))
                TT(xdt[:, 1, :].rearrange("p (h d) -> p h d", d=SSD_P), bank(k)[:, :].rearrange("p (h d) -> p h d", d=SSD_P),
                           s8[:, 14, 0:8].unsqueeze(2).to_broadcast([P, 8, SSD_P]), ALU.mult).then_inc(psum_free(k), 1)
                v.wait_ge(psum_free(k), fills(k))
                TT(mix[:, 1, 512:1024], mix[:, 1, 512:1024], xdt[:, 1, :], ALU.add).then_inc(sem("dve_step"), 1)
                v.wait_ge(sem("dve_step"), n.next("dve_step"))
                for t in range(NT):
                    v.wait_ge(psum_free(T("z") + t), fills(T("z") + t))
                for t in range(NT):
                    TT(mix[:, t, 512:1024], mix[:, t, 512:1024], tm[:, t, 1536:2048], ALU.mult).then_inc(sem("dve_step"), 1)
                    v.wait_ge(sem("dve_step"), n.next("dve_step"))
                head_norm(lambda t: mix[:, t, 512:1024], 4, 256, bc1v(layer, "ssdn").rearrange("p (h d) -> p h d", d=256), 1.0)
                for i in range(2):
                    v.wait_ge(psum_free(T("gqk") + i), fills(T("gqk") + i))
                v.wait_ge(sem("gla_exp"), n.next("gla_exp"))
                STT(qd, gqk[:, 0:2, :], GLA_DK ** -0.5, eb, ALU.mult, ALU.mult).then_inc(sem("dve_step"), 1)
                v.wait_ge(sem("dve_step"), n.next("dve_step"))
                TT(ki, gqk[:, 2:4, :], enb, ALU.mult).then_inc(sem("dve_step"), 1)
                v.wait_ge(sem("dve_step"), n.next("dve_step"))
                TT(ke, gqk[:, 2:4, :], ke, ALU.mult).then_inc(sem("gla_ready"), 1)
                v.wait_ge(sem("gla_ready"), n.next("gla_ready"))
                k = T("keT")
                v.wait_ge(psum_full(k), fills(k))
                v.wait_ge(sem("states_zero"), n.next("states_zero"))
                bk = bank(k)[:, :].rearrange("p (t j) -> p t j", t=2)
                nc.vector.tensor_copy(kz[0:64, 0, :], bk[0:64, 0, :]).then_inc(sem("dve_step"), 1)
                v.wait_ge(sem("dve_step"), n.next("dve_step"))
                nc.vector.tensor_copy(kz[64:P, 1, :], bk[64:P, 0, :]).then_inc(sem("dve_step"), 1)
                v.wait_ge(sem("dve_step"), n.next("dve_step"))
                nc.vector.tensor_copy(kz[0:64, 2, :], bk[0:64, 1, :]).then_inc(psum_free(k), 1)
                v.wait_ge(psum_free(k), fills(k))
                for cc in range(3):
                    k = T("gst") + cc
                    v.wait_ge(psum_full(k), fills(k))
                    for j in range(2):
                        for par in range(2):
                            lo = 64 * par
                            ins = STT(Sh[lo:lo + 64, cc + 1, j, P * par:P * par + P], Sh[lo:lo + 64, cc, j, P * par:P * par + P],
                                      eb[lo:lo + 64, j, GLA_C * (cc + 1) - 1:GLA_C * (cc + 1)],
                                      bank(k)[lo:lo + 64, 256 * j + P * par:256 * j + P * par + P], ALU.mult, ALU.add)
                            if j + par < 2:
                                ins.then_inc(sem("dve_step"), 1)
                                v.wait_ge(sem("dve_step"), n.next("dve_step"))
                    ins.then_inc(psum_free(k), 1)
                    v.wait_ge(psum_free(k), fills(k))
                for par in range(2):
                    k = T("gat") + par
                    v.wait_ge(psum_full(k), fills(k))
                    for t in range(NT):
                        ins = TT(attm[:, t, par:4:2, :], bank(k)[:, 256 * t:256 * t + 256].rearrange("p (j l) -> p j l", j=2),
                                 tri64[:, :].unsqueeze(1).to_broadcast([P, 2, P]), ALU.mult)
                        if t == 0:
                            ins.then_inc(sem("dve_step"), 1)
                            v.wait_ge(sem("dve_step"), n.next("dve_step"))
                    ins.then_inc(psum_free(k), 1)
                    v.wait_ge(psum_free(k), fills(k))
                for t in range(NT):
                    k = T("go") + t
                    v.wait_ge(psum_full(k), fills(k))
                    nc.vector.tensor_copy(mix[:, t, 1024:1536], bank(k)[:, :]).then_inc(psum_free(k), 1)
                    v.wait_ge(psum_free(k), fills(k))
                head_norm(lambda t: mix[:, t, 1024:1536], 8, GLA_DV, bc1v(layer, "glan").unsqueeze(1).to_broadcast([P, 4, GLA_DV]), 1.0)
                for t in range(NT):
                    v.wait_ge(psum_free(T("gg") + t), fills(T("gg") + t))
                TT(mix[:, 0, 1024:1536], mix[:, 0, 1024:1536], tm[:, 0, 2560:3072], ALU.mult).then_inc(sem("dve_step"), 1)
                v.wait_ge(sem("dve_step"), n.next("dve_step"))
                TT(mix[:, 1, 1024:1536], mix[:, 1, 1024:1536], tm[:, 1, 2560:3072], ALU.mult).then_inc(sem("mix_ready"), 1)
                v.wait_ge(sem("mix_ready"), n.next("mix_ready"))
                v.sem_inc(sem("ptm_free"), 1)
                add_rows(T("wo"))
                norm_rows()
                norm_evac(T("n2"), cpl[:, 8:16])
                for f in range(KF):
                    k = T("ffn") + f
                    v.wait_ge(sem("silu_done"), n.next("silu_done"))
                    TT(hid[:, f, :], sil[:, f % 2, :], bank(k)[:, SEQ:2 * SEQ], ALU.mult).then_inc(psum_free(k), 1)
                add_rows(T("dn"))
                v.sem_inc(sem("h_ready"), 1)
                for i in range(4):
                    v.wait_ge(psum_free(T("pg") + i), fills(T("pg") + i))
                for i in range(4):
                    k = T("pp") + i
                    o = 512 * (i % 2)
                    v.wait_ge(psum_full(k), fills(k))
                    s_ = sg[:, i // 2, o:o + 512]
                    TT(s_, s_, bank(k)[:, :], ALU.mult).then_inc(psum_free(k), 1)
                    v.wait_ge(psum_free(k), fills(k))
                    TT(h[:, i // 2, o:o + 512], h[:, i // 2, o:o + 512], s_, ALU.add).then_inc(sem("dve_step"), 1)
                    v.wait_ge(sem("dve_step"), n.next("dve_step"))
                v.sem_inc(sem("layer_done"), 1)
                if layer == 0:
                    v.sem_inc(sem("arena_free"), 1)

            v.wait_ge(sem("route_weights_loaded"), 16 * 6)
            v.wait_ge(sem("late_rows_loaded"), 16 * 5)
            norm_rows(meta=True)
            norm_evac(TILE["m1"], cp2[:, 0:8])
            k = TILE["mm"]
            v.wait_ge(psum_full(k), fills(k))
            TT(xT[:, 0:8, 0:NM], bank(k)[:, 0:P].rearrange("p (k t) -> p k t", k=8),
                    cp2[:, 0:8].unsqueeze(2).to_broadcast([P, 8, NM]), ALU.mult).then_inc(psum_free(k), 1)
            TT(s8[:, 16, 0:4], cp2[:, 8:12], cp2[:, 12:16], ALU.subtract).then_inc(sem("lbd_ready"), 1)
            v.wait_ge(sem("lbd_ready"), n.next("lbd_ready"))
            v.wait_ge(sem("lb_sig"), n.next("lb_sig"))
            TS(s8[:, 18, 0:4], s8[:, 17, 0:4], -1.0, 1.0, ALU.mult, ALU.add).then_inc(sem("dve_step"), 1)
            v.wait_ge(sem("dve_step"), n.next("dve_step"))
            v.wait_ge(sem("f_sig"), n.next("f_sig"))
            oml = s8[:, 18, 0:4].unsqueeze(2).to_broadcast([P, 4, NTOK])
            TT(kT, kT, oml, ALU.mult).then_inc(sem("dve_step"), 1)
            v.wait_ge(sem("dve_step"), n.next("dve_step"))
            TT(fT, fT, oml, ALU.mult).then_inc(sem("dve_step"), 1)
            v.wait_ge(sem("dve_step"), n.next("dve_step"))
            TT(fT, fT, s8[:, 17, 0:4].unsqueeze(2).to_broadcast([P, 4, NTOK]), ALU.add).then_inc(sem("f_ready"), 1)
            v.wait_ge(sem("f_ready"), n.next("f_ready"))
            v.wait_ge(sem("f_ln"), n.next("f_ln"))
            for hh in range(HG_H):
                nc.vector.tensor_tensor_scan(Gm[:, hh, :], ones[:, 0:NM], fT[:, hh, 0:NM], 0.0, ALU.mult, ALU.add).then_inc(sem("dve_step"), 1)
                v.wait_ge(sem("dve_step"), n.next("dve_step"))
                for t in range(NT):
                    nc.vector.tensor_tensor_scan(G[:, hh, P * t:P * t + P], ones[:, :], fT[:, hh, NM + P * t:NM + P * t + P], 0.0, ALU.mult, ALU.add).then_inc(sem("dve_step"), 1)
                    v.wait_ge(sem("dve_step"), n.next("dve_step"))
            v.sem_inc(sem("h_norm"), 1)
            TT(fT[:, :, 0:NM], Gm[:, :, NM - 1:NM].to_broadcast([P, 4, NM]), Gm, ALU.subtract).then_inc(sem("dve_step"), 1)
            v.wait_ge(sem("dve_step"), n.next("dve_step"))
            TT(klev[:, :, 0:P], G[:, :, P - 1:P].to_broadcast([P, 4, P]), G[:, :, 0:P], ALU.subtract).then_inc(sem("dve_step"), 1)
            v.wait_ge(sem("dve_step"), n.next("dve_step"))
            v.sem_inc(sem("gend_ready"), 1)
            v.wait_ge(sem("gend_exp"), n.next("gend_exp"))
            TT(fT[:, :, 0:NM], fT[:, :, 0:NM], kT[:, :, 0:NM], ALU.mult).then_inc(sem("dve_step"), 1)
            v.wait_ge(sem("dve_step"), n.next("dve_step"))
            TT(klev[:, :, 0:P], klev[:, :, 0:P], kT[:, :, NM:NM + P], ALU.mult).then_inc(sem("ke_ready"), 1)
            v.wait_ge(sem("ke_ready"), n.next("ke_ready"))
            k = TILE["hsm"]
            v.wait_ge(psum_full(k), fills(k))
            nc.vector.tensor_copy(S[:, 0], bank(k)[:, :].rearrange("p (h d) -> p h d", h=4)).then_inc(psum_free(k), 1)
            v.wait_ge(psum_free(k), fills(k))
            k = TILE["hs0"]
            v.wait_ge(psum_full(k), fills(k))
            nc.vector.tensor_copy(S[:, 1], bank(k)[:, :].rearrange("p (h d) -> p h d", h=4)).then_inc(psum_free(k), 1)
            v.wait_ge(psum_free(k), fills(k))
            g2 = G.rearrange("p h t -> p (h t)")
            w2 = wlev.rearrange("p h t -> p (h t)")

            def level_diff(i):
                b2 = 2 * LEVELS[i]
                gv = g2.rearrange("p (n b) -> p n b", b=b2)
                TT(w2.rearrange("p (n b) -> p n b", b=b2), gv,
                          gv[:, :, b2 // 2 - 1:b2 // 2].to_broadcast([P, 1024 // b2, b2]), ALU.subtract).then_inc(sem("diff_ready"), 1)
                v.wait_ge(sem("diff_ready"), n.next("diff_ready"))
            level_diff(0)
            for i in range(len(LEVELS) + 1):
                if i < len(LEVELS):
                    v.wait_ge(sem("w_ready"), i + 1)
                    TT(qlev, qT, wlev, ALU.mult).then_inc(sem("qlev_ready"), 1)
                    v.wait_ge(sem("qlev_ready"), n.next("qlev_ready"))
                    v.wait_ge(sem("klev_ready"), i + 1)
                    if i + 1 < len(LEVELS):
                        level_diff(i + 1)
                for t in range(NT):
                    k = TILE["lev", i] + t
                    v.wait_ge(psum_full(k), fills(k))
                    src = bank(k)[:, :].rearrange("p (h l) -> p h l", h=4)
                    mask = lev[:, i, :].unsqueeze(1).to_broadcast([P, 4, P])
                    if i == 0:
                        TT(acc[:, t], src, mask, ALU.mult).then_inc(psum_free(k), 1)
                        v.wait_ge(psum_free(k), fills(k))
                    else:
                        tmp = xn[:, t, 0:512].rearrange("p (h l) -> p h l", h=4)
                        TT(tmp, src, mask, ALU.mult).then_inc(psum_free(k), 1)
                        v.wait_ge(psum_free(k), fills(k))
                        TT(acc[:, t], acc[:, t], tmp, ALU.add).then_inc(sem("dve_step"), 1)
                        v.wait_ge(sem("dve_step"), n.next("dve_step"))
            v.sem_inc(sem("qexp_asked"), 1)
            v.wait_ge(sem("qexp_done"), n.next("qexp_done"))
            for hh in range(HG_H):
                STT(S[:, 1, hh, :], S[:, 0, hh, :], wlev[:, hh, P - 1:P], S[:, 1, hh, :], ALU.mult, ALU.add).then_inc(sem("dve_step"), 1)
                v.wait_ge(sem("dve_step"), n.next("dve_step"))
            TT(qlev, qT, wlev, ALU.mult).then_inc(sem("inter_ready"), 1)
            v.wait_ge(sem("inter_ready"), n.next("inter_ready"))
            for t in range(NT):
                k = TILE["ho"] + t
                v.wait_ge(psum_full(k), fills(k))
                nc.vector.tensor_copy(oa[:, t, :], bank(k)[:, :]).then_inc(psum_free(k), 1)
                v.wait_ge(psum_free(k), fills(k))
            for t in range(NT):
                sq = xn[:, 1, 0:512]
                TT(sq, oa[:, t, :], oa[:, t, :], ALU.mult).then_inc(sem("dve_step"), 1)
                v.wait_ge(sem("dve_step"), n.next("dve_step"))
                nc.vector.reduce_sum(st1[:, 4 * t:4 * t + 4], sq.rearrange("p (h d) -> p h d", d=P), axis=AX.X).then_inc(sem("dve_step"), 1)
                v.wait_ge(sem("dve_step"), n.next("dve_step"))
            rsqrt(8, P)
            for t in range(NT):
                o3 = oa[:, t, :].rearrange("p (h d) -> p h d", d=P)
                TT(o3, o3, st2[:, 4 * t:4 * t + 4].unsqueeze(2).to_broadcast([P, 4, P]), ALU.mult).then_inc(sem("dve_step"), 1)
                v.wait_ge(sem("dve_step"), n.next("dve_step"))
                TT(oa[:, t, :], oa[:, t, :], bc2v("hgn"), ALU.mult).then_inc(sem("dve_step"), 1)
                v.wait_ge(sem("dve_step"), n.next("dve_step"))
                TT(oa[:, t, :], oa[:, t, :], og[:, t, :], ALU.mult).then_inc(sem("dve_step"), 1)
                v.wait_ge(sem("dve_step"), n.next("dve_step"))
            v.sem_inc(sem("oa_ready"), 1)
            for t in range(NT):
                k = TILE["oaT"] + t
                v.wait_ge(psum_full(k), fills(k))
                nc.vector.tensor_copy(oaT[:, :, P * t:P * t + P], bank(k)[:, :].rearrange("p (j t) -> p j t", j=4)).then_inc(psum_free(k), 1)
            v.wait_ge(sem("zeros"), n.next("zeros"))
            for m in range(KD):
                TS(xc[:, m, :], lx[:, m, 0:NTOK], cp2[:, 16 + m:17 + m], cp2[:, 48 + m:49 + m], ALU.mult, ALU.add).then_inc(sem("dve_step"), 1)
                v.wait_ge(sem("dve_step"), n.next("dve_step"))
                for j in range(1, CONV):
                    STT(xc[:, m, :], lx[:, m, j:j + NTOK], cp2[:, 16 + 8 * j + m:17 + 8 * j + m], xc[:, m, :], ALU.mult, ALU.add).then_inc(sem("dve_step"), 1)
                    v.wait_ge(sem("dve_step"), n.next("dve_step"))
            v.sem_inc(sem("xc_ready"), 1)
            v.sem_inc(sem("xc_ready"), 1)
            v.sem_inc(sem("lam_ready"), 1)
            v.wait_ge(sem("lam_ln"), n.next("lam_ln"))
            lam8 = s8[:, 21, 0:8]
            TS(lam8, cp2[:, 72:80], -1.0, 0.0, ALU.mult, ALU.max).then_inc(sem("dve_step"), 1)
            v.wait_ge(sem("dve_step"), n.next("dve_step"))
            TT(lam8, lam8, s8[:, 20, 0:8], ALU.add).then_inc(sem("dve_step"), 1)
            v.wait_ge(sem("dve_step"), n.next("dve_step"))
            TS(lam8, lam8, -8.0, None, ALU.mult).then_inc(sem("dve_step"), 1)
            v.wait_ge(sem("dve_step"), n.next("dve_step"))
            TT(ra, ra, lam8.unsqueeze(2).to_broadcast([P, 8, NTOK]), ALU.mult).then_inc(sem("loga_ready"), 1)
            v.wait_ge(sem("loga_ready"), n.next("loga_ready"))
            TT(xc, xc, iu, ALU.mult).then_inc(sem("dve_step"), 1)
            v.wait_ge(sem("dve_step"), n.next("dve_step"))
            v.wait_ge(sem("a_ready"), n.next("a_ready"))
            for u in range(4):
                v.wait_ge(psum_free(TILE["unit", u]), fills(TILE["unit", u]))
            iux = iu[:, :, NM:]
            TT(iux, ly, ly, ALU.mult).then_inc(sem("dve_step"), 1)
            v.wait_ge(sem("dve_step"), n.next("dve_step"))
            TS(iux, iux, 0.044715, 1.0, ALU.mult, ALU.add).then_inc(sem("dve_step"), 1)
            v.wait_ge(sem("dve_step"), n.next("dve_step"))
            TT(iux, iux, ly, ALU.mult).then_inc(sem("gelu_asked"), 1)
            v.wait_ge(sem("gelu_asked"), n.next("gelu_asked"))
            v.wait_ge(sem("gelu_tanh"), n.next("gelu_tanh"))
            STT(ly, iux, 1.0, ly, ALU.add, ALU.mult).then_inc(sem("dve_step"), 1)
            v.wait_ge(sem("dve_step"), n.next("dve_step"))
            TT(iu, ra, ra, ALU.mult).then_inc(sem("dve_step"), 1)
            v.wait_ge(sem("dve_step"), n.next("dve_step"))
            STT(th, iu, 1.0, th, ALU.add, ALU.mult).then_inc(sem("sq_ready"), 1)
            v.wait_ge(sem("sq_ready"), n.next("sq_ready"))
            v.wait_ge(sem("sq_done"), n.next("sq_done"))
            TT(xc, xc, th, ALU.mult).then_inc(sem("dve_step"), 1)
            v.wait_ge(sem("dve_step"), n.next("dve_step"))
            for m in range(KD):
                nc.vector.tensor_tensor_scan(th[:, m, :], ra[:, m, :], xc[:, m, :], 0.0, ALU.mult, ALU.add).then_inc(sem("dve_step"), 1)
                v.wait_ge(sem("dve_step"), n.next("dve_step"))
            STT(th[:, :, NM:], th[:, :, NM:], 0.5, ly, ALU.mult, ALU.mult).then_inc(sem("lru_ready"), 1)
            v.wait_ge(sem("lru_ready"), n.next("lru_ready"))
            for i in range(4):
                k = TILE["ua"] + i
                v.wait_ge(psum_full(k), fills(k))
                u = TILE["unit", 4 + i]
                v.wait_ge(psum_free(u), fills(u))
                TT(ga[:, 2 * i:2 * i + 2, :], ga[:, 2 * i:2 * i + 2, :], bank(k)[:, :].rearrange("p (m t) -> p m t", m=2), ALU.mult).then_inc(psum_free(k), 1)
                v.wait_ge(psum_free(k), fills(k))
            for i in range(4):
                k = TILE["ub"] + i
                v.wait_ge(psum_full(k), fills(k))
                u = TILE["unit", 8 + i]
                v.wait_ge(psum_free(u), fills(u))
                TT(gb[:, 2 * i:2 * i + 2, :], gb[:, 2 * i:2 * i + 2, :], bank(k)[:, :].rearrange("p (m t) -> p m t", m=2), ALU.mult).then_inc(psum_free(k), 1)
                v.wait_ge(psum_free(k), fills(k))
            TT(mTt, ga, gb, ALU.add).then_inc(sem("merged_ready"), 1)
            v.wait_ge(sem("merged_ready"), n.next("merged_ready"))
            add_rows(TILE["wo2"])
            norm_rows(gain_row=bc2v("n2"))
            norm_evac(TILE["m2"], None)
            k = TILE["rt"]
            v.wait_ge(psum_full(k), fills(k))
            lg = mflat[:, 0:72].rearrange("p (t e) -> p t e", t=2)
            bias = bc[:, 2560:2596].unsqueeze(1).to_broadcast([P, NT, NG + NE])
            TT(lg, bank(k)[:, 0:P].rearrange("p (t e) -> p t e", t=2)[:, :, 0:NG + NE], bias, ALU.add).then_inc(psum_free(k), 1)
            v.wait_ge(psum_free(k), fills(k))
            iof = s8[:, 15, 0:8]
            for i in range(8):
                v.memset(s8[:, 15, i:i + 1], float(i) - 64.0).then_inc(sem("dve_step"), 1)
                v.wait_ge(sem("dve_step"), n.next("dve_step"))

            def first_max(val, w, mx, hot, at):
                b3 = [P, NT, w]
                nc.vector.reduce_max(mx, val, axis=AX.X).then_inc(sem("dve_step"), 1)
                v.wait_ge(sem("dve_step"), n.next("dve_step"))
                TT(hot, val, mx.unsqueeze(2).to_broadcast(b3), ALU.is_equal).then_inc(sem("dve_step"), 1)
                v.wait_ge(sem("dve_step"), n.next("dve_step"))
                TT(hot, hot, iof[:, 0:w].unsqueeze(1).to_broadcast(b3), ALU.mult).then_inc(sem("dve_step"), 1)
                v.wait_ge(sem("dve_step"), n.next("dve_step"))
                nc.vector.tensor_reduce(at, hot, AX.X, ALU.min).then_inc(sem("dve_step"), 1)
                v.wait_ge(sem("dve_step"), n.next("dve_step"))
                TT(hot, iof[:, 0:w].unsqueeze(1).to_broadcast(b3), at.unsqueeze(2).to_broadcast(b3), ALU.is_equal).then_inc(sem("dve_step"), 1)
                v.wait_ge(sem("dve_step"), n.next("dve_step"))

            gl = lg[:, :, 0:NG]
            gmx, gat, ghot = s8[:, 5, 0:2], s8[:, 5, 2:4], s8[:, 6:8, 0:NG]
            first_max(gl, NG, gmx, ghot, gat)
            TT(s8[:, 2:4, 0:NG], gl, gmx.unsqueeze(2).to_broadcast([P, NT, NG]), ALU.subtract).then_inc(sem("dve_step"), 1)
            v.wait_ge(sem("dve_step"), n.next("dve_step"))
            sel = s8[:, 9:11, 0:8]
            tmp = s8[:, 11:13, 0:8]
            for g_ in range(NG):
                dst = sel if g_ == 0 else tmp
                TT(dst, lg[:, :, NG + EPG * g_:NG + EPG * g_ + EPG], ghot[:, :, g_:g_ + 1].to_broadcast([P, NT, EPG]), ALU.mult).then_inc(sem("dve_step"), 1)
                v.wait_ge(sem("dve_step"), n.next("dve_step"))
                if g_:
                    TT(sel, sel, tmp, ALU.add).then_inc(sem("dve_step"), 1)
                    v.wait_ge(sem("dve_step"), n.next("dve_step"))
            m1, a1, h1 = s8[:, 5, 4:6], s8[:, 5, 6:8], s8[:, 13:15, 0:8]
            m2, a2, h2 = s8[:, 5, 8:10], s8[:, 5, 10:12], s8[:, 16:18, 0:8]
            first_max(sel, EPG, m1, h1, a1)
            STT(sel, h1, -3e38, sel, ALU.mult, ALU.add).then_inc(sem("dve_step"), 1)
            v.wait_ge(sem("dve_step"), n.next("dve_step"))
            first_max(sel, EPG, m2, h2, a2)
            TT(s8[:, 4, 0:2], m2, m1, ALU.subtract).then_inc(sem("route_exp_asked"), 1)
            v.wait_ge(sem("route_exp_asked"), n.next("route_exp_asked"))
            hs = s8[:, 19:21, 0:8]
            TT(hs, h1, h2, ALU.add).then_inc(sem("dve_step"), 1)
            v.wait_ge(sem("dve_step"), n.next("dve_step"))
            for g_ in range(NG):
                TT(chosen[:, :, EPG * g_:EPG * g_ + EPG], hs, ghot[:, :, g_:g_ + 1].to_broadcast([P, NT, EPG]), ALU.mult).then_inc(sem("dve_step"), 1)
                v.wait_ge(sem("dve_step"), n.next("dve_step"))
            v.sem_inc(sem("chosen_ready"), 1)
            nc.vector.tensor_copy(place, place_i[:, :]).then_inc(sem("dve_step"), 1)
            v.wait_ge(sem("dve_step"), n.next("dve_step"))
            v.wait_ge(sem("route_exp"), n.next("route_exp"))
            ps_, w1, w2_ = s8[:, 18, 0:2], s8[:, 18, 2:4], s8[:, 18, 4:6]
            nc.vector.reduce_sum(ps_, s8[:, 2:4, 0:NG], axis=AX.X).then_inc(sem("dve_step"), 1)
            v.wait_ge(sem("dve_step"), n.next("dve_step"))
            STT(ps_, s8[:, 4, 0:2], 1.0, ps_, ALU.add, ALU.mult).then_inc(sem("dve_step"), 1)
            v.wait_ge(sem("dve_step"), n.next("dve_step"))
            nc.vector.reciprocal(w1, ps_).then_inc(sem("dve_step"), 1)
            v.wait_ge(sem("dve_step"), n.next("dve_step"))
            TT(w2_, w1, s8[:, 4, 0:2], ALU.mult).then_inc(sem("dve_step"), 1)
            v.wait_ge(sem("dve_step"), n.next("dve_step"))
            TT(h1, h1, w1.unsqueeze(2).to_broadcast([P, NT, 8]), ALU.mult).then_inc(sem("dve_step"), 1)
            v.wait_ge(sem("dve_step"), n.next("dve_step"))
            TT(h2, h2, w2_.unsqueeze(2).to_broadcast([P, NT, 8]), ALU.mult).then_inc(sem("dve_step"), 1)
            v.wait_ge(sem("dve_step"), n.next("dve_step"))
            TT(h1, h1, h2, ALU.add).then_inc(sem("dve_step"), 1)
            v.wait_ge(sem("dve_step"), n.next("dve_step"))
            for g_ in range(NG):
                TT(gate[:, :, EPG * g_:EPG * g_ + EPG], h1, ghot[:, :, g_:g_ + 1].to_broadcast([P, NT, EPG]), ALU.mult).then_inc(sem("dve_step"), 1)
                v.wait_ge(sem("dve_step"), n.next("dve_step"))

            k = TILE["rk"]
            v.wait_ge(psum_full(k), fills(k))
            TT(rank, bank(k)[:, 0:2 * NE].rearrange("p (t e) -> p t e", t=NT), chosen, ALU.mult).then_inc(sem("dve_step"), 1)
            nc.vector.reduce_max(s8[:, 19, 0:1], bank(k)[:, 2 * NE:3 * NE], axis=AX.X).then_inc(psum_free(k), 1)
            v.wait_ge(psum_free(k), fills(k))
            v.wait_ge(sem("dve_step"), n.next("dve_step"))
            TS(rank, rank, float(SL - 1), None, ALU.add).then_inc(sem("dve_step"), 1)
            v.wait_ge(sem("dve_step"), n.next("dve_step"))
            cnt, np_ = s8[:, 19, 0:1], s8[:, 20, 0:1]
            v.memset(np_, 1.0).then_inc(sem("dve_step"), 1)
            v.wait_ge(sem("dve_step"), n.next("dve_step"))
            for lim in range(SL, SEQ, SL):
                STT(np_, cnt, float(lim), np_, ALU.is_gt, ALU.add).then_inc(sem("dve_step"), 1)
                v.wait_ge(sem("dve_step"), n.next("dve_step"))
            nc.vector.tensor_copy(passes[:, :], np_).then_inc(sem("dve_step"), 1)
            v.wait_ge(sem("dve_step"), n.next("dve_step"))
            for b in range(4):
                v.sem_inc(pair_free(b), 2)
            v.sem_inc(sem("passes_ready"), 1)
            n_passes = v.value_load(passes[0:1, 0:1], min_val=1, max_val=MAX_PASSES)
            with v.Fori(0, n_passes) as turn:
                TS(rank, rank, float(SL), None, ALU.subtract).then_inc(sem("rank_shifted"), 1)
                with v.Fori(0, PAIRS) as i:
                    n_ = turn * PAIRS + i
                    v.wait_ge(sem("rank_shifted"), turn + 1)
                    for t in range(NT):
                        for e in range(2):
                            r_ = rank[:, t, bass.ds(i * 2 + e, 1)]
                            g_ = gate[:, t, bass.ds(i * 2 + e, 1)]
                            TS(pick[:, t, SL * e:SL * e + SL], place, r_, None, ALU.is_equal)
                            ins = TS(pickw[:, t, SL * e:SL * e + SL], place, r_, g_, ALU.is_equal, ALU.mult)
                    ins.then_inc(sem("pick_ready"), 1)
                    v.wait_ge(pair_full(0), n_ * 2 + 1)
                    nc.vector.tensor_copy(xsE[:, 0:4, :], psum[0][:, :].rearrange("p (k n) -> p k n", k=4)).then_inc(pair_free(0), 1)
                    v.wait_ge(pair_full(2), n_ * 2 + 1)
                    nc.vector.tensor_copy(pickT, psum[2][:, 0:NT * P]).then_inc(pair_free(2), 1)
                    v.wait_ge(sem("expert_silu"), n_ * 2 + 1)
                    TT(hidE[:, 0].rearrange("p k n -> p (k n)"), silE[:, 0, :], psum[3][:, KE * SL:], ALU.mult).then_inc(pair_free(3), 1)
                    v.wait_ge(sem("expert_silu"), n_ * 2 + 2)
                    TT(hidE[:, 1].rearrange("p k n -> p (k n)"), silE[:, 1, :], psum[0][:, KE * SL:], ALU.mult).then_inc(pair_free(0), 1)
            v.wait_ge(sem("sum_done"), 1)
            for q in range(4):
                dst = h[:, q // 2, 512 * (q % 2):512 * (q % 2) + 512]
                TT(dst, dst, psum[4 + q][:, :], ALU.add).then_inc(sem("dve_step"), 1)
                v.wait_ge(sem("dve_step"), n.next("dve_step"))
            norm_rows(gain_row=bc2v("fin"))


_INS = ['x', 'p', 'positions', 'attn_norm', 'w_in', 'da_q_norm', 'da_k_norm', 'da_lambda_q1', 'da_lambda_k1',
        'da_lambda_q2', 'da_lambda_k2', 'da_sub_norm', 'ssd_conv_w', 'ssd_conv_b', 'ssd_dt_bias', 'ssd_a_log',
        'ssd_d', 'ssd_norm', 'gla_w_gate2', 'gla_b_gate', 'gla_norm', 'w_out', 'ffn_norm', 'w_ffn_gate', 'w_ffn_up',
        'w_ffn_down', 'ple_w_proj', 'ple_w_gate', 'meta_tokens_2', 'norm1_g_2', 'w_in_2', 'hg_lower_bounds_2',
        'hg_norm_g_2', 'conv_w_2', 'conv_b_2', 'lru_w_r_2', 'lru_b_r_2', 'lru_w_i_2', 'lru_b_i_2', 'lru_lambda_2',
        'w_up_a_2', 'w_up_b_2', 'w_out_2', 'norm2_g_2', 'w_group_2', 'b_group_2', 'w_router_2', 'b_router_2',
        'w_gate_2', 'w_up_2', 'w_down_2', 'final_g_2']


def kernel(**inputs):
    import numpy as _np
    import concourse.bacc as _bacc
    from concourse import mybir as _mybir
    from concourse.bass_utils import run_bass_kernel_spmd as _run

    nc = _bacc.Bacc("TRN2", target_bir_lowering=False, num_devices=1)
    arrays, d = {}, {}
    for name in _INS:
        a = _np.ascontiguousarray(inputs[name])
        arrays[f"in_{name}"] = a
        d[name] = nc.dram_tensor(f"in_{name}", a.shape, _mybir.dt.from_np(a.dtype), kind="ExternalInput").ap()
    out = nc.dram_tensor("out_0", (1, SEQ, D), _mybir.dt.float32, kind="ExternalOutput").ap()
    program(nc, d, out)
    r = _run(nc, [arrays], core_ids=[0])
    return r.results[0]["out_0"]
```
